# Optimizing a Trainium2 kernel written in Bass

```python
import jax, jax.numpy as jnp
from jax import lax
import numpy as np

D_MODEL = 1024
BATCH = 1
SEQ = 2048
DEPTH = 1

GRID_W = 64
CTX_LEN = 256
NA_HEADS = 8
HEAD_DIM = 64
NA_WIDTH = NA_HEADS * HEAD_DIM
WIN_ROWS = 8
WIN_COLS = 16
F_GROUPS = 8
F_GROUP_DIM = 64
F_WIDTH = F_GROUPS * F_GROUP_DIM
MIX_WIDTH = NA_WIDTH + F_WIDTH
IN_WIDTH = 3 * NA_WIDTH + F_WIDTH
N_EXPERTS = 16
N_GROUPS = 4
EXPERTS_PER_GROUP = N_EXPERTS // N_GROUPS
TOP_K = 2
GROUP_SCORE_K = 2
D_EXPERT = 256
N_MOD = 6
DEEPNORM_ALPHA = (2.0 * DEPTH) ** 0.25
DEEPNORM_BETA = (8.0 * DEPTH) ** -0.25
LN_EPS = 1e-6

kernel_name = "hybrid_na_fnet_grouped_moe_deepnorm"

def layer_norm(x, g=None, b=None):
    xf = x.astype(jnp.float32)
    mu = jnp.mean(xf, axis=-1, keepdims=True)
    var = jnp.mean(jnp.square(xf - mu), axis=-1, keepdims=True)
    y = (xf - mu) * lax.rsqrt(var + LN_EPS)
    if g is not None:
        y = y * g.astype(jnp.float32) + b.astype(jnp.float32)
    return y.astype(x.dtype)

def modulate(x, shift, scale):
    return layer_norm(x) * (1 + scale) + shift

def post_norm(x, y, g, b):
    return layer_norm(DEEPNORM_ALPHA * x + y, g, b)

def neighborhood_attention(q, k, v, kc, vc, rpb):
    bsz, length = q.shape[0], q.shape[1]
    rows = length // GRID_W
    kh = min(WIN_ROWS, rows)
    n_cb = GRID_W // WIN_COLS
    span = 2 * WIN_COLS
    scale = HEAD_DIM ** -0.5
    grid = lambda t: t.reshape(bsz, rows, GRID_W, NA_HEADS, HEAD_DIM)
    qg, kg, vg = grid(q), grid(k), grid(v)
    row_start = jnp.clip(jnp.arange(rows) - kh // 2, 0, rows - kh)
    cols = jnp.arange(GRID_W)
    col_start = jnp.clip(cols - WIN_COLS // 2, 0, GRID_W - WIN_COLS).reshape(n_cb, WIN_COLS)
    blk_start = jnp.clip(jnp.arange(n_cb) * WIN_COLS - WIN_COLS // 2, 0, GRID_W - span)
    key_cols = blk_start[:, None] + jnp.arange(span)
    q_cols = cols.reshape(n_cb, WIN_COLS)
    kcol = key_cols[:, None, :]
    col_valid = (kcol >= col_start[:, :, None]) & (kcol < col_start[:, :, None] + WIN_COLS)
    dc_idx = jnp.clip(kcol - q_cols[:, :, None] + WIN_COLS - 1, 0, 2 * WIN_COLS - 2)
    bias_cols = rpb[:, :, dc_idx].astype(jnp.float32)
    bias_cols = jnp.where(col_valid, bias_cols, -jnp.inf)

    def row_fn(args):
        r, q_r = args
        rs = row_start[r]
        k_b = lax.dynamic_slice_in_dim(kg, rs, kh, axis=1)[:, :, key_cols]
        v_b = lax.dynamic_slice_in_dim(vg, rs, kh, axis=1)[:, :, key_cols]
        dr_idx = rs + jnp.arange(kh) - r + WIN_ROWS - 1
        bias = jnp.moveaxis(bias_cols[:, dr_idx], 1, 3)
        q_b = q_r.reshape(bsz, n_cb, WIN_COLS, NA_HEADS, HEAD_DIM)
        s_lat = jnp.einsum('bnqhd,bknshd->bhnqks', q_b, k_b).astype(jnp.float32) * scale + bias
        s_ctx = jnp.einsum('bnqhd,bchd->bhnqc', q_b, kc).astype(jnp.float32) * scale
        n_lat = kh * span
        s = jnp.concatenate([s_lat.reshape(bsz, NA_HEADS, n_cb, WIN_COLS, n_lat), s_ctx], axis=-1)
        p = jax.nn.softmax(s, axis=-1).astype(v.dtype)
        p_lat = p[..., :n_lat].reshape(bsz, NA_HEADS, n_cb, WIN_COLS, kh, span)
        p_ctx = p[..., n_lat:]
        o = (jnp.einsum('bhnqks,bknshd->bnqhd', p_lat, v_b)
             + jnp.einsum('bhnqc,bchd->bnqhd', p_ctx, vc))
        return o.reshape(bsz, GRID_W, NA_HEADS, HEAD_DIM)

    o = lax.map(row_fn, (jnp.arange(rows), jnp.moveaxis(qg, 1, 0)))
    return jnp.moveaxis(o, 0, 1).reshape(bsz, length, NA_WIDTH)

def context_attention(qc, kc, vc):
    s = jnp.einsum('bqhd,bkhd->bhqk', qc, kc).astype(jnp.float32) * HEAD_DIM ** -0.5
    p = jax.nn.softmax(s, axis=-1).astype(vc.dtype)
    o = jnp.einsum('bhqk,bkhd->bqhd', p, vc)
    return o.reshape(qc.shape[0], qc.shape[1], NA_WIDTH)

def fourier_mix(f, w_four):
    bsz, n = f.shape[0], f.shape[1]
    fg = f.reshape(bsz, n, F_GROUPS, F_GROUP_DIM).astype(jnp.float32).transpose(0, 2, 1, 3)
    y = jnp.fft.fft2(fg, norm='ortho').real.transpose(0, 2, 1, 3).astype(f.dtype)
    y = jnp.einsum('bngc,gce->bnge', y, w_four)
    return y.reshape(bsz, n, F_WIDTH)

def grouped_moe(h, w_router, router_bias, w_gate, w_up, w_down):
    shp = h.shape
    t = h.reshape(-1, shp[-1])
    s = jax.nn.sigmoid((t @ w_router).astype(jnp.float32))
    sb = s + router_bias.astype(jnp.float32)
    g_score = lax.top_k(sb.reshape(-1, N_GROUPS, EXPERTS_PER_GROUP), GROUP_SCORE_K)[0].sum(-1)
    g_sel = jnp.argmax(g_score, axis=-1)
    in_group = (jnp.arange(N_EXPERTS) // EXPERTS_PER_GROUP)[None, :] == g_sel[:, None]
    _, idx = lax.top_k(jnp.where(in_group, sb, -jnp.inf), TOP_K)
    w = jnp.take_along_axis(s, idx, axis=-1)
    w = w / jnp.sum(w, axis=-1, keepdims=True)
    combine = jnp.sum(jax.nn.one_hot(idx, N_EXPERTS, dtype=jnp.float32) * w[..., None], axis=1)
    hid = jax.nn.silu(jnp.einsum('nd,edf->nef', t, w_gate)) * jnp.einsum('nd,edf->nef', t, w_up)
    hid = hid * combine[:, :, None].astype(hid.dtype)
    y = jnp.einsum('nef,efd->nd', hid, w_down)
    return y.reshape(shp)

def split_heads(t):
    return t.reshape(t.shape[0], t.shape[1], NA_HEADS, HEAD_DIM)

def hybrid_layer(x, xc, c, c_ctx, w_mod, b_mod, w_in, rpb, w_four, w_out, ln1_g, ln1_b, ln2_g, ln2_b,
                 w_router, router_bias, w_gate, w_up, w_down, last):
    bsz = x.shape[0]
    m = (jax.nn.silu(c) @ w_mod + b_mod).reshape(bsz, N_MOD, 1, D_MODEL)
    mc = (jax.nn.silu(c_ctx) @ w_mod + b_mod).reshape(N_MOD, 1, D_MODEL)

    h = modulate(x, m[:, 0], m[:, 1])
    p = h @ w_in
    q = split_heads(p[..., :NA_WIDTH])
    k = split_heads(p[..., NA_WIDTH:2 * NA_WIDTH])
    v = split_heads(p[..., 2 * NA_WIDTH:3 * NA_WIDTH])
    f = p[..., 3 * NA_WIDTH:]
    hc = modulate(xc, mc[0], mc[1])
    if last:
        pc_kv = hc @ w_in[:, NA_WIDTH:3 * NA_WIDTH]
        kc = split_heads(pc_kv[..., :NA_WIDTH])
        vc = split_heads(pc_kv[..., NA_WIDTH:])
    else:
        pc = hc @ w_in
        qc = split_heads(pc[..., :NA_WIDTH])
        kc = split_heads(pc[..., NA_WIDTH:2 * NA_WIDTH])
        vc = split_heads(pc[..., 2 * NA_WIDTH:3 * NA_WIDTH])
        fc = pc[..., 3 * NA_WIDTH:]

    o_mix = jnp.concatenate([neighborhood_attention(q, k, v, kc, vc, rpb), fourier_mix(f, w_four)], axis=-1)
    x = post_norm(x, m[:, 2] * (o_mix @ w_out), ln1_g, ln1_b)

    h2 = modulate(x, m[:, 3], m[:, 4])
    x = post_norm(x, m[:, 5] * grouped_moe(h2, w_router, router_bias, w_gate, w_up, w_down), ln2_g, ln2_b)
    if last:
        return x, xc

    oc_mix = jnp.concatenate([context_attention(qc, kc, vc), fourier_mix(fc, w_four)], axis=-1)
    xc = post_norm(xc, mc[2] * (oc_mix @ w_out), ln1_g, ln1_b)
    h2c = modulate(xc, mc[3], mc[4])
    xc = post_norm(xc, mc[5] * grouped_moe(h2c, w_router, router_bias, w_gate, w_up, w_down), ln2_g, ln2_b)
    return x, xc

def setup_inputs(seed: int = 0) -> dict:
    key = jax.random.key(seed)
    ks = jax.random.split(key, 20)
    nrm = lambda k, shp: jax.random.normal(k, shp, dtype=jnp.float32)
    x = nrm(ks[0], (BATCH, SEQ, D_MODEL))
    c = nrm(ks[1], (BATCH, D_MODEL))
    ctx = nrm(ks[2], (BATCH, CTX_LEN, D_MODEL))
    c_ctx = nrm(ks[3], (D_MODEL,))
    w_mod = nrm(ks[4], (DEPTH, D_MODEL, N_MOD * D_MODEL)) * (0.5 * D_MODEL ** -0.5)
    b_mod = 0.02 * nrm(ks[5], (DEPTH, N_MOD * D_MODEL))
    w_in = nrm(ks[6], (DEPTH, D_MODEL, IN_WIDTH)) * D_MODEL ** -0.5
    w_in = w_in.at[:, :, 2 * NA_WIDTH:3 * NA_WIDTH].multiply(DEEPNORM_BETA)
    rpb = 0.2 * nrm(ks[7], (DEPTH, NA_HEADS, 2 * WIN_ROWS - 1, 2 * WIN_COLS - 1))
    w_four = nrm(ks[8], (DEPTH, F_GROUPS, F_GROUP_DIM, F_GROUP_DIM)) * (F_GROUP_DIM ** -0.5 * DEEPNORM_BETA)
    w_out = nrm(ks[9], (DEPTH, MIX_WIDTH, D_MODEL)) * (MIX_WIDTH ** -0.5 * DEEPNORM_BETA)
    ln1_g = 1.0 + 0.02 * nrm(ks[10], (DEPTH, D_MODEL))
    ln1_b = 0.02 * nrm(ks[11], (DEPTH, D_MODEL))
    ln2_g = 1.0 + 0.02 * nrm(ks[12], (DEPTH, D_MODEL))
    ln2_b = 0.02 * nrm(ks[13], (DEPTH, D_MODEL))
    w_router = nrm(ks[14], (D_MODEL, N_EXPERTS)) * D_MODEL ** -0.5
    router_bias = 0.01 * nrm(ks[15], (N_EXPERTS,))
    w_gate = nrm(ks[16], (DEPTH, N_EXPERTS, D_MODEL, D_EXPERT)) * D_MODEL ** -0.5
    w_up = nrm(ks[17], (DEPTH, N_EXPERTS, D_MODEL, D_EXPERT)) * D_MODEL ** -0.5
    w_down = nrm(ks[18], (DEPTH, N_EXPERTS, D_EXPERT, D_MODEL)) * (D_EXPERT ** -0.5 * DEEPNORM_BETA)
    return {"x": x, "c": c, "ctx": ctx, "c_ctx": c_ctx, "w_mod": w_mod, "b_mod": b_mod, "w_in": w_in,
            "rpb": rpb, "w_four": w_four, "w_out": w_out, "ln1_g": ln1_g, "ln1_b": ln1_b,
            "ln2_g": ln2_g, "ln2_b": ln2_b, "w_router": w_router, "router_bias": router_bias,
            "w_gate": w_gate, "w_up": w_up, "w_down": w_down}

def reference(x, c, ctx, c_ctx, w_mod, b_mod, w_in, rpb, w_four, w_out, ln1_g, ln1_b, ln2_g, ln2_b,
              w_router, router_bias, w_gate, w_up, w_down):
    xc = ctx
    for i in range(DEPTH):
        x, xc = hybrid_layer(x, xc, c, c_ctx, w_mod[i], b_mod[i], w_in[i], rpb[i], w_four[i], w_out[i],
                             ln1_g[i], ln1_b[i], ln2_g[i], ln2_b[i], w_router, router_bias,
                             w_gate[i], w_up[i], w_down[i], i == DEPTH - 1)
    return x


_drawn_inputs = setup_inputs


def setup_inputs(seed=0):
    import zlib

    import numpy as np

    out = dict(_drawn_inputs(seed))
    spreads = {}
    factors = {'ctx': 185.272,
     'c_ctx': 28.328,
     'b_mod': 3.305,
     'rpb': 28.195,
     'ln2_g': 24.101,
     'ln2_b': 22.922,
     'router_bias': 3.53}
    for name, (base, spread) in spreads.items():
        noise = np.random.default_rng([zlib.crc32(name.encode()), seed]).standard_normal(out[name].shape)
        drawn = base * np.exp(spread * noise) if base else spread * noise
        out[name] = __import__('jax').numpy.asarray(drawn.astype(out[name].dtype))
    for name, factor in factors.items():
        out[name] = (out[name] * factor).astype(out[name].dtype)
    return out
```

```python
from contextlib import ExitStack, contextmanager

import numpy as np

import concourse.bass as bass
from concourse import mybir
from concourse.alu_op_type import AluOpType as ALU

F32 = mybir.dt.float32
F32R = mybir.dt.float32r
I32 = mybir.dt.int32
U32 = mybir.dt.uint32
ACT = mybir.ActivationFunctionType
AX = mybir.AxisListType
ds = bass.ds

P = 128
D = 1024
DC = D // P
SEQ, CTX = 2048, 256
TILES = SEQ // P
GRID_W, ROWS = 64, SEQ // 64
HEADS, HD = 8, 64
PAIRS = HEADS // 2
NAW = HEADS * HD
WIN_R, WIN_C = 8, 16
SPAN = 2 * WIN_C
FW = 512
IN_W = 3 * NAW + FW
E, EG, NG = 16, 4, 4
DE = 256
SLOT_TILES = 48
SLOTS = SLOT_TILES * P
ALPHA = 2.0 ** 0.25
EPS = 1e-6
BIG = 1.0e30
QB = 4
RAD = 16
MODS = 6


def pos(eng, sem, value):
    if not isinstance(value, int) or value > 0:
        eng.wait_ge(sem, value)


@contextmanager
def steps(eng, start, stop, step=1):
    with eng.Fori(0, (stop - start) // step) as i:
        yield i * step + start


def modulation(nc, sem, A, c, c_ctx, w_mod, b_mod, rpb, colmask, ident_d, xbias_d):
    modc, gate2, gate5, ident = A["modc"], A["gate2"], A["gate5"], A["ident"]
    NCH = MODS * DC
    PW = 512
    NP = MODS * D // PW
    NB = 3
    HR = HEADS * 15
    with ExitStack() as ctx:
        sb = lambda name, shape, dt=F32: ctx.enter_context(nc.sbuf_tensor(name, shape, dt))
        ps = lambda name, shape, dt=F32: ctx.enter_context(nc.psum_tensor(name, shape, dt))
        cv = sb("mo_cv", [P, 2, DC])
        sig = sb("mo_sig", [P, 2, DC])
        sc = sb("mo_sc", [P, 2, DC])
        scb = sb("mo_scb", [P, DC, P])
        ones = sb("mo_ones", [P, P])
        w = sb("mo_w", [P, NB, DC, PW])
        brow = sb("mo_brow", [NCH, P])
        bcol = sb("mo_bcol", [P, NCH])
        pad = sb("mo_pad", [HR, 64])
        msk = sb("mo_msk", [HR, QB, WIN_C, SPAN])
        xb = sb("mo_xb", [HR, QB, WIN_C, SPAN])
        pcol = ps("mo_pcol", [P, 512])
        prow = ps("mo_prow", [P, 2, 512])
        pT = ps("mo_pT", [P, 512])
        s_in, s_rpb, s_id = sem("mo_in"), sem("mo_rpb_in"), sem("mo_ident_in")
        s_w = [sem(f"mo_piece_in{i}") for i in range(NB)]
        s_sig, s_silu, s_ones, s_bc = sem("mo_sigmoid"), sem("mo_silu"), sem("mo_ones"), sem("mo_silu_wide")
        s_done, s_row, s_bT, s_bcol = sem("mo_piece_done"), sem("mo_row_added"), sem("mo_b_turned"), sem("mo_b_col")
        s_col, s_pad, s_xb, s_st = sem("mo_cols"), sem("mo_pad_set"), sem("mo_xbias"), sem("mo_xbias_out")
        rows_of = {4: (gate2, 0), 5: (gate2, 1), 10: (gate5, 0), 11: (gate5, 1)}
        order = [p for p in range(NP)]
        w_v = w_mod.rearrange("(p j) n -> p j n", j=DC)
        block = ctx.enter_context(nc.Block())

        @block.sync
        def _(sp):
            sp.dma_start(cv[:, 0, :], c.rearrange("(p j) -> p j", j=DC)).then_inc(s_in, 16)
            sp.dma_start(cv[:, 1, :], c_ctx.rearrange("(p j) -> p j", j=DC)).then_inc(s_in, 16)
            sp.dma_start(ident[:, :], ident_d).then_inc(s_id, 16)
            sp.dma_start(brow[:, :], b_mod.rearrange("(n p) -> n p", p=P)).then_inc(s_id, 16)
            for i, p in enumerate(order):
                if i >= NB:
                    sp.wait_ge(s_done, i - NB + 1)
                sp.dma_start(w[:, i % NB, :, :], w_v[:, :, p * PW:(p + 1) * PW]).then_inc(s_w[i % NB], 16)
                if i == 0:
                    sp.dma_start(gate2[:, :], b_mod[2 * D:3 * D].partition_broadcast(P)).then_inc(s_rpb, 16)
                    sp.dma_start(gate5[:, :], b_mod[5 * D:6 * D].partition_broadcast(P)).then_inc(s_rpb, 16)
                    sp.wait_ge(s_pad, 1)
                    sp.dma_start(pad[:, 16:47], rpb.rearrange("h r c -> (h r) c")).then_inc(s_rpb, 16)
                    sp.dma_start(msk[:, :, :, :], colmask.partition_broadcast(HR)).then_inc(s_rpb, 16)
            sp.wait_ge(s_xb, QB)
            for n in range(QB):
                sp.dma_start(xbias_d[n].rearrange("q h r k -> (h r) q k"), xb[:, n, :, :]).then_inc(s_st, 16)
            sp.wait_ge(s_st, 16 * QB)

        @block.gpsimd
        def _(pool):
            pool.memset(pad[:, :], 0.0).then_inc(s_pad, 1)
            pool.memset(ones[:, :], 1.0).then_inc(s_ones, 1)

        @block.scalar
        def _(act):
            act.wait_ge(s_in, 32)
            act.activation(sig[:, :, :], cv[:, :, :], ACT.Sigmoid).then_inc(s_sig, 1)

        @block.vector
        def _(dve):
            dve.wait_ge(s_sig, 1)
            dve.tensor_tensor(sc[:, :, :], cv[:, :, :], sig[:, :, :], ALU.mult).then_inc(s_silu, 1)
            dve.wait_ge(s_silu, 1)
            dve.wait_ge(s_ones, 1)
            for j in range(DC):
                dve.tensor_scalar(scb[:, j, :], ones[:, :], sc[:, 0, j:j + 1], None, ALU.mult).then_inc(s_bc, 1)
            dve.wait_ge(s_rpb, 64)
            for n, shift in enumerate((0, -8, -8, -16)):
                base = pad[:, 31 + shift:32 + shift]
                skew = bass.AP(base.tensor, base.offset, [list(base.ap[0]), [-1, WIN_C], [1, SPAN]])
                dve.tensor_tensor(xb[:, n, :, :], skew, msk[:, n, :, :], ALU.add).then_inc(s_xb, 1)
            for k, p in enumerate(sorted(rows_of)):
                gate, half = rows_of[p]
                dve.wait_ge(s_done, order.index(p) + 1)
                g = gate[:, half * PW:(half + 1) * PW]
                dve.tensor_tensor(g, prow[:, k % 2, :], g, ALU.add).then_inc(s_row, 1)
            dve.wait_ge(s_bT, 1)
            dve.tensor_copy(bcol[:, :], pT[:, 0:NCH]).then_inc(s_bcol, 1)
            dve.wait_ge(s_bcol, 1)
            dve.wait_ge(s_done, NP)
            for v in range(2):
                for n0 in (0, 3 * DC):
                    n = slice(n0, n0 + 2 * DC)
                    dve.tensor_tensor(modc[:, v, n], pcol[:, 0:2 * NCH].rearrange("p (n v) -> p v n", v=2)[:, v, n],
                                      bcol[:, n], ALU.add).then_inc(s_col, 1)
            dve.wait_ge(s_col, 4)
            for n0 in (DC, 4 * DC):
                dve.tensor_scalar(modc[:, :, n0:n0 + DC], modc[:, :, n0:n0 + DC], 1.0, None, ALU.add).then_inc(s_col, 1)
            dve.wait_ge(s_col, 6)

        @block.tensor
        def _(pe):
            pe.wait_ge(s_id, 32)
            pe.transpose(pT[:, 0:NCH], brow[:, :], ident[0:NCH, 0:NCH]).then_inc(s_bT, 1)
            pe.wait_ge(s_silu, 1)
            k = 0
            for i, p in enumerate(order):
                pe.wait_ge(s_w[i % NB], 16 * (i // NB + 1))
                if p in rows_of:
                    if k == 0:
                        pe.wait_ge(s_bc, DC)
                    if k >= 2:
                        pe.wait_ge(s_row, k - 1)
                    for j in range(DC):
                        mm = pe.matmul(prow[:, k % 2, :], scb[:, j, :], w[:, i % NB, j, :], start=(j == 0), stop=(j == DC - 1))
                    k += 1
                else:
                    for n in range(PW // P):
                        col = 2 * (p * (PW // P) + n)
                        for j in range(DC):
                            mm = pe.matmul(pcol[:, col:col + 2], w[:, i % NB, j, n * P:(n + 1) * P], sc[:, :, j],
                                           start=(j == 0), stop=(j == DC - 1))
                mm.then_inc(s_done, 1)


def projection(nc, sem, A, x, ctx_in, w_in, S):
    modc, ident = A["modc"], A["ident"]
    GW = 2 * P
    NGRP = SEQ // GW
    NO = 6
    OUTS_CTX, OUTS = 6, 12
    with ExitStack() as ctx:
        sb = lambda name, shape, dt=F32: ctx.enter_context(nc.sbuf_tensor(name, shape, dt))
        ps = lambda name, shape, dt=F32: ctx.enter_context(nc.psum_tensor(name, shape, dt))
        whi = sb("pr_whi", [P, DC, IN_W], F32R)
        wlo = sb("pr_wlo", [P, DC, IN_W], F32R)
        hhi = sb("pr_hhi", [P, 2, DC, GW], F32R)
        hlo = sb("pr_hlo", [P, 2, DC, GW], F32R)
        h = sb("pr_h", [P, DC, P])
        xt = sb("pr_x", [P, 2, D])
        stage = sb("pr_stage", [P, 4, 1024])
        st = sb("pr_st", [P, 2, 12])
        mv = sb("pr_mv", [P, 2, 2])
        ve = sb("pr_ve", [P, 2])
        rs = sb("pr_rs", [P, 2])
        half = sb("pr_half", [P, 2])
        turned = ps("pr_turned", [P, 2, 512])
        out = ps("pr_out", [P, NO, 512])
        s_x = [sem(f"pr_x_in{i}") for i in range(2)]
        s_w = [sem(f"pr_w_in{i}") for i in range(2)]
        s_whi, s_wlo = sem("pr_w_hi"), sem("pr_w_lo")
        s_stats, s_mom, s_ve, s_rstd, s_z = sem("pr_stats"), sem("pr_moments"), sem("pr_var_eps"), sem("pr_rstd"), sem("pr_z")
        s_turn, s_mod, s_hi, s_lo = sem("pr_turned"), sem("pr_modulated"), sem("pr_h_hi"), sem("pr_h_lo")
        s_out, s_ev, s_half = sem("pr_out_ready"), sem("pr_out_read"), sem("pr_half")
        s_st = [sem(f"pr_stage_out{i}") for i in range(4)]
        xv = x.rearrange("(t p) d -> t p d", p=P)
        cvw = ctx_in.rearrange("(t p) d -> t p d", p=P)
        wst = [stage[:, 2 * i:2 * i + 2, :].rearrange("p a b -> p (a b)") for i in range(2)]
        block = ctx.enter_context(nc.Block())

        @block.sync
        def _(sp):
            for t in range(2):
                sp.dma_start(xt[:, t, :], cvw[t]).then_inc(s_x[t], 16)
            for j in range(DC):
                if j >= 2:
                    sp.wait_ge(s_wlo, j - 1)
                sp.dma_start(wst[j % 2], w_in[j * P:(j + 1) * P, :]).then_inc(s_w[j % 2], 16)
            with steps(sp, 2, 2 + TILES, 2) as t0:
                for u in range(2):
                    sp.wait_ge(s_turn, t0 + u - 1)
                    sp.dma_start(xt[:, u, :], x[ds((t0 + u - 2) * P, P), :]).then_inc(s_x[u], 16)

        @block.gpsimd
        def _(pool):
            pool.memset(half[:, 0:1], -0.5).then_inc(s_half, 1)
            pool.memset(half[:, 1:2], EPS).then_inc(s_half, 1)
            pool.wait_ge(s_half, 2)

            def tile(t, u, par):
                pool.wait_ge(s_mom, t + 1)
                pool.tensor_tensor(ve[:, u:u + 1], mv[:, u, 1:2], half[:, 1:2], ALU.add).then_inc(s_ve, 1)
                pool.wait_ge(s_ve, t + 1)
                pool.tensor_tensor(rs[:, u:u + 1], ve[:, u:u + 1], half[:, 0:1], ALU.pow).then_inc(s_rstd, 1)
                pool.wait_ge(s_hi, t + 1)
                hs = slice(u * P, (u + 1) * P)
                pool.tensor_tensor(hlo[:, par, :, hs], h[:, :, :], hhi[:, par, :, hs].bitcast(F32), ALU.subtract).then_inc(s_lo, 1)

            tile(0, 0, 0)
            tile(1, 1, 0)
            with steps(pool, 2, 2 + TILES, 4) as t0:
                for k in range(4):
                    tile(t0 + k, k % 2, (1 + k // 2) % 2)

        @block.vector
        def _(dve):
            def tile(t, u, v):
                dve.wait_ge(s_x[u], 16 * (t // 2 + 1) if isinstance(t, int) else (t - u) * 8 + 16)
                for i in range(2):
                    dve.bn_stats(st[:, u, 6 * i:6 * i + 6], xt[:, u, 512 * i:512 * i + 512]).then_inc(s_stats, 1)
                dve.wait_ge(s_stats, 2 * t + 2)
                dve.nop(nofuse=True)
                dve.bn_aggr(mv[:, u, :], st[:, u, :]).then_inc(s_mom, 1)
                dve.wait_ge(s_rstd, t + 1)
                dve.tensor_scalar(xt[:, u, :], xt[:, u, :], mv[:, u, 0:1], rs[:, u:u + 1], ALU.subtract, ALU.mult).then_inc(s_z, 1)
                dve.wait_ge(s_turn, t + 1)
                pos(dve, s_lo, t)
                for j in range(DC):
                    ins = dve.tensor_scalar(h[:, j, :], turned[:, j // 4, (j % 4) * P:(j % 4 + 1) * P],
                                            modc[:, v, DC + j:DC + j + 1], modc[:, v, j:j + 1], ALU.mult, ALU.add)
                ins.then_inc(s_mod, 1)

            for j in range(DC):
                dve.wait_ge(s_whi, j + 1)
                dve.tensor_tensor(wlo[:, j, :], wst[j % 2], whi[:, j, :].bitcast(F32), ALU.subtract).then_inc(s_wlo, 1)
            tile(0, 0, 1)
            tile(1, 1, 1)
            with steps(dve, 2, 2 + TILES, 2) as t0:
                for u in range(2):
                    tile(t0 + u, u, 0)

        def base(s):
            return 0 if isinstance(s, int) and s == 0 else s * OUTS - (OUTS - OUTS_CTX)

        @block.scalar
        def _(act):
            def hi(t, u, par):
                act.wait_ge(s_mod, t + 1)
                act.activation(hhi[:, par, :, u * P:(u + 1) * P], h[:, :, :], ACT.Copy).then_inc(s_hi, 1)

            def evac(n, slot, width, dst, scale=1.0):
                act.wait_ge(s_out, n + 1)
                act.activation(dst, out[:, slot, 0:width], ACT.Copy, scale=scale).then_inc(s_ev, 1)

            def group(s, par, is_ctx, last):
                n, k = base(s), 0
                per = 2 if is_ctx else 4
                cols = slice(0, GW) if is_ctx else ds((s - 1) * GW, GW)
                for which in range(2):
                    pos(act, s_st[which], 16 * s)
                    for o in range(per):
                        evac(n + k, k % NO, GW, stage[:, which, o * GW:(o + 1) * GW],
                             HD ** -0.5 if which == 0 and not is_ctx else 1.0)
                        k += 1
                    act.wait_ge(s_ev, n + k)
                    dst = S["kcT"][which * 2 * P:(which + 1) * 2 * P, :] if is_ctx else S["qT"] if which == 0 else S["kT"]
                    act.dma_start(dst.rearrange("(c p) t -> p c t", p=P)[:, :, cols],
                                  stage[:, which, 0:per * GW].rearrange("p (c t) -> p c t", c=per)).then_inc(s_st[which], 16)
                    if not last:
                        hi(2 * s + 2 + which, which, 1 - par)
                for u in range(2):
                    pos(act, s_st[2 + u], 16 * s)
                    for f in range(1 if is_ctx else 2):
                        evac(n + k, k % NO, 512, stage[:, 2 + u, 512 * f:512 * f + 512])
                        k += 1
                    act.wait_ge(s_ev, n + k)
                    dst, width = (S["vc"][u * P:(u + 1) * P, :], 512) if is_ctx else (S["vf"][ds((s - 1) * GW + u * P, P), :], 1024)
                    act.dma_start(dst, stage[:, 2 + u, 0:width]).then_inc(s_st[2 + u], 16)

            for j in range(DC):
                act.wait_ge(s_w[j % 2], 16 * (j // 2 + 1))
                act.activation(whi[:, j, :], wst[j % 2], ACT.Copy).then_inc(s_whi, 1)
            hi(0, 0, 0)
            hi(1, 1, 0)
            group(0, 0, True, False)
            with steps(act, 1, NGRP - 1, 2) as s0:
                group(s0, 1, False, False)
                group(s0 + 1, 0, False, False)
            group(NGRP - 1, 1, False, False)
            group(NGRP, 0, False, True)
            for i in range(4):
                act.wait_ge(s_st[i], 16 * (NGRP + 1))

        @block.tensor
        def _(pe):
            def turn(t, u):
                pe.wait_ge(s_z, t + 1)
                pos(pe, s_mod, t)
                for j in range(DC):
                    ins = pe.transpose(turned[:, j // 4, (j % 4) * P:(j % 4 + 1) * P], xt[:, u, j * P:(j + 1) * P], ident[:, :])
                ins.then_inc(s_turn, 1)

            def begin(n):
                pos(pe, s_ev, n - NO + 1)

            def by_channel(n, slot, par, col):
                begin(n)
                o = out[:, slot, 0:GW]
                for j in range(DC):
                    a, b = whi[:, j, col:col + P], wlo[:, j, col:col + P]
                    pe.matmul(o, a, hhi[:, par, j, :], start=(j == 0), stop=False)
                    pe.matmul(o, a, hlo[:, par, j, :], start=False, stop=False)
                    ins = pe.matmul(o, b, hhi[:, par, j, :], start=False, stop=(j == DC - 1))
                ins.then_inc(s_out, 1)

            def by_token(n, slot, par, u, col):
                begin(n)
                o = out[:, slot, :]
                for j in range(DC):
                    a, b = hhi[:, par, j, u * P:(u + 1) * P], hlo[:, par, j, u * P:(u + 1) * P]
                    pe.matmul(o, a, whi[:, j, col:col + 512], start=(j == 0), stop=False)
                    pe.matmul(o, a, wlo[:, j, col:col + 512], start=False, stop=False)
                    ins = pe.matmul(o, b, whi[:, j, col:col + 512], start=False, stop=(j == DC - 1))
                ins.then_inc(s_out, 1)

            def group(s, par, is_ctx, last):
                n, k = base(s), 0
                pe.wait_ge(s_lo, 2 * s + 2)
                for which in range(2):
                    for o in range(2 if is_ctx else 4):
                        by_channel(n + k, k % NO, par, NAW + k * P if is_ctx else k * P)
                        k += 1
                    if not last:
                        turn(2 * s + 2 + which, which)
                for u in range(2):
                    for f in range(1 if is_ctx else 2):
                        by_token(n + k, k % NO, par, u, 2 * NAW + 512 * f)
                        k += 1

            turn(0, 0)
            turn(1, 1)
            pe.wait_ge(s_wlo, DC)
            group(0, 0, True, False)
            with steps(pe, 1, NGRP - 1, 2) as s0:
                group(s0, 1, False, False)
                group(s0 + 1, 0, False, False)
            group(NGRP - 1, 1, False, False)
            group(NGRP, 0, False, True)


def fourier(nc, sem, A, w_four, K, S):
    NK = RAD // 2 + 1
    Q = FW // P
    part = {("cos", k): k for k in range(NK)} | {("sin", k): NK - 1 + k for k in range(1, NK - 1)}
    with ExitStack() as ctx:
        sb = lambda name, shape, dt=F32: ctx.enter_context(nc.sbuf_tensor(name, shape, dt))
        ps = lambda name, shape, dt=F32: ctx.enter_context(nc.psum_tensor(name, shape, dt))
        short = sb("fo_short", [P, P])
        long = sb("fo_long", [P, NK, 4 * P])
        chan = sb("fo_chan", [P, 2, P])
        w4 = sb("fo_w4", [P, Q, P])
        mix = sb("fo_mix", [P, 3, Q, P])
        f = sb("fo_f", [P, RAD, FW])
        hs = sb("fo_hs", [P, RAD, FW])
        hb = sb("fo_hb", [P, RAD, FW])
        us = sb("fo_us", [P, 2, Q, 2 * P])
        yT = sb("fo_yT", [P, Q, SEQ])
        pu = ps("fo_pu", [P, Q, 512])
        py = ps("fo_py", [P, Q, 512])
        s_k, s_w4z, s_w4, s_lk = sem("fo_consts_in"), sem("fo_w4_zeroed"), sem("fo_w4_in"), sem("fo_long_in")
        s_f = [sem(f"fo_f_in{i}") for i in range(4)]
        s_hp, s_hs, s_hst = sem("fo_short_done"), sem("fo_short_read"), sem("fo_short_out")
        s_hd = sem("fo_short_read_dve")
        s_hb = [sem(f"fo_part_in{i}") for i in range(NK)]
        s_mp, s_mix = sem("fo_mix_done"), sem("fo_mix_read")
        s_u, s_us, s_y, s_yr, s_yst = sem("fo_u_done"), sem("fo_u_read"), sem("fo_y_done"), sem("fo_y_read"), sem("fo_y_out")
        f_v = S["vf"][:, NAW:].rearrange("(a t j) c -> t a j c", a=RAD, j=8)
        h_v = S["hpart"].rearrange("c (t j) k -> t c j k", j=8)
        block = ctx.enter_context(nc.Block())

        @block.sync
        def _(sp):
            sp.dma_start(short[:, :], K["k_short"]).then_inc(s_k, 16)
            sp.dma_start(chan[:, :, :], K["k_chan"].rearrange("v p c -> p v c")).then_inc(s_k, 16)
            for t in range(RAD):
                sp.dma_start(f[:, t, :], f_v[t]).then_inc(s_f[t // 4], 16)
            sp.wait_ge(s_w4z, 1)
            for g in range(2):
                sp.dma_start(w4[64 * g:64 * g + 64, :, 64 * g:64 * g + 64],
                             w_four.rearrange("(q g) c e -> g c q e", g=2)[g]).then_inc(s_w4, 16)
            sp.dma_start(long[:, :, :], K["k_long"].rearrange("k b n -> b k n")).then_inc(s_lk, 16)
            sp.wait_ge(s_hst, 16 * RAD)
            for k in range(NK):
                for kind in ("cos", "sin"):
                    if (kind, k) in part:
                        c = part[kind, k]
                        sp.dma_start(hb[:, c, :], S["hpart"][c]).then_inc(s_hb[k], 16)
            for q in range(Q):
                sp.wait_ge(s_yr, Q * (NK - 1) + q + 1)
                sp.dma_start(S["mixT"][NAW + q * P:NAW + (q + 1) * P, :], yT[:, q, :]).then_inc(s_yst, 16)
            sp.wait_ge(s_yst, 16 * Q)

        @block.gpsimd
        def _(pool):
            pool.memset(w4[:, :, :], 0.0).then_inc(s_w4z, 1)

        @block.scalar
        def _(act):
            for t in range(RAD):
                act.wait_ge(s_hp, t + 1)
                act.activation(hs[:, t, :], pu[:, t % 4, :], ACT.Copy).then_inc(s_hs, 1)
                act.wait_ge(s_hs, t + 1)
                act.dma_start(h_v[t], hs[:, t, :]).then_inc(s_hst, 16)
            for k in range(NK):
                for q in range(Q):
                    act.wait_ge(s_y, k * Q + q + 1)
                    last = act.activation(yT[:, q, k::RAD], py[:, q, 0:P], ACT.Copy)
                    if 0 < k < NK - 1:
                        last = act.activation(yT[:, q, SEQ - k::-RAD], py[:, q, P:2 * P], ACT.Copy)
                    last.then_inc(s_yr, 1)

        @block.vector
        def _(dve):
            for v in range(2):
                dve.wait_ge(s_mp, v + 1)
                dve.tensor_copy(mix[:, v, :, :], py[:, v, :].rearrange("p (q c) -> p q c", q=Q)).then_inc(s_mix, 1)
            dve.tensor_scalar(mix[:, 2, :, :], py[:, 1, :].rearrange("p (q c) -> p q c", q=Q), -1.0, None, ALU.mult).then_inc(s_mix, 1)
            for k in range(NK):
                for q in range(Q):
                    n = k * Q + q
                    dve.wait_ge(s_u, n + 1)
                    if k >= 2:
                        dve.wait_ge(s_y, (k - 2) * Q + q + 1)
                    dve.tensor_copy(us[:, k % 2, q, :], pu[:, q, 0:2 * P]).then_inc(s_us, 1)

        @block.tensor
        def _(pe):
            pe.wait_ge(s_k, 32)
            for t in range(RAD):
                pe.wait_ge(s_f[t // 4], 64)
                if t >= 4:
                    pe.wait_ge(s_hs, t - 3)
                pe.matmul(pu[:, t % 4, :], short[:, :], f[:, t, :], start=True, stop=True).then_inc(s_hp, 1)
            pe.wait_ge(s_w4, 32)
            for v in range(2):
                pe.matmul(py[:, v, :], chan[:, v, :], w4[:, :, :].rearrange("p q c -> p (q c)"), start=True, stop=True).then_inc(s_mp, 1)
            pe.wait_ge(s_lk, 16)
            pe.wait_ge(s_hs, RAD)
            pe.wait_ge(s_mix, 3)

            def u(k):
                both = ("sin", k) in part
                pe.wait_ge(s_hb[k], 32 if both else 16)
                for q in range(Q):
                    if k:
                        pe.wait_ge(s_us, (k - 1) * Q + q + 1)
                    cs = slice(q * P, (q + 1) * P)
                    ins = pe.matmul(pu[:, q, 0:2 * P], hb[:, part["cos", k], cs], long[:, k, 0:2 * P], start=True, stop=not both)
                    if both:
                        ins = pe.matmul(pu[:, q, 0:2 * P], hb[:, part["sin", k], cs], long[:, k, 2 * P:4 * P], start=False, stop=True)
                    ins.then_inc(s_u, 1)

            def y(k):
                for q in range(Q):
                    pe.wait_ge(s_us, k * Q + q + 1)
                    if k:
                        pe.wait_ge(s_yr, (k - 1) * Q + q + 1)
                    for sign in ((0, 1) if 0 < k < NK - 1 else (0,)):
                        o = py[:, q, sign * P:(sign + 1) * P]
                        pe.matmul(o, mix[:, 0, q, :], us[:, k % 2, q, 0:P], start=True, stop=False)
                        ins = pe.matmul(o, mix[:, 1 + sign, q, :], us[:, k % 2, q, P:2 * P], start=False, stop=True)
                    ins.then_inc(s_y, 1)

            u(0)
            for k in range(1, NK):
                u(k)
                y(k - 1)
            y(NK - 1)


def attention(nc, sem, A, S):
    ident = A["ident"]
    NBLK = QB * QB
    KR = 16
    LAT = KR * SPAN
    ALL = LAT + CTX
    with ExitStack() as ctx:
        sb = lambda name, shape, dt=F32: ctx.enter_context(nc.sbuf_tensor(name, shape, dt))
        ps = lambda name, shape, dt=F32: ctx.enter_context(nc.psum_tensor(name, shape, dt))
        qT = sb("at_qT", [P, PAIRS, SEQ])
        kT = sb("at_kT", [P, PAIRS, SEQ])
        kcT = sb("at_kcT", [P, PAIRS, CTX])
        vc = sb("at_vc", [P, 2, NAW])
        v = sb("at_v", [P, 2, LAT // P, NAW])
        bias = sb("at_bias", [P, 2, HEADS, LAT])
        qs = sb("at_qs", [P, 2, HEADS, P])
        sn = sb("at_sn", [P, 2, LAT])
        nm = sb("at_nm", [P, 2, 3])
        pr = sb("at_pr", [P, 2, ALL])
        pT = sb("at_pT", [P, 2, ALL])
        sums = sb("at_sums", [P, 2, 2, HEADS])
        den = sb("at_den", [P, 2, HEADS])
        on = sb("at_on", [P, NAW])
        oT = sb("at_oT", [P, PAIRS, SEQ])
        sl = ps("at_sl", [P, 2, LAT])
        sx = ps("at_sx", [P, 2, 512])
        tl = ps("at_tl", [P, LAT])
        tx = ps("at_tx", [P, 512])
        po = ps("at_po", [P, 2, NAW])
        s_q, s_k, s_c = sem("at_q_in"), sem("at_k_in"), sem("at_ctx_in")
        s_v = [sem(f"at_v_in{i}") for i in range(2)]
        s_b = [sem(f"at_bias_in{i}") for i in range(2)]
        s_clr, s_qs, s_qz = sem("at_bias_cleared"), sem("at_queries"), sem("at_queries_zeroed")
        s_s, s_red, s_m = sem("at_scores"), sem("at_reduced"), sem("at_max")
        s_e, s_t, s_evl, s_evx, s_pv = sem("at_exp"), sem("at_turned"), sem("at_turn_read_dve"), sem("at_turn_read_act"), sem("at_pv")
        s_den, s_on, s_ot, s_oe, s_st = sem("at_den"), sem("at_normed"), sem("at_o_turned"), sem("at_o_read"), sem("at_o_out")
        mix_v = S["mixT"][0:NAW, :].rearrange("(c p) t -> p c t", p=P)
        block = ctx.enter_context(nc.Block())

        def corner(t, u):
            R, m = t // 2, t % 2
            return (R + t // 4) * (4 * GRID_W) + (m * 3 + u) * 8, R * (8 * GRID_W) + (m * 2 + u) * WIN_C

        @block.sync
        def _(sp):
            sp.dma_start(qT[:, :, :], S["qT"].rearrange("(c p) t -> p c t", p=P)).then_inc(s_q, 16)
            sp.dma_start(kT[:, :, :], S["kT"].rearrange("(c p) t -> p c t", p=P)).then_inc(s_k, 16)
            sp.dma_start(kcT[:, :, :], S["kcT"].rearrange("(c p) t -> p c t", p=P)).then_inc(s_c, 16)
            sp.dma_start(vc[:, :, :], S["vc"].rearrange("(c p) n -> p c n", p=P)).then_inc(s_c, 16)

            def load(R, m, u):
                row0 = 4 * (R + R // 2)
                b = m * 2 + (4 * R + u)
                if isinstance(b, int) and b < 2:
                    pass
                else:
                    sp.wait_ge(s_pv, (b - 1) * HEADS)
                for kr in range(4):
                    first = m * 24 + (u * 8 + (row0 + kr) * GRID_W)
                    base = S["vf"][ds(first, 32), 0:NAW]
                    src = bass.AP(base.tensor, base.offset, [list(base.ap[0]), [4 * GRID_W * (NAW + FW), 4], [1, NAW]])
                    sp.dma_start(v[32 * kr:32 * kr + 32, u, :, :], src).then_inc(s_v[u], 16)
                sp.wait_ge(s_clr, b + 1)
                for qr in range(8):
                    rel = (max(qr - 4, 0), qr, qr, 4 + min(qr, 4))[R]
                    dr = row0 + rel - (8 * R + qr) + 7
                    src = S["xbias"][ds(m * 2 + u, 1), :, :, dr:dr + 8, :].rearrange("n q h r k -> (n q) h (r k)")
                    sp.dma_start(bias[16 * qr:16 * qr + 16, u, :, rel * SPAN:(rel + 8) * SPAN], src).then_inc(s_b[u], 16)

            for R in range(QB):
                if R == 0:
                    for m in range(2):
                        for u in range(2):
                            load(R, m, u)
                else:
                    with steps(sp, 0, 2) as m:
                        for u in range(2):
                            load(R, m, u)
            sp.wait_ge(s_oe, NBLK)
            for c in range(PAIRS):
                sp.dma_start(mix_v[:, c, :], oT[:, c, :]).then_inc(s_st, 16)
            sp.wait_ge(s_st, 16 * PAIRS)

        @block.gpsimd
        def _(pool):
            def queries(t, u):
                q0 = corner(t, u)[1]
                for a in range(2):
                    base = qT[64 * a:64 * a + 64, 0, q0:q0 + 1] if isinstance(q0, int) else qT[64 * a:64 * a + 64, 0, ds(q0, 1)]
                    src = bass.AP(base.tensor, base.offset, [list(base.ap[0]), [SEQ, PAIRS], [GRID_W, 8], [1, WIN_C]])
                    pool.tensor_copy(qs[64 * a:64 * a + 64, u, a::2, :].rearrange("p c (r k) -> p c r k", r=8), src).then_inc(s_qs, 1)

            pool.memset(qs[:, :, :, :], 0.0).then_inc(s_qz, 1)
            for u in range(2):
                pool.memset(bias[:, u, :, :], -BIG).then_inc(s_clr, 1)
            pool.wait_ge(s_qz, 1)
            pool.wait_ge(s_clr, 2)
            pool.wait_ge(s_q, 16)
            queries(0, 0)
            queries(0, 1)
            with steps(pool, 1, QB * 2) as t:
                for u in range(2):
                    b = t * 2 + u
                    pool.wait_ge(s_clr, b)
                    pool.wait_ge(s_s, (b - 1) * HEADS)
                    pool.nop(nofuse=True)
                    queries(t, u)
                    pool.wait_ge(s_qs, b * 2 + 2)
                    pool.wait_ge(s_m, (b - 1) * HEADS)
                    pool.nop(nofuse=True)
                    pool.memset(bias[:, u, :, :], -BIG).then_inc(s_clr, 1)

        @block.vector
        def _(dve):
            def reduce(t, u, h):
                b = t * 2 + u
                i, w = b * HEADS + h, h % 2
                if h == 0:
                    dve.wait_ge(s_b[u], t * 128 + 128)
                dve.wait_ge(s_s, i + 1)
                pos(dve, s_e, (i - 1) * 2)
                dve.tensor_reduce(nm[:, w, 1:2], sx[:, w, 0:CTX], AX.X, ALU.max, negate=True).then_inc(s_red, 1)
                dve.tensor_tensor_reduce(sn[:, w, :], sl[:, w, :], bias[:, u, h, :], -1.0, 2 * BIG, ALU.add, ALU.min,
                                         nm[:, w, 0:1]).then_inc(s_red, 1)
                dve.wait_ge(s_red, i * 2 + 2)
                dve.tensor_tensor(nm[:, w, 2:3], nm[:, w, 0:1], nm[:, w, 1:2], ALU.min).then_inc(s_m, 1)

            def read_turned(t, u, h):
                i = (t * 2 + u) * HEADS + h
                dve.wait_ge(s_t, i + 1)
                pos(dve, s_pv, i - 1)
                dve.tensor_copy(pT[:, h % 2, 0:LAT], tl[:, :]).then_inc(s_evl, 1)

            def norm(t, u):
                b = t * 2 + u
                dve.wait_ge(s_pv, b * HEADS + HEADS)
                pos(dve, s_ot, b)
                dve.tensor_tensor(den[:, 0, :], sums[:, u, 0, :], sums[:, u, 1, :], ALU.add).then_inc(s_den, 1)
                dve.wait_ge(s_den, b * 2 + 1)
                dve.reciprocal(den[:, 1, :], den[:, 0, :]).then_inc(s_den, 1)
                dve.wait_ge(s_den, b * 2 + 2)
                wide = bass.AP(den[:, 1, :].tensor, den[:, 1, :].offset, [list(den[:, 1, :].ap[0]), [1, HEADS], [0, HD]])
                dve.tensor_tensor(on[:, :].rearrange("p (h d) -> p h d", h=HEADS), po[:, u, :].rearrange("p (h d) -> p h d", h=HEADS),
                                  wide, ALU.mult).then_inc(s_on, 1)

            def body(t):
                first = isinstance(t, int) and t == 0
                for u in range(2):
                    for h in range(HEADS):
                        reduce(t, u, h)
                        if h:
                            read_turned(t, u, h - 1)
                        elif u:
                            read_turned(t, 0, HEADS - 1)
                        elif not first:
                            read_turned(t - 1, 1, HEADS - 1)
                        if h == 2 and not (first and u == 0):
                            norm(t, 0) if u else norm(t - 1, 1)

            body(0)
            with steps(dve, 1, QB * 2) as t:
                body(t)
            read_turned(QB * 2 - 1, 1, HEADS - 1)
            norm(QB * 2 - 1, 1)

        @block.scalar
        def _(act):
            def exps(t, u, h):
                i, w = (t * 2 + u) * HEADS + h, h % 2
                act.wait_ge(s_m, i + 1)
                pos(act, s_t, i - 1)
                act.activation(pr[:, w, LAT:ALL], sx[:, w, 0:CTX], ACT.Exp, bias=nm[:, w, 2:3],
                               accum_out=sums[:, u, 1, h:h + 1]).then_inc(s_e, 1)
                act.activation(pr[:, w, 0:LAT], sn[:, w, :], ACT.Exp, bias=nm[:, w, 2:3], scale=-1.0,
                               accum_out=sums[:, u, 0, h:h + 1]).then_inc(s_e, 1)

            def read_turned(t, u, h):
                i = (t * 2 + u) * HEADS + h
                act.wait_ge(s_t, i + 1)
                act.activation(pT[:, h % 2, LAT:ALL], tx[:, 0:CTX], ACT.Copy).then_inc(s_evx, 1)

            def keep(t, u):
                b = t * 2 + u
                act.wait_ge(s_ot, b + 1)
                q0 = corner(t, u)[1]
                base = oT[:, 0, ds(q0, 1)] if not isinstance(q0, int) else oT[:, 0, q0:q0 + 1]
                dst = bass.AP(base.tensor, base.offset, [list(base.ap[0]), [SEQ, PAIRS], [GRID_W, 8], [1, WIN_C]])
                act.activation(dst, po[:, u, :].rearrange("p (c r k) -> p c r k", c=PAIRS, r=8), ACT.Copy).then_inc(s_oe, 1)

            def body(t):
                first = isinstance(t, int) and t == 0
                for u in range(2):
                    for h in range(HEADS):
                        exps(t, u, h)
                        if h:
                            read_turned(t, u, h - 1)
                        elif u:
                            read_turned(t, 0, HEADS - 1)
                        elif not first:
                            read_turned(t - 1, 1, HEADS - 1)
                        if h == 5 and not (first and u == 0):
                            keep(t, 0) if u else keep(t - 1, 1)

            body(0)
            with steps(act, 1, QB * 2) as t:
                body(t)
            read_turned(QB * 2 - 1, 1, HEADS - 1)
            keep(QB * 2 - 1, 1)

        @block.tensor
        def _(pe):
            def scores(t, u, h):
                b = t * 2 + u
                i, w = b * HEADS + h, h % 2
                if h == 0:
                    pe.wait_ge(s_qs, b * 2 + 2)
                pos(pe, s_m, i - 1)
                pos(pe, s_e, (i - 1) * 2)
                k0 = corner(t, u)[0]
                base = kT[:, h // 2, ds(k0, 1)] if not isinstance(k0, int) else kT[:, h // 2, k0:k0 + 1]
                keys = bass.AP(base.tensor, base.offset, [list(base.ap[0]), [GRID_W, KR], [1, SPAN]])
                q = qs[:, u, h, :]
                pe.matmul(sl[:, w, :], q, keys, start=True, stop=True)
                pe.matmul(sx[:, w, 0:CTX], q, kcT[:, h // 2, :], start=True, stop=True).then_inc(s_s, 1)

            def turn(t, u, h):
                i, w = (t * 2 + u) * HEADS + h, h % 2
                pe.wait_ge(s_e, i * 2 + 2)
                pos(pe, s_evl, i)
                pos(pe, s_evx, i)
                for c in range(LAT // P):
                    pe.transpose(tl[:, c * P:(c + 1) * P], pr[:, w, c * P:(c + 1) * P], ident[:, :])
                for c in range(CTX // P):
                    ins = pe.transpose(tx[:, c * P:(c + 1) * P], pr[:, w, LAT + c * P:LAT + (c + 1) * P], ident[:, :])
                ins.then_inc(s_t, 1)

            def weigh(t, u, h):
                b = t * 2 + u
                i, w = b * HEADS + h, h % 2
                if h == 0:
                    pe.wait_ge(s_v[u], t * 64 + 64)
                    pos(pe, s_oe, b - 1)
                pe.wait_ge(s_evl, i + 1)
                pe.wait_ge(s_evx, i + 1)
                o = po[:, u, h * HD:(h + 1) * HD]
                n = LAT // P
                for c in range(n):
                    pe.matmul(o, pT[:, w, c * P:(c + 1) * P], v[:, u, c, h * HD:(h + 1) * HD], start=(c == 0), stop=False)
                for c in range(2):
                    ins = pe.matmul(o, pT[:, w, LAT + c * P:LAT + (c + 1) * P], vc[:, c, h * HD:(h + 1) * HD], start=False, stop=(c == 1))
                ins.then_inc(s_pv, 1)

            def turn_o(t, u):
                pe.wait_ge(s_on, t * 2 + u + 1)
                for c in range(PAIRS):
                    ins = pe.transpose(po[:, u, c * P:(c + 1) * P], on[:, c * P:(c + 1) * P], ident[:, :])
                ins.then_inc(s_ot, 1)

            def body(t, last):
                first = isinstance(t, int) and t == 0
                for u in range(2):
                    for h in range(HEADS):
                        if h < HEADS - 1:
                            scores(t, u, h + 1)
                        elif not u:
                            scores(t, 1, 0)
                        elif not last:
                            scores(t + 1, 0, 0)
                        turn(t, u, h)
                        if h:
                            weigh(t, u, h - 1)
                        elif u:
                            weigh(t, 0, HEADS - 1)
                        elif not first:
                            weigh(t - 1, 1, HEADS - 1)
                        if h == 4 and not (first and u == 0):
                            turn_o(t, 0) if u else turn_o(t - 1, 1)

            pe.wait_ge(s_k, 16)
            pe.wait_ge(s_c, 32)
            scores(0, 0, 0)
            body(0, False)
            with steps(pe, 1, QB * 2 - 1) as t:
                body(t, False)
            body(QB * 2 - 1, True)
            weigh(QB * 2 - 1, 1, HEADS - 1)
            turn_o(QB * 2 - 1, 1)


def mixing(nc, sem, A, x, w_out, ln_g, ln_b, w_router, S):
    modc, ident, gate2, score = A["modc"], A["ident"], A["gate2"], A["score"]
    N0 = 3 * DC
    with ExitStack() as ctx:
        sb = lambda name, shape, dt=F32: ctx.enter_context(nc.sbuf_tensor(name, shape, dt))
        ps = lambda name, shape, dt=F32: ctx.enter_context(nc.psum_tensor(name, shape, dt))
        whi = sb("mi_whi", [P, DC, D], F32R)
        wlo = sb("mi_wlo", [P, DC, D], F32R)
        wst = sb("mi_wst", [P, 2, D])
        mt = sb("mi_mt", [P, 2, DC, P])
        mhi = sb("mi_mhi", [P, 2, DC, P], F32R)
        mlo = sb("mi_mlo", [P, 2, DC, P], F32R)
        xt = sb("mi_x", [P, 2, D])
        r = sb("mi_r", [P, D])
        x1 = sb("mi_x1", [P, 2, D])
        z2 = sb("mi_z2", [P, 2, D])
        h2 = sb("mi_h2", [P, 2, DC, P])
        g, b = sb("mi_g", [P, D]), sb("mi_b", [P, D])
        wr = sb("mi_wr", [P, DC, E])
        st, mv, rs = sb("mi_st", [P, 2, 12]), sb("mi_mv", [P, 2, 2]), sb("mi_rs", [P, 2, 2])
        half = sb("mi_half", [P, 2])
        y = ps("mi_y", [P, 2, D])
        turned = ps("mi_turned", [P, 2, 512])
        logit = ps("mi_logit", [P, 512])
        s_w = [sem(f"mi_w_in{i}") for i in range(2)]
        s_g, s_m2 = sem("mi_ln_in"), sem("mi_w_gated")
        s_whi, s_wlo = sem("mi_w_hi"), sem("mi_w_lo")
        s_mt = [sem(f"mi_mix_in{i}") for i in range(2)]
        s_x = [sem(f"mi_x_in{i}") for i in range(2)]
        s_mhi, s_mlo, s_y = sem("mi_mix_hi"), sem("mi_mix_lo"), sem("mi_y_done")
        s_r, s_dv, s_mom, s_ve, s_rs = sem("mi_residual"), sem("mi_dve_step"), sem("mi_moments"), sem("mi_var_eps"), sem("mi_rstd")
        s_x1, s_z2 = sem("mi_x1"), sem("mi_z2")
        s_x1s = [sem(f"mi_x1_out{i}") for i in range(2)]
        s_z2s = [sem(f"mi_z2_out{i}") for i in range(2)]
        s_turn, s_h2, s_lg, s_sg, s_half = sem("mi_turned"), sem("mi_h2"), sem("mi_logits"), sem("mi_score"), sem("mi_half")
        mix_v = S["mixT"].rearrange("(c p) t -> p c t", p=P)
        block = ctx.enter_context(nc.Block())
        DV = 4

        @block.sync
        def _(sp):
            for j in range(DC):
                if j >= 2:
                    sp.wait_ge(s_wlo, j - 1)
                sp.dma_start(wst[:, j % 2, :], w_out[j * P:(j + 1) * P, :]).then_inc(s_w[j % 2], 16)
                if j == 1:
                    for t in range(2):
                        sp.dma_start(mt[:, t, :, :], mix_v[:, :, t * P:(t + 1) * P]).then_inc(s_mt[t], 16)
                        sp.dma_start(xt[:, t, :], x[t * P:(t + 1) * P, :]).then_inc(s_x[t], 16)
            sp.dma_start(wr[:, :, :], w_router.rearrange("(j p) e -> p j e", p=P)).then_inc(s_g, 16)
            sp.dma_start(g[:, :], ln_g.partition_broadcast(P)).then_inc(s_g, 16)
            sp.dma_start(b[:, :], ln_b.partition_broadcast(P)).then_inc(s_g, 16)
            with steps(sp, 2, TILES, 2) as t0:
                for u in range(2):
                    t = t0 + u
                    sp.wait_ge(s_mlo, t - 1)
                    sp.dma_start(mt[:, u, :, :], mix_v[:, :, ds(t * P, P)]).then_inc(s_mt[u], 16)
                    sp.wait_ge(s_r, (t - 1) * 2)
                    sp.dma_start(xt[:, u, :], x[ds(t * P, P), :]).then_inc(s_x[u], 16)

        @block.gpsimd
        def _(pool):
            pool.memset(half[:, 0:1], -0.5).then_inc(s_half, 1)
            pool.memset(half[:, 1:2], EPS).then_inc(s_half, 1)
            pool.wait_ge(s_half, 2)

            def lo(t, u):
                pool.wait_ge(s_mhi, t + 1)
                pool.tensor_tensor(mlo[:, u, :, :], mt[:, u, :, :], mhi[:, u, :, :].bitcast(F32), ALU.subtract).then_inc(s_mlo, 1)

            def rstd(n, k):
                pool.wait_ge(s_mom, n + 1)
                pool.tensor_tensor(rs[:, k, 0:1], mv[:, k, 1:2], half[:, 1:2], ALU.add).then_inc(s_ve, 1)
                pool.wait_ge(s_ve, n + 1)
                pool.tensor_tensor(rs[:, k, 1:2], rs[:, k, 0:1], half[:, 0:1], ALU.pow).then_inc(s_rs, 1)

            lo(0, 0)
            lo(1, 1)
            with steps(pool, 0, TILES - 2, 2) as t0:
                for u in range(2):
                    t = t0 + u
                    rstd(t * 2, 0)
                    lo(t + 2, u)
                    rstd(t * 2 + 1, 1)
            for t in range(TILES - 2, TILES):
                rstd(2 * t, 0)
                rstd(2 * t + 1, 1)

        @block.vector
        def _(dve):
            for j in range(DC):
                dve.wait_ge(s_w[j % 2], 16 * (j // 2 + 1))
                dve.tensor_tensor(wst[:, j % 2, :], wst[:, j % 2, :], gate2[:, :], ALU.mult).then_inc(s_m2, 1)
                dve.wait_ge(s_whi, j + 1)
                dve.tensor_tensor(wlo[:, j, :], wst[:, j % 2, :], whi[:, j, :].bitcast(F32), ALU.subtract).then_inc(s_wlo, 1)

            def stats(src, k):
                for i in range(2):
                    ins = dve.bn_stats(st[:, k, 6 * i:6 * i + 6], src[:, 512 * i:512 * i + 512])
                ins.then_inc(s_dv, 1)

            def tile(t, u, first):
                d = t * DV
                dve.wait_ge(s_x[u], t * 8 + 16 - 8 * u)
                dve.wait_ge(s_y, t + 1)
                for i in range(2):
                    c = slice(512 * i, 512 * i + 512)
                    dve.scalar_tensor_tensor(out=r[:, c], in0=xt[:, u, c], scalar=ALPHA, in1=y[:, u, c],
                                             op0=ALU.mult, op1=ALU.add).then_inc(s_r, 1)
                dve.wait_ge(s_r, t * 2 + 2)
                stats(r, 0)
                dve.wait_ge(s_dv, d + 1)
                dve.nop(nofuse=True)
                dve.bn_aggr(mv[:, 0, :], st[:, 0, :]).then_inc(s_mom, 1)
                dve.wait_ge(s_rs, t * 2 + 1)
                dve.tensor_scalar(r[:, :], r[:, :], mv[:, 0, 0:1], rs[:, 0, 1:2], ALU.subtract, ALU.mult).then_inc(s_dv, 1)
                dve.wait_ge(s_dv, d + 2)
                dve.tensor_tensor(r[:, :], r[:, :], g[:, :], ALU.mult).then_inc(s_dv, 1)
                if not first:
                    dve.wait_ge(s_x1s[u], t * 8 - 8 * u)
                dve.wait_ge(s_dv, d + 3)
                dve.tensor_tensor(x1[:, u, :], r[:, :], b[:, :], ALU.add).then_inc(s_x1, 1)
                dve.wait_ge(s_x1, t + 1)
                stats(x1[:, u, :], 1)
                dve.wait_ge(s_dv, d + 4)
                dve.nop(nofuse=True)
                dve.bn_aggr(mv[:, 1, :], st[:, 1, :]).then_inc(s_mom, 1)
                dve.wait_ge(s_rs, t * 2 + 2)
                if not first:
                    dve.wait_ge(s_z2s[u], t * 8 - 8 * u)
                    dve.wait_ge(s_turn, t - 1)
                dve.tensor_scalar(z2[:, u, :], x1[:, u, :], mv[:, 1, 0:1], rs[:, 1, 1:2], ALU.subtract, ALU.mult).then_inc(s_z2, 1)

            dve.wait_ge(s_g, 48)
            tile(0, 0, True)
            tile(1, 1, True)
            with steps(dve, 2, TILES, 2) as t0:
                for u in range(2):
                    tile(t0 + u, u, False)

        @block.scalar
        def _(act):
            def hi(t, u):
                act.wait_ge(s_mt[u], t * 8 + 16 - 8 * u)
                pos(act, s_y, t - 1)
                act.activation(mhi[:, u, :, :], mt[:, u, :, :], ACT.Copy).then_inc(s_mhi, 1)

            def modulate(t, u):
                act.wait_ge(s_turn, t + 1)
                pos(act, s_lg, t - 1)
                for j in range(DC):
                    ins = act.activation(h2[:, u, j, :], turned[:, j // 4, (j % 4) * P:(j % 4 + 1) * P], ACT.Identity,
                                         bias=modc[:, 0, N0 + j:N0 + j + 1], scale=modc[:, 0, N0 + DC + j:N0 + DC + j + 1])
                ins.then_inc(s_h2, 1)

            def scores(t):
                act.wait_ge(s_lg, t + 1)
                cols = score[:, ds(t, 1), :].rearrange("p a e -> p (a e)") if not isinstance(t, int) else score[:, t, :]
                act.activation(cols, logit[:, 0:E], ACT.Sigmoid).then_inc(s_sg, 1)

            def store(t, u):
                rows = ds(t * P, P) if not isinstance(t, int) else slice(t * P, (t + 1) * P)
                act.wait_ge(s_x1, t + 1)
                act.dma_start(S["x1"][rows, :], x1[:, u, :]).then_inc(s_x1s[u], 16)
                act.wait_ge(s_z2, t + 1)
                act.dma_start(S["z2"][rows, :], z2[:, u, :]).then_inc(s_z2s[u], 16)

            for j in range(DC):
                act.wait_ge(s_m2, j + 1)
                act.activation(whi[:, j, :], wst[:, j % 2, :], ACT.Copy).then_inc(s_whi, 1)
                if j == 1:
                    hi(0, 0)
                    hi(1, 1)
            hi(2, 0)
            store(0, 0)
            hi(3, 1)
            modulate(0, 0)
            store(1, 1)
            with steps(act, 2, TILES - 2, 2) as t0:
                for u in range(2):
                    t = t0 + u
                    hi(t + 2, u)
                    modulate(t - 1, 1 - u)
                    scores(t - 2)
                    store(t, u)
            for t in range(TILES - 2, TILES + 2):
                if t - 1 < TILES:
                    modulate(t - 1, (t - 1) % 2)
                scores(t - 2)
                if t < TILES:
                    store(t, t % 2)
            act.wait_ge(s_sg, TILES)
            for u in range(2):
                act.wait_ge(s_x1s[u], 8 * TILES)
                act.wait_ge(s_z2s[u], 8 * TILES)

        @block.tensor
        def _(pe):
            def products(t, u):
                pe.wait_ge(s_mlo, t + 1)
                pos(pe, s_r, (t - 1) * 2)
                for j in range(DC):
                    for i in range(2):
                        c = slice(512 * i, 512 * i + 512)
                        pe.matmul(y[:, u, c], mhi[:, u, j, :], whi[:, j, c], start=(j == 0), stop=False)
                        pe.matmul(y[:, u, c], mhi[:, u, j, :], wlo[:, j, c], start=False, stop=False)
                    for i in range(2):
                        c = slice(512 * i, 512 * i + 512)
                        ins = pe.matmul(y[:, u, c], mlo[:, u, j, :], whi[:, j, c], start=False, stop=(j == DC - 1))
                ins.then_inc(s_y, 1)

            def turn(t, u):
                pe.wait_ge(s_z2, t + 1)
                pos(pe, s_h2, t)
                for j in range(DC):
                    ins = pe.transpose(turned[:, j // 4, (j % 4) * P:(j % 4 + 1) * P], z2[:, u, j * P:(j + 1) * P], ident[:, :])
                ins.then_inc(s_turn, 1)

            def route(t, u):
                pe.wait_ge(s_h2, t + 1)
                pos(pe, s_sg, t)
                for j in range(DC):
                    ins = pe.matmul(logit[:, 0:E], h2[:, u, j, :], wr[:, j, :], start=(j == 0), stop=(j == DC - 1))
                ins.then_inc(s_lg, 1)

            pe.wait_ge(s_wlo, DC)
            pe.wait_ge(s_g, 48)
            products(0, 0)
            products(1, 1)
            turn(0, 0)
            with steps(pe, 2, TILES, 2) as t0:
                for u in range(2):
                    t = t0 + u
                    products(t, u)
                    turn(t - 1, 1 - u)
                    route(t - 2, u)
            turn(TILES - 1, 1)
            route(TILES - 2, 0)
            route(TILES - 1, 1)


def routing(nc, sem, A, router_bias, K, S):
    score, slots, gates, table = A["score"], A["slots"], A["gates"], A["table"]
    T, J, KT = TILES, SLOT_TILES, SEQ // P
    with ExitStack() as ctx:
        sb = lambda name, shape, dt=F32: ctx.enter_context(nc.sbuf_tensor(name, shape, dt))
        ps = lambda name, shape, dt=F32: ctx.enter_context(nc.psum_tensor(name, shape, dt))
        rb = sb("ro_rb", [P, E])
        less4, less16 = sb("ro_less4", [P, 4, 4]), sb("ro_less16", [P, E, E])
        iot = sb("ro_iota", [P, J])
        k128 = sb("ro_k128", [P, KT])
        triu, ones = sb("ro_triu", [P, P]), sb("ro_ones", [P, P])
        sbias = sb("ro_sbias", [P, T, E])
        gt, eq = sb("ro_gt", [P, T * NG, 4, 4]), sb("ro_eq", [P, T * NG, 4, 4])
        rank, top = sb("ro_rank", [P, T * NG, 4]), sb("ro_top", [P, T * NG, 4])
        gs = sb("ro_gs", [P, T, NG])
        grank = sb("ro_grank", [P, T, NG])
        sel, w = sb("ro_sel", [P, T, E]), sb("ro_w", [P, T, E])
        tmp = sb("ro_tmp", [P, T, E])
        tsum = sb("ro_tsum", [P, 2, T])
        cnt = sb("ro_cnt", [P, E])
        full = sb("ro_full", [P, E, KT])
        nt, start, end, used = (sb(f"ro_{n}", [P, E]) for n in ("nt", "start", "end", "used"))
        sq = sb("ro_sq", [P, E, E])
        slot = sb("ro_slot", [P, T, E])
        ab = sb("ro_ab", [P, 2, T])
        jt = sb("ro_jt", [P, J, E])
        jt2 = sb("ro_jt2", [P, J, E])
        jrow = sb("ro_jrow", [P, 3, J])
        zero = sb("ro_zero", [P, J], U32)
        tok = sb("ro_tok", [P, T], U32)
        lo7, hi7, where = sb("ro_lo7", [P, 2, T], U32), sb("ro_hi7", [P, 2, T], U32), sb("ro_where", [P, 2, T], U32)
        before = ps("ro_before", [P, T, E])
        total = ps("ro_total", [P, E])
        s_in, s_one, s_z, s_zst, s_tok = sem("ro_in"), sem("ro_ones"), sem("ro_zero"), sem("ro_zero_out"), sem("ro_tok")
        s_dv, s_sel, s_cnt, s_where, s_sc = sem("ro_dve_step"), sem("ro_sel"), sem("ro_counted"), sem("ro_where"), sem("ro_scattered")
        block = ctx.enter_context(nc.Block())

        @block.sync
        def _(sp):
            sp.dma_start(rb[:, :], router_bias.partition_broadcast(P)).then_inc(s_in, 16)
            sp.dma_start(less4[:, :, :], K["k_less4"].partition_broadcast(P)).then_inc(s_in, 16)
            sp.dma_start(less16[:, :, :], K["k_less16"].partition_broadcast(P)).then_inc(s_in, 16)
            sp.dma_start(iot[:, :], K["k_iota"].partition_broadcast(P)).then_inc(s_in, 16)
            sp.dma_start(triu[:, :], K["k_triu"]).then_inc(s_in, 16)
            sp.wait_ge(s_z, 1)
            sp.dma_start(S["tokens"].rearrange("(p j) a -> p (j a)", p=P), zero[:, :]).then_inc(s_zst, 16)

        @block.gpsimd
        def _(pool):
            pool.memset(ones[:, :], 1.0).then_inc(s_one, 1)
            pool.memset(zero[:, :], 0).then_inc(s_z, 1)
            pool.iota(tok[:, :], pattern=[[P, T]], base=0, channel_multiplier=1).then_inc(s_tok, 1)
            pool.wait_ge(s_tok, 1)
            pool.wait_ge(s_zst, 16)
            pool.wait_ge(s_where, 1)
            for t in range(T):
                for k in range(2):
                    pool.indirect_dma_start(out=S["tokens"], out_offset=bass.IndirectOffsetOnAxis(ap=where[:, k, t:t + 1], axis=0),
                                            in_=tok[:, t:t + 1], in_offset=None).then_inc(s_sc, 16)
            pool.wait_ge(s_sc, 32 * T)

        @block.vector
        def _(dve):
            n = [0]

            def step(ins):
                n[0] += 1
                ins.then_inc(s_dv, 1)
                dve.wait_ge(s_dv, n[0])

            def wide(ap, pattern):
                return bass.AP(ap.tensor, ap.offset, [list(ap.ap[0])] + pattern)

            def ranks(vals, count, out):
                mine, other = wide(vals, [[4, count], [1, 4], [0, 4]]), wide(vals, [[4, count], [0, 4], [1, 4]])
                dve.tensor_tensor(gt[:, 0:count], other, mine, ALU.is_gt)
                step(dve.tensor_tensor(eq[:, 0:count], other, mine, ALU.is_equal))
                step(dve.tensor_tensor(eq[:, 0:count], eq[:, 0:count], wide(less4[:, 0, 0:1], [[0, count], [4, 4], [1, 4]]), ALU.mult))
                step(dve.tensor_tensor(gt[:, 0:count], gt[:, 0:count], eq[:, 0:count], ALU.add))
                step(dve.tensor_reduce(out, gt[:, 0:count], AX.X, ALU.add))

            dve.wait_ge(s_in, 80)
            step(dve.tensor_scalar(k128[:, :], iot[:, 0:KT], float(P), None, ALU.mult))
            step(dve.tensor_tensor(sbias[:, :, :], score[:, :, :], wide(rb[:, 0:1], [[0, T], [1, E]]), ALU.add))
            ranks(sbias[:, 0, 0:1], T * NG, rank[:, :, :])
            step(dve.tensor_scalar(top[:, :, :], rank[:, :, :], 2.0, None, ALU.is_lt))
            top_e = top[:, :, :].rearrange("p (t g) j -> p t (g j)", g=NG)
            step(dve.tensor_tensor(tmp[:, :, :], sbias[:, :, :], top_e, ALU.mult))
            step(dve.tensor_reduce(gs[:, :, :], tmp[:, :, :].rearrange("p t (g j) -> p t g j", g=NG), AX.X, ALU.add))
            ranks(gs[:, 0, 0:1], T, grank[:, :, :])
            step(dve.tensor_scalar(grank[:, :, :], grank[:, :, :], 1.0, None, ALU.is_lt))
            step(dve.tensor_tensor(sel[:, :, :].rearrange("p t (g j) -> p (t g) j", g=NG), top[:, :, :],
                                   wide(grank[:, 0, 0:1], [[1, T * NG], [0, 4]]), ALU.mult))
            step(dve.tensor_tensor(w[:, :, :], sel[:, :, :], score[:, :, :], ALU.mult))
            n[0] += 1
            dve.tensor_reduce(tsum[:, 0, :], w[:, :, :], AX.X, ALU.add).then_inc(s_dv, 1)
            dve.wait_ge(s_dv, n[0])
            step(dve.reciprocal(tsum[:, 1, :], tsum[:, 0, :]))
            dve.tensor_tensor(w[:, :, :], w[:, :, :], wide(tsum[:, 1, 0:1], [[1, T], [0, E]]), ALU.mult).then_inc(s_sel, 1)
            dve.wait_ge(s_sel, 1)
            dve.wait_ge(s_cnt, 1)
            step(dve.tensor_copy(cnt[:, :], total[:, :]))
            step(dve.tensor_tensor(full[:, :, :], wide(cnt[:, 0:1], [[1, E], [0, KT]]), wide(k128[:, 0:1], [[0, E], [1, KT]]), ALU.is_gt))
            step(dve.tensor_reduce(nt[:, :], full[:, :, :], AX.X, ALU.add))
            step(dve.tensor_tensor(sq[:, :, :], less16[:, :, :], wide(nt[:, 0:1], [[0, E], [1, E]]), ALU.mult))
            step(dve.tensor_reduce(start[:, :], sq[:, :, :], AX.X, ALU.add))
            dve.tensor_tensor(end[:, :], start[:, :], nt[:, :], ALU.add)
            dve.tensor_scalar(used[:, :], nt[:, :], 0.0, None, ALU.is_gt)
            step(dve.tensor_scalar(start[:, :], start[:, :], float(P), None, ALU.mult))
            step(dve.tensor_tensor(slot[:, :, :], before[:, :, :], wide(start[:, 0:1], [[0, T], [1, E]]), ALU.add))
            step(dve.tensor_scalar(tmp[:, :, :], sel[:, :, :], -1.0e6, 1.0e6, ALU.mult, ALU.add))
            step(dve.tensor_tensor(tmp[:, :, :], tmp[:, :, :], slot[:, :, :], ALU.add))
            step(dve.tensor_reduce(ab[:, 0, :], tmp[:, :, :], AX.X, ALU.min))
            step(dve.tensor_tensor(tmp[:, :, :], sel[:, :, :], slot[:, :, :], ALU.mult))
            step(dve.tensor_reduce(ab[:, 1, :], tmp[:, :, :], AX.X, ALU.max))
            step(dve.tensor_copy(slots[:, :, :], ab[:, :, :]))
            for k in range(2):
                step(dve.tensor_tensor(tmp[:, :, :], slot[:, :, :], wide(ab[:, k, 0:1], [[1, T], [0, E]]), ALU.is_equal))
                step(dve.tensor_tensor(tmp[:, :, :], tmp[:, :, :], w[:, :, :], ALU.mult))
                step(dve.tensor_reduce(gates[:, k, :], tmp[:, :, :], AX.X, ALU.add))
            dve.tensor_scalar(lo7[:, :, :], slots[:, :, :], P - 1, None, ALU.bitwise_and)
            step(dve.tensor_scalar(hi7[:, :, :], slots[:, :, :], 7, None, ALU.logical_shift_right))
            dve.scalar_tensor_tensor(out=where[:, :, :], in0=lo7[:, :, :], scalar=float(J), in1=hi7[:, :, :],
                                     op0=ALU.mult, op1=ALU.add).then_inc(s_where, 1)
            step(dve.tensor_tensor(jt[:, :, :], wide(end[:, 0:1], [[0, J], [1, E]]), wide(iot[:, 0:1], [[1, J], [0, E]]), ALU.is_le))
            dve.tensor_reduce(jrow[:, 0, :], jt[:, :, :], AX.X, ALU.add)
            step(dve.tensor_tensor(jt2[:, :, :], jt[:, :, :], wide(used[:, 0:1], [[0, J], [1, E]]), ALU.mult))
            step(dve.tensor_reduce(jrow[:, 1, :], jt2[:, :, :], AX.X, ALU.add))
            step(dve.tensor_scalar(jrow[:, 0, :], jrow[:, 0, :], float(E - 1), None, ALU.min))
            dve.tensor_tensor(jrow[:, 2, 1:J], jrow[:, 1, 1:J], jrow[:, 1, 0:J - 1], ALU.subtract)
            step(dve.memset(jrow[:, 2, 0:1], 1.0))
            step(dve.tensor_copy(table[:, :, :], jrow[:, :, :]))
            step(dve.tensor_scalar(table[:, 1, :], table[:, 1, :], 1, None, ALU.bitwise_and))

        @block.tensor
        def _(pe):
            pe.wait_ge(s_in, 80)
            pe.wait_ge(s_one, 1)
            pe.wait_ge(s_sel, 1)
            flat = before[:, :, :].rearrange("p t e -> p (t e)")
            pe.matmul(flat, triu[:, :], sel[:, :, :].rearrange("p t e -> p (t e)"), start=True, stop=False, skip_group_check=True)
            for t in range(T - 1):
                one = sel[:, t, 0:1]
                moving = bass.AP(one.tensor, one.offset, [list(one.ap[0]), [0, T - 1 - t], [1, E]])
                pe.matmul(flat[:, (t + 1) * E:T * E], ones[:, :], moving, start=False, stop=(t == T - 2), skip_group_check=True)
            for t in range(T):
                ins = pe.matmul(total[:, :], ones[:, :], sel[:, t, :], start=(t == 0), stop=(t == T - 1))
            ins.then_inc(s_cnt, 1)


def experts(nc, sem, A, w_gate, w_up, w_down, S):
    modc, ident, gate5, table = A["modc"], A["ident"], A["gate5"], A["table"]
    N0, J, FC = 3 * DC, SLOT_TILES, DE // P
    with ExitStack() as ctx:
        sb = lambda name, shape, dt=F32: ctx.enter_context(nc.sbuf_tensor(name, shape, dt))
        ps = lambda name, shape, dt=F32: ctx.enter_context(nc.psum_tensor(name, shape, dt))
        tok = sb("ex_tok", [P, J], U32)
        cell = sb("ex_cell", [P, 2, 1], U32)
        xg = sb("ex_x", [P, 2, D])
        hT = sb("ex_hT", [P, 2, DC, P])
        wgu = sb("ex_wgu", [P, 2, DC, 2 * DE])
        wd = sb("ex_wd", [P, 2, FC, D])
        sg = sb("ex_silu", [P, 2, DE])
        hid = sb("ex_hid", [P, 2, DE])
        hidT = sb("ex_hidT", [P, 2, DE])
        y = sb("ex_y", [P, 2, D])
        pg = ps("ex_pgu", [P, 2, 2 * DE])
        ph = ps("ex_phid", [P, 512])
        py = ps("ex_py", [P, D])
        turned = ps("ex_turned", [P, 2, 512])
        s_tok, s_cell = sem("ex_tok_in"), sem("ex_cell")
        s_x = [sem(f"ex_x_in{i}") for i in range(2)]
        s_wg = [sem(f"ex_gate_up_in{i}") for i in range(2)]
        s_wd = [sem(f"ex_down_in{i}") for i in range(2)]
        s_turn, s_hT, s_gu, s_silu, s_hid = sem("ex_turned"), sem("ex_hT"), sem("ex_gate_up"), sem("ex_silu"), sem("ex_hid")
        s_th, s_hidT, s_dn, s_y = sem("ex_hid_turned"), sem("ex_hidT"), sem("ex_down"), sem("ex_y")
        s_yst = [sem(f"ex_y_out{i}") for i in range(2)]
        block = ctx.enter_context(nc.Block())

        def tile_value(eng, row, j, top):
            cell = table[0:1, row, j:j + 1] if isinstance(j, int) else table[0:1, row, ds(j, 1)]
            return eng.value_load(cell, min_val=0, max_val=top)

        @block.sync
        def _(sp):
            sp.dma_start(tok[:, :], S["tokens"].rearrange("(p j) a -> p (j a)", p=P)).then_inc(s_tok, 16)

            def gate_up(j, u):
                pos(sp, s_gu, j - 1)
                sp.nop(nofuse=True)
                e, par, new = (tile_value(sp, k, j, m) for k, m in enumerate((E - 1, 1, 1)))
                for k, w in enumerate((w_gate, w_up)):
                    sp.dma_start(wgu[:, ds(par, 1), :, k * DE:(k + 1) * DE].rearrange("p a j f -> p (a j) f"),
                                 w[ds(e, 1), :, :].rearrange("a (j p) f -> p (a j) f", p=P), cond=new).then_inc(s_wg[u], 16)

            def down(j, u):
                e, par, new = (tile_value(sp, k, j, m) for k, m in enumerate((E - 1, 1, 1)))
                sp.dma_start(wd[:, ds(par, 1), :, :].rearrange("p a c n -> p (a c) n"),
                             w_down[ds(e, 1), :, :].rearrange("a (c p) n -> p (a c) n", p=P), cond=new).then_inc(s_wd[u], 16)

            gate_up(0, 0)
            down(0, 0)
            gate_up(1, 1)
            down(1, 1)
            with steps(sp, 2, J, 2) as j0:
                for u in range(2):
                    gate_up(j0 + u, u)
                    sp.wait_ge(s_dn, j0 + u - 1)
                    sp.nop(nofuse=True)
                    down(j0 + u, u)

        @block.gpsimd
        def _(pool):
            pool.wait_ge(s_tok, 16)

            def gather(j, u):
                pool.tensor_copy(cell[:, u, :], tok[:, j:j + 1] if isinstance(j, int) else tok[:, ds(j, 1)]).then_inc(s_cell, 1)
                pool.wait_ge(s_cell, j + 1)
                pool.nop(nofuse=True)
                pool.indirect_dma_start(out=xg[:, u, :], out_offset=None, in_=S["z2"],
                                        in_offset=bass.IndirectOffsetOnAxis(ap=cell[:, u, :], axis=0)).then_inc(s_x[u], 16)

            gather(0, 0)
            gather(1, 1)
            with steps(pool, 2, J, 2) as j0:
                for u in range(2):
                    pool.wait_ge(s_turn, j0 + u - 1)
                    pool.nop(nofuse=True)
                    gather(j0 + u, u)

        @block.scalar
        def _(act):
            def modulate(j, u):
                act.wait_ge(s_turn, j + 1)
                pos(act, s_gu, j - 1)
                for c in range(DC):
                    ins = act.activation(hT[:, u, c, :], turned[:, c // 4, (c % 4) * P:(c % 4 + 1) * P], ACT.Identity,
                                         bias=modc[:, 0, N0 + c:N0 + c + 1], scale=modc[:, 0, N0 + DC + c:N0 + DC + c + 1])
                ins.then_inc(s_hT, 1)

            def gate(j, u):
                act.wait_ge(s_gu, j + 1)
                pos(act, s_hid, j - 1)
                act.activation(sg[:, u, :], pg[:, u, 0:DE], ACT.Silu).then_inc(s_silu, 1)

            def store(j, u):
                rows = ds(j * P, P) if not isinstance(j, int) else slice(j * P, (j + 1) * P)
                act.wait_ge(s_y, j * 2 + 2)
                act.dma_start(S["ye"][rows, :], y[:, u, :]).then_inc(s_yst[u], 16)

            modulate(0, 0)
            modulate(1, 1)
            gate(0, 0)
            modulate(2, 0)
            gate(1, 1)
            store(0, 0)
            with steps(act, 2, J - 2, 2) as j0:
                for u in range(2):
                    modulate(j0 + u + 1, 1 - u)
                    gate(j0 + u, u)
                    store(j0 + u - 1, 1 - u)
            modulate(J - 1, 1)
            gate(J - 2, 0)
            store(J - 3, 1)
            gate(J - 1, 1)
            store(J - 2, 0)
            store(J - 1, 1)
            for u in range(2):
                act.wait_ge(s_yst[u], 8 * J)

        @block.vector
        def _(dve):
            def hidden(j, u):
                dve.wait_ge(s_silu, j + 1)
                pos(dve, s_th, j - 1)
                dve.tensor_tensor(hid[:, u, :], sg[:, u, :], pg[:, u, DE:2 * DE], ALU.mult).then_inc(s_hid, 1)

            def read_turned(j, u):
                dve.wait_ge(s_th, j + 1)
                pos(dve, s_dn, j - 1)
                dve.tensor_copy(hidT[:, u, :], ph[:, 0:DE]).then_inc(s_hidT, 1)

            def out(j, u):
                dve.wait_ge(s_dn, j + 1)
                if not (isinstance(j, int) and j < 2):
                    dve.wait_ge(s_yst[u], j * 8 - 8 * u)
                for i in range(2):
                    c = slice(512 * i, 512 * i + 512)
                    dve.tensor_tensor(y[:, u, c], py[:, c], gate5[:, c], ALU.mult).then_inc(s_y, 1)

            hidden(0, 0)
            for j in range(2):
                read_turned(j, j)
                out(j, j)
                hidden(j + 1, 1 - j)
            with steps(dve, 2, J - 2, 2) as j0:
                for u in range(2):
                    read_turned(j0 + u, u)
                    out(j0 + u, u)
                    hidden(j0 + u + 1, 1 - u)
            read_turned(J - 2, 0)
            out(J - 2, 0)
            hidden(J - 1, 1)
            read_turned(J - 1, 1)
            out(J - 1, 1)

        @block.tensor
        def _(pe):
            def turn(j, u):
                pe.wait_ge(s_x[u], (j // 2 + 1) * 16 if isinstance(j, int) else j * 8 + 16 - 8 * u)
                pos(pe, s_hT, j)
                for c in range(DC):
                    ins = pe.transpose(turned[:, c // 4, (c % 4) * P:(c % 4 + 1) * P], xg[:, u, c * P:(c + 1) * P], ident[:, :])
                ins.then_inc(s_turn, 1)

            def gate_up(j, u, between):
                par = tile_value(pe, 1, j, 1)
                pe.wait_ge(s_wg[u], (j - u) * 16 + 32)
                pe.wait_ge(s_hT, j + 1)
                pos(pe, s_hid, j - 1)
                for c in range(DC):
                    if c == DC // 2:
                        between()
                    ins = pe.matmul(pg[:, u, :], hT[:, u, c, :], wgu[:, ds(par, 1), c, :].rearrange("p a f -> p (a f)"),
                                    start=(c == 0), stop=(c == DC - 1))
                ins.then_inc(s_gu, 1)

            def turn_hid(j, u):
                pe.wait_ge(s_hid, j + 1)
                pos(pe, s_hidT, j)
                for c in range(FC):
                    ins = pe.transpose(ph[:, c * P:(c + 1) * P], hid[:, u, c * P:(c + 1) * P], ident[:, :])
                ins.then_inc(s_th, 1)

            def down(j, u):
                par = tile_value(pe, 1, j, 1)
                pe.wait_ge(s_wd[u], (j - u) * 8 + 16)
                pe.wait_ge(s_hidT, j + 1)
                pos(pe, s_y, j * 2)
                for i in range(2):
                    for c in range(FC):
                        ins = pe.matmul(py[:, 512 * i:512 * i + 512], hidT[:, u, c * P:(c + 1) * P],
                                        wd[:, ds(par, 1), c, 512 * i:512 * i + 512].rearrange("p a f -> p (a f)"),
                                        start=(c == 0), stop=(c == FC - 1))
                ins.then_inc(s_dn, 1)

            turn(0, 0)
            turn(1, 1)
            gate_up(0, 0, lambda: None)
            turn(2, 0)
            gate_up(1, 1, lambda: turn_hid(0, 0))
            down(0, 0)
            turn(3, 1)
            with steps(pe, 2, J - 2, 2) as j0:
                for u in range(2):
                    j = j0 + u
                    gate_up(j, u, lambda: turn_hid(j - 1, 1 - u))
                    down(j - 1, 1 - u)
                    turn(j + 2, u)
            for j in range(J - 2, J):
                gate_up(j, j % 2, lambda: turn_hid(j - 1, 1 - j % 2))
                down(j - 1, 1 - j % 2)
            turn_hid(J - 1, 1)
            down(J - 1, 1)


def combine(nc, sem, A, ln_g, ln_b, S, out):
    slots, gates = A["slots"], A["gates"]
    with ExitStack() as ctx:
        sb = lambda name, shape, dt=F32: ctx.enter_context(nc.sbuf_tensor(name, shape, dt))
        NB = 2
        ya, yb = sb("co_ya", [P, NB, D]), sb("co_yb", [P, NB, D])
        cell = sb("co_cell", [P, 2, NB, 1], U32)
        xt = sb("co_x1", [P, NB, D])
        r = sb("co_r", [P, NB, D])
        o = sb("co_o", [P, NB, D])
        g, b = sb("co_g", [P, D]), sb("co_b", [P, D])
        st, mv, rs = sb("co_st", [P, 12]), sb("co_mv", [P, 2]), sb("co_rs", [P, 2])
        half = sb("co_half", [P, 2])
        s_g, s_half, s_cell = sem("co_ln_in"), sem("co_half"), sem("co_cell")
        s_ya, s_yb, s_x = ([sem(f"co_{n}_in{i}") for i in range(NB)] for n in ("ya", "yb", "x1"))
        s_a, s_b, s_r, s_st, s_mom, s_ve, s_rs = (sem(f"co_{n}") for n in ("a", "b", "residual", "stats", "moments", "var_eps", "rstd"))
        s_z, s_zg, s_o = sem("co_z"), sem("co_zg"), sem("co_o")
        s_os = [sem(f"co_out{i}") for i in range(NB)]
        block = ctx.enter_context(nc.Block())

        @block.sync
        def _(sp):
            sp.dma_start(g[:, :], ln_g.partition_broadcast(P)).then_inc(s_g, 16)
            sp.dma_start(b[:, :], ln_b.partition_broadcast(P)).then_inc(s_g, 16)
            for t in range(NB):
                sp.dma_start(xt[:, t, :], S["x1"][t * P:(t + 1) * P, :]).then_inc(s_x[t], 16)
            with steps(sp, NB, TILES, NB) as t0:
                for u in range(NB):
                    sp.wait_ge(s_r, t0 + u - 1)
                    sp.dma_start(xt[:, u, :], S["x1"][ds((t0 + u) * P, P), :]).then_inc(s_x[u], 16)

        @block.gpsimd
        def _(pool):
            pool.memset(half[:, 0:1], -0.5).then_inc(s_half, 1)
            pool.memset(half[:, 1:2], EPS).then_inc(s_half, 1)
            pool.wait_ge(s_half, 2)

            def gather(t, u):
                for k, (dst, s) in enumerate(((ya, s_ya), (yb, s_yb))):
                    pool.tensor_copy(cell[:, k, u, :], slots[:, k, t:t + 1] if isinstance(t, int) else slots[:, k, ds(t, 1)]).then_inc(s_cell, 1)
                    pool.wait_ge(s_cell, t * 2 + k + 1)
                    pool.nop(nofuse=True)
                    pool.indirect_dma_start(out=dst[:, u, :], out_offset=None, in_=S["ye"],
                                            in_offset=bass.IndirectOffsetOnAxis(ap=cell[:, k, u, :], axis=0)).then_inc(s[u], 16)

            def rstd(t):
                pool.wait_ge(s_mom, t + 1)
                pool.tensor_tensor(rs[:, 0:1], mv[:, 1:2], half[:, 1:2], ALU.add).then_inc(s_ve, 1)
                pool.wait_ge(s_ve, t + 1)
                pool.tensor_tensor(rs[:, 1:2], rs[:, 0:1], half[:, 0:1], ALU.pow).then_inc(s_rs, 1)

            gather(0, 0)
            gather(1, 1)
            with steps(pool, 0, TILES - NB, NB) as t0:
                for u in range(NB):
                    rstd(t0 + u)
                    pool.wait_ge(s_b, t0 + u + 1)
                    gather(t0 + u + NB, u)
            for t in range(TILES - NB, TILES):
                rstd(t)

        @block.scalar
        def _(act):
            def first(t, u):
                act.wait_ge(s_ya[u], t * 8 + 16 - 8 * u)
                pos(act, s_z, t - 1)
                gcol = gates[:, 0, t:t + 1] if isinstance(t, int) else gates[:, 0, ds(t, 1)]
                act.activation(r[:, u, :], ya[:, u, :], ACT.Copy, scale=gcol).then_inc(s_a, 1)

            def store(t, u):
                rows = ds(t * P, P) if not isinstance(t, int) else slice(t * P, (t + 1) * P)
                act.wait_ge(s_o, t + 1)
                act.dma_start(out[rows, :], o[:, u, :]).then_inc(s_os[u], 16)

            first(0, 0)
            first(1, 1)
            store(0, 0)
            with steps(act, NB, TILES, NB) as t0:
                for u in range(NB):
                    first(t0 + u, u)
                    store(t0 + u - 1, 1 - u)
            store(TILES - 1, 1)
            for u in range(NB):
                act.wait_ge(s_os[u], 8 * TILES)

        @block.vector
        def _(dve):
            dve.wait_ge(s_g, 32)

            def tile(t, u, first):
                dve.wait_ge(s_yb[u], t * 8 + 16 - 8 * u)
                dve.wait_ge(s_a, t + 1)
                gcol = gates[:, 1, t:t + 1] if isinstance(t, int) else gates[:, 1, ds(t, 1)]
                dve.scalar_tensor_tensor(out=r[:, u, :], in0=yb[:, u, :], scalar=gcol, in1=r[:, u, :],
                                         op0=ALU.mult, op1=ALU.add).then_inc(s_b, 1)
                dve.wait_ge(s_b, t + 1)
                dve.wait_ge(s_x[u], t * 8 + 16 - 8 * u)
                dve.scalar_tensor_tensor(out=r[:, u, :], in0=xt[:, u, :], scalar=ALPHA, in1=r[:, u, :],
                                         op0=ALU.mult, op1=ALU.add).then_inc(s_r, 1)
                dve.wait_ge(s_r, t + 1)
                for i in range(2):
                    dve.bn_stats(st[:, 6 * i:6 * i + 6], r[:, u, 512 * i:512 * i + 512]).then_inc(s_st, 1)
                dve.wait_ge(s_st, t * 2 + 2)
                dve.nop(nofuse=True)
                dve.bn_aggr(mv[:, :], st[:, :]).then_inc(s_mom, 1)
                dve.wait_ge(s_rs, t + 1)
                dve.tensor_scalar(r[:, u, :], r[:, u, :], mv[:, 0:1], rs[:, 1:2], ALU.subtract, ALU.mult).then_inc(s_z, 1)
                if not first:
                    dve.wait_ge(s_os[u], t * 8 - 8 * u)
                dve.wait_ge(s_z, t + 1)
                dve.tensor_tensor(o[:, u, :], r[:, u, :], g[:, :], ALU.mult).then_inc(s_zg, 1)
                dve.wait_ge(s_zg, t + 1)
                dve.tensor_tensor(o[:, u, :], o[:, u, :], b[:, :], ALU.add).then_inc(s_o, 1)

            tile(0, 0, True)
            tile(1, 1, True)
            with steps(dve, NB, TILES, NB) as t0:
                for u in range(NB):
                    tile(t0 + u, u, False)


def constants():
    qc, kc = np.arange(WIN_C)[:, None], np.arange(SPAN)[None, :]
    mask = np.zeros((QB, WIN_C, SPAN), np.float32)
    for n in range(QB):
        q = n * WIN_C + qc
        k = min(max(n * WIN_C - WIN_C // 2, 0), GRID_W - SPAN) + kc
        first = np.clip(q - WIN_C // 2, 0, GRID_W - WIN_C)
        mask[n] = np.where((k >= first) & (k < first + WIN_C), 0.0, -BIG)
    a, b = np.arange(RAD), np.arange(P)
    nk = RAD // 2 + 1
    turn = 2 * np.pi * np.outer(a, np.arange(nk)) / RAD
    parts = np.concatenate([np.cos(turn), -np.sin(turn[:, 1:nk - 1])], 1)
    short = np.einsum("ac,jk->ajck", parts, np.eye(8)).reshape(P, P)
    th = 2 * np.pi * b[None, :, None] * (RAD * b[None, None, :] + np.arange(nk)[:, None, None]) / SEQ
    long = np.concatenate([np.cos(th), -np.sin(th), np.sin(th), np.cos(th)], 2)
    tc = 2 * np.pi * np.outer(np.arange(64), np.arange(64)) / 64
    norm = (SEQ * 64) ** -0.5
    chan = np.stack([np.kron(np.eye(2), np.cos(tc)), np.kron(np.eye(2), np.sin(tc))]) * norm
    return {"k_mask": mask, "k_ident": np.eye(P, dtype=np.float32), "k_short": short.astype(np.float32),
            "k_long": long.astype(np.float32), "k_chan": chan.astype(np.float32),
            "k_less4": np.tril(np.ones((4, 4), np.float32), -1), "k_less16": np.tril(np.ones((E, E), np.float32), -1),
            "k_iota": np.arange(SLOT_TILES, dtype=np.float32), "k_triu": np.triu(np.ones((P, P), np.float32), 1)}


INPUTS = ["x", "c", "ctx", "c_ctx", "w_mod", "b_mod", "w_in", "rpb", "w_four", "w_out", "ln1_g", "ln1_b", "ln2_g",
          "ln2_b", "w_router", "router_bias", "w_gate", "w_up", "w_down"]
SCRATCH = {"xbias": [QB, WIN_C, HEADS, 15, SPAN], "qT": [NAW, SEQ], "kT": [NAW, SEQ], "kcT": [NAW, CTX],
           "vc": [CTX, NAW], "vf": [SEQ, NAW + FW],
           "hpart": [RAD, P, FW], "mixT": [NAW + FW, SEQ], "x1": [SEQ, D], "z2": [SEQ, D],
           "tokens": [SLOTS, 1], "ye": [SLOTS, D]}


def build(nc, T, S, out):
    with ExitStack() as top:
        first_half = []

        def sem(name):
            first_half.append(nc.alloc_semaphore(name=name))
            return first_half[-1]

        keep = lambda name, shape, dt=F32: top.enter_context(nc.sbuf_tensor(name, shape, dt))
        A = {"modc": keep("modc", [P, 2, MODS * DC]), "gate2": keep("gate2", [P, D]), "gate5": keep("gate5", [P, D]),
             "ident": keep("ident", [P, P]), "score": keep("score", [P, TILES, E]),
             "slots": keep("slots", [P, 2, TILES], U32), "gates": keep("gates", [P, 2, TILES]),
             "table": keep("table", [P, 3, SLOT_TILES], U32)}
        modulation(nc, sem, A, T["c"], T["c_ctx"], T["w_mod"], T["b_mod"], T["rpb"], T["k_mask"], T["k_ident"], S["xbias"])
        projection(nc, sem, A, T["x"], T["ctx"], T["w_in"], S)
        fourier(nc, sem, A, T["w_four"], T, S)
        attention(nc, sem, A, S)
        nc.clear_and_free_semaphores(first_half)
        nc.all_engine_barrier()
        sem = lambda name: top.enter_context(nc.semaphore(name))
        mixing(nc, sem, A, T["x"], T["w_out"], T["ln1_g"], T["ln1_b"], T["w_router"], S)
        routing(nc, sem, A, T["router_bias"], T, S)
        experts(nc, sem, A, T["w_gate"], T["w_up"], T["w_down"], S)
        combine(nc, sem, A, T["ln2_g"], T["ln2_b"], S, out)


def kernel(**inputs):
    import numpy as _np
    import concourse.bacc as _bacc
    from concourse import mybir as _mybir
    from concourse.bass_utils import run_bass_kernel_spmd as _run

    nc = _bacc.Bacc("TRN2", target_bir_lowering=False, num_devices=1)
    arrays = {name: _np.ascontiguousarray(inputs[name]) for name in INPUTS}
    arrays.update(constants())
    T = {}
    for name, a in arrays.items():
        t = nc.dram_tensor(f"in_{name}", a.shape, _mybir.dt.float32, kind="ExternalInput").ap()
        lead = name not in ("c_ctx", "w_router", "router_bias") and not name.startswith("k_")
        T[name] = t[0] if lead else t
    S = {name: nc.dram_tensor(f"s_{name}", shape, U32 if name == "tokens" else F32, kind="Internal").ap() for name, shape in SCRATCH.items()}
    out = nc.dram_tensor("out", (1, SEQ, D), _mybir.dt.float32, kind="ExternalOutput").ap()
    build(nc, T, S, out[0])
    r = _run(nc, [{f"in_{k}": v for k, v in arrays.items()}], core_ids=[0])
    return r.results[0]["out"]
```

```python
from contextlib import ExitStack, contextmanager

import numpy as np

import concourse.bass as bass
from concourse import mybir
from concourse.alu_op_type import AluOpType as ALU

F32 = mybir.dt.float32
F32R = mybir.dt.float32r
I32 = mybir.dt.int32
U32 = mybir.dt.uint32
ACT = mybir.ActivationFunctionType
AX = mybir.AxisListType
ds = bass.ds

P = 128
D = 1024
DC = D // P
SEQ, CTX = 2048, 256
TILES = SEQ // P
GRID_W, ROWS = 64, SEQ // 64
HEADS, HD = 8, 64
PAIRS = HEADS // 2
NAW = HEADS * HD
WIN_R, WIN_C = 8, 16
SPAN = 2 * WIN_C
FW = 512
IN_W = 3 * NAW + FW
E, EG, NG = 16, 4, 4
DE = 256
SLOT_TILES = 48
SLOTS = SLOT_TILES * P
ALPHA = 2.0 ** 0.25
EPS = 1e-6
BIG = 1.0e30
QB = 4
RAD = 16
MODS = 6


def pos(eng, sem, value):
    if not isinstance(value, int) or value > 0:
        eng.wait_ge(sem, value)


@contextmanager
def steps(eng, start, stop, step=1):
    with eng.Fori(0, (stop - start) // step) as i:
        yield i * step + start


def modulation(nc, sem, A, M, c, c_ctx, w_mod, b_mod, rpb, colmask, ident_d, xbias_d, w_in, ctx_in):
    modc, ident, sc, bcol = A["modc"], A["ident"], M["sc"], M["bcol"]
    NCH = MODS * DC
    PW = 512
    NP = 2 * D // PW
    HR = HEADS * 15
    with ExitStack() as ctx:
        sb = lambda name, shape, dt=F32: ctx.enter_context(nc.sbuf_tensor(name, shape, dt))
        ps = lambda name, shape, dt=F32: ctx.enter_context(nc.psum_tensor(name, shape, dt))
        cv = sb("mo_cv", [P, 2, DC])
        sig = sb("mo_sig", [P, 2, DC])
        w = sb("mo_w", [P, NP, DC, PW])
        brow = sb("mo_brow", [NCH, P])
        pad = sb("mo_pad", [HR, 64])
        msk = sb("mo_msk", [HR, QB, WIN_C, SPAN])
        xb = sb("mo_xb", [HR, QB, WIN_C, SPAN])
        pcol = ps("mo_pcol", [P, 512])
        pT = ps("mo_pT", [P, 512])
        s_in, s_rpb, s_id = sem("mo_in"), sem("mo_rpb_in"), sem("mo_ident_in")
        s_w = [sem(f"mo_piece_in{i}") for i in range(NP)]
        s_sig, s_silu = sem("mo_sigmoid"), sem("mo_silu")
        s_done, s_bT, s_bcol = sem("mo_pieces_done"), sem("mo_b_turned"), sem("mo_b_col")
        s_col, s_pad, s_xb, s_st = sem("mo_cols"), sem("mo_pad_set"), sem("mo_xbias"), sem("mo_xbias_out")
        w_v = w_mod.rearrange("(p j) n -> p j n", j=DC)
        block = ctx.enter_context(nc.Block())

        @block.sync
        def _(sp):
            sp.dma_start(cv[:, 0, :], c.rearrange("(p j) -> p j", j=DC)).then_inc(s_in, 16)
            sp.dma_start(cv[:, 1, :], c_ctx.rearrange("(p j) -> p j", j=DC)).then_inc(s_in, 16)
            sp.dma_start(ident[:, :], ident_d).then_inc(s_id, 16)
            sp.dma_start(brow[:, :], b_mod.rearrange("(n p) -> n p", p=P)).then_inc(s_id, 16)
            for p in range(NP):
                sp.dma_start(w[:, p, :, :], w_v[:, :, p * PW:(p + 1) * PW]).then_inc(s_w[p], 16)
                if p == 0:
                    sp.wait_ge(s_pad, 1)
                    sp.dma_start(pad[:, 16:47], rpb.rearrange("h r c -> (h r) c")).then_inc(s_rpb, 16)
                    sp.dma_start(msk[:, :, :, :], colmask.partition_broadcast(HR)).then_inc(s_rpb, 16)
            for t in range(2):
                sp.dma_start(M["x"][:, t, :], ctx_in[t * P:(t + 1) * P, :]).then_inc(M["s_x"][t], 16)
            for j in range(2):
                sp.dma_start(M["wst"][j], w_in[j * P:(j + 1) * P, :]).then_inc(M["s_w"][j], 16)
            sp.wait_ge(s_xb, QB)
            for n in range(QB):
                sp.dma_start(xbias_d[n].rearrange("q h r k -> (h r) q k"), xb[:, n, :, :]).then_inc(s_st, 16)
            sp.wait_ge(s_st, 16 * QB)

        @block.gpsimd
        def _(pool):
            pool.memset(pad[:, :], 0.0).then_inc(s_pad, 1)

        @block.scalar
        def _(act):
            act.wait_ge(s_in, 32)
            act.activation(sig[:, :, :], cv[:, :, :], ACT.Sigmoid).then_inc(s_sig, 1)

        @block.vector
        def _(dve):
            dve.wait_ge(s_sig, 1)
            dve.tensor_tensor(sc[:, :, :], cv[:, :, :], sig[:, :, :], ALU.mult).then_inc(s_silu, 1)
            dve.wait_ge(s_rpb, 32)
            for n, shift in enumerate((0, -8, -8, -16)):
                base = pad[:, 31 + shift:32 + shift]
                skew = bass.AP(base.tensor, base.offset, [list(base.ap[0]), [-1, WIN_C], [1, SPAN]])
                dve.tensor_tensor(xb[:, n, :, :], skew, msk[:, n, :, :], ALU.add).then_inc(s_xb, 1)
            dve.wait_ge(s_bT, 1)
            dve.tensor_copy(bcol[:, :], pT[:, 0:NCH]).then_inc(s_bcol, 1)
            dve.wait_ge(s_bcol, 1)
            dve.wait_ge(s_done, NP)
            n = slice(0, 2 * DC)
            for v in range(2):
                dve.tensor_tensor(modc[:, v, n], pcol[:, 0:4 * DC].rearrange("p (n v) -> p v n", v=2)[:, v, :],
                                  bcol[:, n], ALU.add).then_inc(s_col, 1)
            dve.wait_ge(s_col, 2)
            dve.tensor_scalar(modc[:, :, DC:2 * DC], modc[:, :, DC:2 * DC], 1.0, None, ALU.add).then_inc(s_col, 1)
            dve.wait_ge(s_col, 3)

        @block.tensor
        def _(pe):
            pe.wait_ge(s_id, 32)
            pe.transpose(pT[:, 0:NCH], brow[:, :], ident[0:NCH, 0:NCH]).then_inc(s_bT, 1)
            pe.wait_ge(s_silu, 1)
            for p in range(NP):
                pe.wait_ge(s_w[p], 16)
                for n in range(PW // P):
                    col = 2 * (p * (PW // P) + n)
                    for j in range(DC):
                        mm = pe.matmul(pcol[:, col:col + 2], w[:, p, j, n * P:(n + 1) * P], sc[:, :, j],
                                       start=(j == 0), stop=(j == DC - 1))
                mm.then_inc(s_done, 1)


def projection(nc, sem, A, M, x, w_in, w_mod, S):
    modc, ident = A["modc"], A["ident"]
    PW = 512
    GW = 2 * P
    NGRP = SEQ // GW
    NO = 6
    OUTS_CTX, OUTS = 6, 12
    with ExitStack() as ctx:
        sb = lambda name, shape, dt=F32: ctx.enter_context(nc.sbuf_tensor(name, shape, dt))
        ps = lambda name, shape, dt=F32: ctx.enter_context(nc.psum_tensor(name, shape, dt))
        whi = sb("pr_whi", [P, DC, IN_W], F32R)
        wlo = sb("pr_wlo", [P, DC, IN_W], F32R)
        hhi = sb("pr_hhi", [P, 2, DC, GW], F32R)
        hlo = sb("pr_hlo", [P, 2, DC, GW], F32R)
        h = sb("pr_h", [P, DC, P])
        xt, stage = M["x"], M["stage"]
        wm = sb("pr_w_mod", [P, 4, PW])
        acc = sb("pr_acc", [P, PW])
        ones = sb("pr_ones", [P, 1])
        st = sb("pr_st", [P, 2, 12])
        mv = sb("pr_mv", [P, 2, 2])
        ve = sb("pr_ve", [P, 2])
        rs = sb("pr_rs", [P, 2])
        half = sb("pr_half", [P, 2])
        turned = ps("pr_turned", [P, 2, 512])
        out = ps("pr_out", [P, NO, 512])
        s_x, s_w, wst = M["s_x"], M["s_w"], M["wst"]
        s_wm = [sem(f"pr_w_mod_in{i}") for i in range(4)]
        s_ones, s_mac, s_pc, s_mc = sem("pr_ones"), sem("pr_mac"), sem("pr_piece"), sem("pr_piece_added")
        s_whi, s_wlo = sem("pr_w_hi"), sem("pr_w_lo")
        s_stats, s_mom, s_ve, s_rstd, s_z = sem("pr_stats"), sem("pr_moments"), sem("pr_var_eps"), sem("pr_rstd"), sem("pr_z")
        s_turn, s_mod, s_hi, s_lo = sem("pr_turned"), sem("pr_modulated"), sem("pr_h_hi"), sem("pr_h_lo")
        s_out, s_ev, s_half = sem("pr_out_ready"), sem("pr_out_read"), sem("pr_half")
        s_st = [sem(f"pr_stage_out{i}") for i in range(4)]
        mod_v = w_mod.rearrange("(p j) n -> p j n", j=DC)
        block = ctx.enter_context(nc.Block())

        @block.sync
        def _(sp):
            def load_x(t, u):
                sp.wait_ge(s_turn, t - 1)
                sp.dma_start(xt[:, u, :], x[ds((t - 2) * P, P), :]).then_inc(s_x[u], 16)

            def load_mod(g, u):
                cols = slice(2 * D, 2 * D + PW) if isinstance(g, int) and g == 0 else ds(g * PW + 2 * D, PW)
                for i in range(4):
                    pos(sp, s_mac, g * 8 + 4 * u + i - 3)
                    sp.dma_start(wm[:, i, :], mod_v[:, 4 * u + i, cols]).then_inc(s_wm[i], 16)

            for j in range(2, DC):
                sp.wait_ge(s_wlo, j - 1)
                sp.dma_start(wst[j % 2], w_in[j * P:(j + 1) * P, :]).then_inc(s_w[j % 2], 16)
            load_x(2, 0)
            load_x(3, 1)
            load_mod(0, 0)
            with steps(sp, 1, NGRP) as g:
                load_x(g * 2 + 2, 0)
                load_mod(g - 1, 1)
                load_x(g * 2 + 3, 1)
                load_mod(g, 0)
            load_mod(NGRP - 1, 1)

        @block.gpsimd
        def _(pool):
            pool.memset(half[:, 0:1], -0.5).then_inc(s_half, 1)
            pool.memset(half[:, 1:2], EPS).then_inc(s_half, 1)
            pool.memset(ones[:, :], 1.0).then_inc(s_ones, 1)
            pool.wait_ge(s_half, 2)

            def tile(t, u, par):
                pool.wait_ge(s_mom, t + 1)
                pool.tensor_tensor(ve[:, u:u + 1], mv[:, u, 1:2], half[:, 1:2], ALU.add).then_inc(s_ve, 1)
                pool.wait_ge(s_ve, t + 1)
                pool.tensor_tensor(rs[:, u:u + 1], ve[:, u:u + 1], half[:, 0:1], ALU.pow).then_inc(s_rstd, 1)
                pool.wait_ge(s_hi, t + 1)
                hs = slice(u * P, (u + 1) * P)
                pool.tensor_tensor(hlo[:, par, :, hs], h[:, :, :], hhi[:, par, :, hs].bitcast(F32), ALU.subtract).then_inc(s_lo, 1)

            tile(0, 0, 0)
            tile(1, 1, 0)
            with steps(pool, 2, 2 + TILES, 4) as t0:
                for k in range(4):
                    tile(t0 + k, k % 2, (1 + k // 2) % 2)

        @block.vector
        def _(dve):
            def add_piece(g):
                cols = ds(g * 4 + 2 * DC, 4) if not isinstance(g, int) else slice(2 * DC + 4 * g, 2 * DC + 4 * g + 4)
                dve.wait_ge(s_pc, g + 1)
                dve.nop(nofuse=True)
                dve.tensor_tensor(modc[:, 0, cols], turned[:, 0, 0:4], M["bcol"][:, cols], ALU.add).then_inc(s_mc, 1)

            def mac(g, u):
                for i in range(4):
                    n, j = g * 8 + 4 * u + i, 4 * u + i
                    dve.wait_ge(s_wm[i], (g * 2 + u + 1) * 16)
                    pos(dve, s_mac, n)
                    if j == 0:
                        pos(dve, s_pc, g)
                        dve.tensor_scalar(acc[:, :], wm[:, i, :], M["sc"][:, 0, 0:1], None, ALU.mult).then_inc(s_mac, 1)
                    else:
                        dve.scalar_tensor_tensor(out=acc[:, :], in0=wm[:, i, :], scalar=M["sc"][:, 0, j:j + 1], in1=acc[:, :],
                                                 op0=ALU.mult, op1=ALU.add).then_inc(s_mac, 1)

            def tile(t, u, v, piece=None):
                dve.wait_ge(s_x[u], (t - u) * 8 + 16)
                for i in range(2):
                    dve.bn_stats(st[:, u, 6 * i:6 * i + 6], xt[:, u, 512 * i:512 * i + 512]).then_inc(s_stats, 1)
                dve.wait_ge(s_stats, 2 * t + 2)
                dve.nop(nofuse=True)
                dve.bn_aggr(mv[:, u, :], st[:, u, :]).then_inc(s_mom, 1)
                dve.wait_ge(s_rstd, t + 1)
                dve.tensor_scalar(xt[:, u, :], xt[:, u, :], mv[:, u, 0:1], rs[:, u:u + 1], ALU.subtract, ALU.mult).then_inc(s_z, 1)
                if piece is not None:
                    add_piece(piece)
                dve.wait_ge(s_turn, t + 1)
                pos(dve, s_lo, t)
                for j in range(DC):
                    ins = dve.tensor_scalar(h[:, j, :], turned[:, j // 4, (j % 4) * P:(j % 4 + 1) * P],
                                            modc[:, v, DC + j:DC + j + 1], modc[:, v, j:j + 1], ALU.mult, ALU.add)
                ins.then_inc(s_mod, 1)

            for j in range(DC):
                dve.wait_ge(s_whi, j + 1)
                dve.tensor_tensor(wlo[:, j, :], wst[j % 2], whi[:, j, :].bitcast(F32), ALU.subtract).then_inc(s_wlo, 1)
                if 1 <= j <= 2:
                    tile(j - 1, j - 1, 1)
            tile(2, 0, 0)
            mac(0, 0)
            tile(3, 1, 0)
            mac(0, 1)
            with steps(dve, 1, NGRP) as g:
                tile(g * 2 + 2, 0, 0, g - 1)
                mac(g, 0)
                tile(g * 2 + 3, 1, 0)
                mac(g, 1)
            add_piece(NGRP - 1)
            dve.wait_ge(s_mc, NGRP)
            dve.tensor_scalar(modc[:, 0, 4 * DC:5 * DC], modc[:, 0, 4 * DC:5 * DC], 1.0, None, ALU.add).then_inc(s_mc, 1)
            dve.wait_ge(s_mc, NGRP + 1)

        def base(s):
            return 0 if isinstance(s, int) and s == 0 else s * OUTS - (OUTS - OUTS_CTX)

        @block.scalar
        def _(act):
            def hi(t, u, par):
                act.wait_ge(s_mod, t + 1)
                act.activation(hhi[:, par, :, u * P:(u + 1) * P], h[:, :, :], ACT.Copy).then_inc(s_hi, 1)

            def evac(n, slot, width, dst, scale=1.0):
                act.wait_ge(s_out, n + 1)
                act.activation(dst, out[:, slot, 0:width], ACT.Copy, scale=scale).then_inc(s_ev, 1)

            def group(s, par, is_ctx, last):
                n, k = base(s), 0
                per = 2 if is_ctx else 4
                cols = slice(0, GW) if is_ctx else ds((s - 1) * GW, GW)
                for which in range(2):
                    pos(act, s_st[which], 16 * s)
                    for o in range(per):
                        evac(n + k, k % NO, GW, stage[:, which, o * GW:(o + 1) * GW],
                             HD ** -0.5 if which == 0 and not is_ctx else 1.0)
                        k += 1
                    act.wait_ge(s_ev, n + k)
                    dst = S["kcT"][which * 2 * P:(which + 1) * 2 * P, :] if is_ctx else S["qT"] if which == 0 else S["kT"]
                    act.dma_start(dst.rearrange("(c p) t -> p c t", p=P)[:, :, cols],
                                  stage[:, which, 0:per * GW].rearrange("p (c t) -> p c t", c=per)).then_inc(s_st[which], 16)
                    if not last:
                        hi(2 * s + 2 + which, which, 1 - par)
                for u in range(2):
                    pos(act, s_st[2 + u], 16 * s)
                    for f in range(1 if is_ctx else 2):
                        evac(n + k, k % NO, 512, stage[:, 2 + u, 512 * f:512 * f + 512])
                        k += 1
                    act.wait_ge(s_ev, n + k)
                    dst, width = (S["vc"][u * P:(u + 1) * P, :], 512) if is_ctx else (S["vf"][ds((s - 1) * GW + u * P, P), :], 1024)
                    act.dma_start(dst, stage[:, 2 + u, 0:width]).then_inc(s_st[2 + u], 16)

            for j in range(DC):
                act.wait_ge(s_w[j % 2], 16 * (j // 2 + 1))
                act.activation(whi[:, j, :], wst[j % 2], ACT.Copy).then_inc(s_whi, 1)
                if 2 <= j <= 3:
                    hi(j - 2, j - 2, 0)
            group(0, 0, True, False)
            with steps(act, 1, NGRP - 1, 2) as s0:
                group(s0, 1, False, False)
                group(s0 + 1, 0, False, False)
            group(NGRP - 1, 1, False, False)
            group(NGRP, 0, False, True)
            for i in range(4):
                act.wait_ge(s_st[i], 16 * (NGRP + 1))

        @block.tensor
        def _(pe):
            def turn(t, u):
                pe.wait_ge(s_z, t + 1)
                pos(pe, s_mod, t)
                for j in range(DC):
                    ins = pe.transpose(turned[:, j // 4, (j % 4) * P:(j % 4 + 1) * P], xt[:, u, j * P:(j + 1) * P], ident[:, :])
                ins.then_inc(s_turn, 1)

            def begin(n):
                pos(pe, s_ev, n - NO + 1)

            def by_channel(n, slot, par, col):
                begin(n)
                o = out[:, slot, 0:GW]
                for j in range(DC):
                    a, b = whi[:, j, col:col + P], wlo[:, j, col:col + P]
                    pe.matmul(o, a, hhi[:, par, j, :], start=(j == 0), stop=False)
                    pe.matmul(o, a, hlo[:, par, j, :], start=False, stop=False)
                    ins = pe.matmul(o, b, hhi[:, par, j, :], start=False, stop=(j == DC - 1))
                ins.then_inc(s_out, 1)

            def by_token(n, slot, par, u, col):
                begin(n)
                o = out[:, slot, :]
                for j in range(DC):
                    a, b = hhi[:, par, j, u * P:(u + 1) * P], hlo[:, par, j, u * P:(u + 1) * P]
                    pe.matmul(o, a, whi[:, j, col:col + 512], start=(j == 0), stop=False)
                    pe.matmul(o, a, wlo[:, j, col:col + 512], start=False, stop=False)
                    ins = pe.matmul(o, b, whi[:, j, col:col + 512], start=False, stop=(j == DC - 1))
                ins.then_inc(s_out, 1)

            def turn_next(s, which):
                if which == 0:
                    pos(pe, s_mc, s)
                turn(s * 2 + 2 + which, which)

            def piece(g):
                pe.wait_ge(s_mac, g * 8 + 8)
                for n in range(PW // P):
                    ins = pe.matmul(turned[:, 0, n:n + 1], acc[:, n * P:(n + 1) * P], ones[:, :], start=True, stop=True)
                ins.then_inc(s_pc, 1)

            def context():
                pe.wait_ge(s_lo, 2)
                for j in range(DC):
                    pe.wait_ge(s_wlo, j + 1)
                    for k in range(4):
                        o, col = out[:, k, 0:GW], NAW + k * P
                        a, b = whi[:, j, col:col + P], wlo[:, j, col:col + P]
                        pe.matmul(o, a, hhi[:, 0, j, :], start=(j == 0), stop=False)
                        pe.matmul(o, a, hlo[:, 0, j, :], start=False, stop=False)
                        ins = pe.matmul(o, b, hhi[:, 0, j, :], start=False, stop=(j == DC - 1))
                        if j == DC - 1:
                            ins.then_inc(s_out, 1)
                    for u in range(2):
                        o, col = out[:, 4 + u, :], 2 * NAW
                        a, b = hhi[:, 0, j, u * P:(u + 1) * P], hlo[:, 0, j, u * P:(u + 1) * P]
                        pe.matmul(o, a, whi[:, j, col:col + NAW], start=(j == 0), stop=False)
                        pe.matmul(o, a, wlo[:, j, col:col + NAW], start=False, stop=False)
                        ins = pe.matmul(o, b, whi[:, j, col:col + NAW], start=False, stop=(j == DC - 1))
                        if j == DC - 1:
                            ins.then_inc(s_out, 1)
                for which in range(2):
                    turn_next(0, which)
                piece(0)

            def group(s, par, last):
                n, k = base(s), 0
                pe.wait_ge(s_lo, s * 2 + 2)
                for which in range(2):
                    for o in range(4):
                        by_channel(n + k, k % NO, par, k * P)
                        k += 1
                    if not last:
                        turn_next(s, which)
                for u in range(2):
                    for f in range(2):
                        by_token(n + k, k % NO, par, u, 2 * NAW + 512 * f)
                        k += 1
                if not last:
                    piece(s)

            turn(0, 0)
            turn(1, 1)
            context()
            with steps(pe, 1, NGRP - 1, 2) as s0:
                group(s0, 1, False)
                group(s0 + 1, 0, False)
            group(NGRP - 1, 1, False)
            group(NGRP, 0, True)


def fourier(nc, sem, A, w_four, K, S, L, room):
    NK = RAD // 2 + 1
    Q = FW // P
    part = {("cos", k): k for k in range(NK)} | {("sin", k): NK - 1 + k for k in range(1, NK - 1)}
    with ExitStack() as ctx:
        sb = lambda name, shape, dt=F32: ctx.enter_context(nc.sbuf_tensor(name, shape, dt))
        ps = lambda name, shape, dt=F32: ctx.enter_context(nc.psum_tensor(name, shape, dt))
        short = sb("fo_short", [P, P])
        long = sb("fo_long", [P, NK, 4 * P])
        chan = sb("fo_chan", [P, 2, P])
        w4 = sb("fo_w4", [P, Q, P])
        mix = sb("fo_mix", [P, 3, Q, P])
        f = room[:, :, :].rearrange("p a (b c) -> p (a b) c", c=FW)
        hs = sb("fo_hs", [P, RAD, FW])
        hb = f
        us = sb("fo_us", [P, 2, Q, 2 * P])
        yT = hs[:, :, :].rearrange("p (q t) c -> p q (t c)", q=Q)
        pu = ps("fo_pu", [P, Q, 512])
        py = ps("fo_py", [P, Q, 512])
        s_k, s_w4z, s_w4, s_lk = sem("fo_consts_in"), sem("fo_w4_zeroed"), sem("fo_w4_in"), sem("fo_long_in")
        s_f = [sem(f"fo_f_in{i}") for i in range(4)]
        s_hp, s_hs, s_hst = sem("fo_short_done"), sem("fo_short_read"), sem("fo_short_out")
        s_hd = sem("fo_short_read_dve")
        s_hb = [sem(f"fo_part_in{i}") for i in range(NK)]
        s_gp, s_gr = sem("fo_gate_done"), sem("fo_gate_read")
        s_mp, s_mix = sem("fo_mix_done"), sem("fo_mix_read")
        s_u, s_us, s_y, s_yr, s_yst = sem("fo_u_done"), sem("fo_u_read"), sem("fo_y_done"), sem("fo_y_read"), sem("fo_y_out")
        f_v = S["vf"][:, NAW:].rearrange("(a t j) c -> t a j c", a=RAD, j=8)
        h_v = S["hpart"].rearrange("c (t j) k -> t c j k", j=8)
        block = ctx.enter_context(nc.Block())

        @block.sync
        def _(sp):
            sp.dma_start(short[:, :], K["k_short"]).then_inc(s_k, 16)
            sp.dma_start(chan[:, :, :], K["k_chan"].rearrange("v p c -> p v c")).then_inc(s_k, 16)
            for t in range(RAD):
                sp.dma_start(f[:, t, :], f_v[t]).then_inc(s_f[t // 4], 16)
            sp.wait_ge(s_w4z, 1)
            for g in range(2):
                sp.dma_start(w4[64 * g:64 * g + 64, :, 64 * g:64 * g + 64],
                             w_four.rearrange("(q g) c e -> g c q e", g=2)[g]).then_inc(s_w4, 16)
            sp.dma_start(long[:, :, :], K["k_long"].rearrange("k b n -> b k n")).then_inc(s_lk, 16)
            sp.wait_ge(s_hst, 16 * RAD)
            for k in range(NK):
                for kind in ("cos", "sin"):
                    if (kind, k) in part:
                        c = part[kind, k]
                        sp.dma_start(hb[:, c, :], S["hpart"][c]).then_inc(s_hb[k], 16)
            for name, s in (("kT", "s_k"), ("qT", "s_q"), ("kcT", "s_c"), ("vc", "s_c")):
                sp.dma_start(L[name][:, :, :], S[name].rearrange("(c p) t -> p c t", p=P)).then_inc(L[s], 16)
            for q in range(Q):
                sp.wait_ge(s_yr, Q * (NK - 1) + q + 1)
                sp.dma_start(S["mixT"][NAW + q * P:NAW + (q + 1) * P, :], yT[:, q, :]).then_inc(s_yst, 16)
            sp.wait_ge(s_yst, 16 * Q)

        @block.gpsimd
        def _(pool):
            pool.memset(w4[:, :, :], 0.0).then_inc(s_w4z, 1)

        @block.scalar
        def _(act):
            for t in range(RAD):
                act.wait_ge(s_hp, t + 1)
                act.activation(hs[:, t, :], pu[:, t % 4, :], ACT.Copy).then_inc(s_hs, 1)
                act.wait_ge(s_hs, t + 1)
                act.dma_start(h_v[t], hs[:, t, :]).then_inc(s_hst, 16)
            act.wait_ge(s_hst, 16 * RAD)
            for k in range(NK):
                for q in range(Q):
                    act.wait_ge(s_y, k * Q + q + 1)
                    last = act.activation(yT[:, q, k::RAD], py[:, q, 0:P], ACT.Copy)
                    if 0 < k < NK - 1:
                        last = act.activation(yT[:, q, SEQ - k::-RAD], py[:, q, P:2 * P], ACT.Copy)
                    last.then_inc(s_yr, 1)

        @block.vector
        def _(dve):
            for k, gate in enumerate((A["gate2"], A["gate5"])):
                dve.wait_ge(s_gp, k + 1)
                dve.tensor_copy(gate[:, :], py[:, 2 * k:2 * k + 2, :].rearrange("p a n -> p (a n)")).then_inc(s_gr, 1)
            for v in range(2):
                dve.wait_ge(s_mp, v + 1)
                dve.tensor_copy(mix[:, v, :, :], py[:, v, :].rearrange("p (q c) -> p q c", q=Q)).then_inc(s_mix, 1)
            dve.tensor_scalar(mix[:, 2, :, :], py[:, 1, :].rearrange("p (q c) -> p q c", q=Q), -1.0, None, ALU.mult).then_inc(s_mix, 1)
            for k in range(NK):
                for q in range(Q):
                    n = k * Q + q
                    dve.wait_ge(s_u, n + 1)
                    if k >= 2:
                        dve.wait_ge(s_y, (k - 2) * Q + q + 1)
                    dve.tensor_copy(us[:, k % 2, q, :], pu[:, q, 0:2 * P]).then_inc(s_us, 1)

        @block.tensor
        def _(pe):
            for k, first in enumerate((2 * DC, 5 * DC)):
                for j in range(DC):
                    m = A["modc"][:, 0, first + j:first + j + 1]
                    ins = pe.matmul(py[:, 2 * k + j // 4, (j % 4) * P:(j % 4 + 1) * P],
                                    bass.AP(m.tensor, m.offset, [list(m.ap[0]), [0, P]]), A["ident"][:, :], start=True, stop=True)
                ins.then_inc(s_gp, 1)
            pe.wait_ge(s_k, 32)
            for t in range(RAD):
                pe.wait_ge(s_f[t // 4], 64)
                if t >= 4:
                    pe.wait_ge(s_hs, t - 3)
                pe.matmul(pu[:, t % 4, :], short[:, :], f[:, t, :], start=True, stop=True).then_inc(s_hp, 1)
            pe.wait_ge(s_w4, 32)
            pe.wait_ge(s_gr, 2)
            for v in range(2):
                pe.matmul(py[:, v, :], chan[:, v, :], w4[:, :, :].rearrange("p q c -> p (q c)"), start=True, stop=True).then_inc(s_mp, 1)
            pe.wait_ge(s_lk, 16)
            pe.wait_ge(s_hs, RAD)
            pe.wait_ge(s_mix, 3)

            def u(k):
                both = ("sin", k) in part
                pe.wait_ge(s_hb[k], 32 if both else 16)
                for q in range(Q):
                    if k:
                        pe.wait_ge(s_us, (k - 1) * Q + q + 1)
                    cs = slice(q * P, (q + 1) * P)
                    ins = pe.matmul(pu[:, q, 0:2 * P], hb[:, part["cos", k], cs], long[:, k, 0:2 * P], start=True, stop=not both)
                    if both:
                        ins = pe.matmul(pu[:, q, 0:2 * P], hb[:, part["sin", k], cs], long[:, k, 2 * P:4 * P], start=False, stop=True)
                    ins.then_inc(s_u, 1)

            def y(k):
                for q in range(Q):
                    pe.wait_ge(s_us, k * Q + q + 1)
                    if k:
                        pe.wait_ge(s_yr, (k - 1) * Q + q + 1)
                    for sign in ((0, 1) if 0 < k < NK - 1 else (0,)):
                        o = py[:, q, sign * P:(sign + 1) * P]
                        pe.matmul(o, mix[:, 0, q, :], us[:, k % 2, q, 0:P], start=True, stop=False)
                        ins = pe.matmul(o, mix[:, 1 + sign, q, :], us[:, k % 2, q, P:2 * P], start=False, stop=True)
                    ins.then_inc(s_y, 1)

            u(0)
            for k in range(1, NK):
                u(k)
                y(k - 1)
            y(NK - 1)


def attention(nc, sem, A, S, L, w_out, wraw):
    ident = A["ident"]
    NBLK = QB * QB
    KR = 16
    LAT = KR * SPAN
    ALL = LAT + CTX
    with ExitStack() as ctx:
        sb = lambda name, shape, dt=F32: ctx.enter_context(nc.sbuf_tensor(name, shape, dt))
        ps = lambda name, shape, dt=F32: ctx.enter_context(nc.psum_tensor(name, shape, dt))
        qT, kT, kcT, vc = (L[name] for name in ("qT", "kT", "kcT", "vc"))
        v = sb("at_v", [P, 2, LAT // P, NAW])
        bias = sb("at_bias", [P, 2, HEADS, LAT])
        qs = sb("at_qs", [P, 2, HEADS, P])
        sn = sb("at_sn", [P, 2, LAT])
        nm = sb("at_nm", [P, 2, 3])
        pr = sb("at_pr", [P, 2, ALL])
        pT = sb("at_pT", [P, 2, ALL])
        sums = sb("at_sums", [P, 2, 2, HEADS])
        den = sb("at_den", [P, 2, HEADS])
        on = sb("at_on", [P, NAW])
        oT = qT
        sl = ps("at_sl", [P, 2, LAT])
        sx = ps("at_sx", [P, 2, 512])
        tl = ps("at_tl", [P, LAT])
        tx = ps("at_tx", [P, 512])
        po = ps("at_po", [P, 2, NAW])
        s_q, s_k, s_c = L["s_q"], L["s_k"], L["s_c"]
        s_wr, s_m2 = sem("at_w_out_in"), sem("at_w_out_gated")
        s_v = [sem(f"at_v_in{i}") for i in range(2)]
        s_b = [sem(f"at_bias_in{i}") for i in range(2)]
        s_clr, s_qs, s_qz = sem("at_bias_cleared"), sem("at_queries"), sem("at_queries_zeroed")
        s_s, s_red, s_m = sem("at_scores"), sem("at_reduced"), sem("at_max")
        s_e, s_t, s_evl, s_evx, s_pv = sem("at_exp"), sem("at_turned"), sem("at_turn_read_dve"), sem("at_turn_read_act"), sem("at_pv")
        s_den, s_on, s_ot, s_oe, s_st = sem("at_den"), sem("at_normed"), sem("at_o_turned"), sem("at_o_read"), sem("at_o_out")
        mix_v = S["mixT"][0:NAW, :].rearrange("(c p) t -> p c t", p=P)
        block = ctx.enter_context(nc.Block())

        def corner(t, u):
            R, m = t // 2, t % 2
            return (R + t // 4) * (4 * GRID_W) + (m * 3 + u) * 8, R * (8 * GRID_W) + (m * 2 + u) * WIN_C

        @block.sync
        def _(sp):
            def load(R, m, u):
                row0 = 4 * (R + R // 2)
                b = m * 2 + (4 * R + u)
                if isinstance(b, int) and b < 2:
                    pass
                else:
                    sp.wait_ge(s_pv, (b - 1) * HEADS)
                for kr in range(4):
                    first = m * 24 + (u * 8 + (row0 + kr) * GRID_W)
                    base = S["vf"][ds(first, 32), 0:NAW]
                    src = bass.AP(base.tensor, base.offset, [list(base.ap[0]), [4 * GRID_W * (NAW + FW), 4], [1, NAW]])
                    sp.dma_start(v[32 * kr:32 * kr + 32, u, :, :], src).then_inc(s_v[u], 16)
                sp.wait_ge(s_clr, b + 1)
                for qr in range(8):
                    rel = (max(qr - 4, 0), qr, qr, 4 + min(qr, 4))[R]
                    dr = row0 + rel - (8 * R + qr) + 7
                    src = S["xbias"][ds(m * 2 + u, 1), :, :, dr:dr + 8, :].rearrange("n q h r k -> (n q) h (r k)")
                    sp.dma_start(bias[16 * qr:16 * qr + 16, u, :, rel * SPAN:(rel + 8) * SPAN], src).then_inc(s_b[u], 16)

            for R in range(QB):
                if R == 0:
                    for m in range(2):
                        for u in range(2):
                            load(R, m, u)
                    sp.dma_start(wraw[:, :, :], w_out.rearrange("(j p) n -> p j n", p=P)).then_inc(s_wr, 16)
                else:
                    with steps(sp, 0, 2) as m:
                        for u in range(2):
                            load(R, m, u)
            sp.wait_ge(s_oe, NBLK)
            for c in range(PAIRS):
                sp.dma_start(mix_v[:, c, :], oT[:, c, :]).then_inc(s_st, 16)
            sp.wait_ge(s_st, 16 * PAIRS)

        @block.gpsimd
        def _(pool):
            def queries(t, u):
                q0 = corner(t, u)[1]
                for a in range(2):
                    base = qT[64 * a:64 * a + 64, 0, q0:q0 + 1] if isinstance(q0, int) else qT[64 * a:64 * a + 64, 0, ds(q0, 1)]
                    src = bass.AP(base.tensor, base.offset, [list(base.ap[0]), [SEQ, PAIRS], [GRID_W, 8], [1, WIN_C]])
                    pool.tensor_copy(qs[64 * a:64 * a + 64, u, a::2, :].rearrange("p c (r k) -> p c r k", r=8), src).then_inc(s_qs, 1)

            pool.memset(qs[:, :, :, :], 0.0).then_inc(s_qz, 1)
            for u in range(2):
                pool.memset(bias[:, u, :, :], -BIG).then_inc(s_clr, 1)
            pool.wait_ge(s_qz, 1)
            pool.wait_ge(s_clr, 2)
            pool.wait_ge(s_q, 16)
            queries(0, 0)
            queries(0, 1)
            with steps(pool, 1, QB * 2) as t:
                for u in range(2):
                    b = t * 2 + u
                    pool.wait_ge(s_clr, b)
                    pool.wait_ge(s_s, (b - 1) * HEADS)
                    pool.nop(nofuse=True)
                    queries(t, u)
                    pool.wait_ge(s_qs, b * 2 + 2)
                    pool.wait_ge(s_m, (b - 1) * HEADS)
                    pool.nop(nofuse=True)
                    pool.memset(bias[:, u, :, :], -BIG).then_inc(s_clr, 1)
            pool.wait_ge(s_wr, 16)
            for j in range(DC):
                pool.tensor_tensor(wraw[:, j, :], wraw[:, j, :], A["gate2"][:, :], ALU.mult).then_inc(s_m2, 1)
            pool.wait_ge(s_m2, DC)

        @block.vector
        def _(dve):
            def reduce(t, u, h):
                b = t * 2 + u
                i, w = b * HEADS + h, h % 2
                if h == 0:
                    dve.wait_ge(s_b[u], t * 128 + 128)
                dve.wait_ge(s_s, i + 1)
                pos(dve, s_e, (i - 1) * 2)
                dve.tensor_reduce(nm[:, w, 1:2], sx[:, w, 0:CTX], AX.X, ALU.max, negate=True).then_inc(s_red, 1)
                dve.tensor_tensor_reduce(sn[:, w, :], sl[:, w, :], bias[:, u, h, :], -1.0, 2 * BIG, ALU.add, ALU.min,
                                         nm[:, w, 0:1]).then_inc(s_red, 1)
                dve.wait_ge(s_red, i * 2 + 2)
                dve.tensor_tensor(nm[:, w, 2:3], nm[:, w, 0:1], nm[:, w, 1:2], ALU.min).then_inc(s_m, 1)

            def read_turned(t, u, h):
                i = (t * 2 + u) * HEADS + h
                dve.wait_ge(s_t, i + 1)
                pos(dve, s_pv, i - 1)
                dve.tensor_copy(pT[:, h % 2, 0:LAT], tl[:, :]).then_inc(s_evl, 1)

            def norm(t, u):
                b = t * 2 + u
                dve.wait_ge(s_pv, b * HEADS + HEADS)
                pos(dve, s_ot, b)
                dve.tensor_tensor(den[:, 0, :], sums[:, u, 0, :], sums[:, u, 1, :], ALU.add).then_inc(s_den, 1)
                dve.wait_ge(s_den, b * 2 + 1)
                dve.reciprocal(den[:, 1, :], den[:, 0, :]).then_inc(s_den, 1)
                dve.wait_ge(s_den, b * 2 + 2)
                wide = bass.AP(den[:, 1, :].tensor, den[:, 1, :].offset, [list(den[:, 1, :].ap[0]), [1, HEADS], [0, HD]])
                dve.tensor_tensor(on[:, :].rearrange("p (h d) -> p h d", h=HEADS), po[:, u, :].rearrange("p (h d) -> p h d", h=HEADS),
                                  wide, ALU.mult).then_inc(s_on, 1)

            def body(t):
                first = isinstance(t, int) and t == 0
                for u in range(2):
                    for h in range(HEADS):
                        reduce(t, u, h)
                        if h:
                            read_turned(t, u, h - 1)
                        elif u:
                            read_turned(t, 0, HEADS - 1)
                        elif not first:
                            read_turned(t - 1, 1, HEADS - 1)
                        if h == 2 and not (first and u == 0):
                            norm(t, 0) if u else norm(t - 1, 1)

            body(0)
            with steps(dve, 1, QB * 2) as t:
                body(t)
            read_turned(QB * 2 - 1, 1, HEADS - 1)
            norm(QB * 2 - 1, 1)

        @block.scalar
        def _(act):
            def exps(t, u, h):
                i, w = (t * 2 + u) * HEADS + h, h % 2
                act.wait_ge(s_m, i + 1)
                pos(act, s_t, i - 1)
                act.activation(pr[:, w, LAT:ALL], sx[:, w, 0:CTX], ACT.Exp, bias=nm[:, w, 2:3],
                               accum_out=sums[:, u, 1, h:h + 1]).then_inc(s_e, 1)
                act.activation(pr[:, w, 0:LAT], sn[:, w, :], ACT.Exp, bias=nm[:, w, 2:3], scale=-1.0,
                               accum_out=sums[:, u, 0, h:h + 1]).then_inc(s_e, 1)

            def read_turned(t, u, h):
                i = (t * 2 + u) * HEADS + h
                act.wait_ge(s_t, i + 1)
                act.activation(pT[:, h % 2, LAT:ALL], tx[:, 0:CTX], ACT.Copy).then_inc(s_evx, 1)

            def keep(t, u):
                b = t * 2 + u
                act.wait_ge(s_ot, b + 1)
                q0 = corner(t, u)[1]
                base = oT[:, 0, ds(q0, 1)] if not isinstance(q0, int) else oT[:, 0, q0:q0 + 1]
                dst = bass.AP(base.tensor, base.offset, [list(base.ap[0]), [SEQ, PAIRS], [GRID_W, 8], [1, WIN_C]])
                act.activation(dst, po[:, u, :].rearrange("p (c r k) -> p c r k", c=PAIRS, r=8), ACT.Copy).then_inc(s_oe, 1)

            def body(t):
                first = isinstance(t, int) and t == 0
                for u in range(2):
                    for h in range(HEADS):
                        exps(t, u, h)
                        if h:
                            read_turned(t, u, h - 1)
                        elif u:
                            read_turned(t, 0, HEADS - 1)
                        elif not first:
                            read_turned(t - 1, 1, HEADS - 1)
                        if h == 5 and not (first and u == 0):
                            keep(t, 0) if u else keep(t - 1, 1)

            body(0)
            with steps(act, 1, QB * 2) as t:
                body(t)
            read_turned(QB * 2 - 1, 1, HEADS - 1)
            keep(QB * 2 - 1, 1)

        @block.tensor
        def _(pe):
            def scores(t, u, h):
                b = t * 2 + u
                i, w = b * HEADS + h, h % 2
                if h == 0:
                    pe.wait_ge(s_qs, b * 2 + 2)
                pos(pe, s_m, i - 1)
                pos(pe, s_e, (i - 1) * 2)
                k0 = corner(t, u)[0]
                base = kT[:, h // 2, ds(k0, 1)] if not isinstance(k0, int) else kT[:, h // 2, k0:k0 + 1]
                keys = bass.AP(base.tensor, base.offset, [list(base.ap[0]), [GRID_W, KR], [1, SPAN]])
                q = qs[:, u, h, :]
                pe.matmul(sl[:, w, :], q, keys, start=True, stop=True)
                pe.matmul(sx[:, w, 0:CTX], q, kcT[:, h // 2, :], start=True, stop=True).then_inc(s_s, 1)

            def turn(t, u, h):
                i, w = (t * 2 + u) * HEADS + h, h % 2
                pe.wait_ge(s_e, i * 2 + 2)
                pos(pe, s_evl, i)
                pos(pe, s_evx, i)
                for c in range(LAT // P):
                    pe.transpose(tl[:, c * P:(c + 1) * P], pr[:, w, c * P:(c + 1) * P], ident[:, :])
                for c in range(CTX // P):
                    ins = pe.transpose(tx[:, c * P:(c + 1) * P], pr[:, w, LAT + c * P:LAT + (c + 1) * P], ident[:, :])
                ins.then_inc(s_t, 1)

            def weigh(t, u, h):
                b = t * 2 + u
                i, w = b * HEADS + h, h % 2
                if h == 0:
                    pe.wait_ge(s_v[u], t * 64 + 64)
                    pos(pe, s_oe, b - 1)
                pe.wait_ge(s_evl, i + 1)
                pe.wait_ge(s_evx, i + 1)
                o = po[:, u, h * HD:(h + 1) * HD]
                n = LAT // P
                for c in range(n):
                    pe.matmul(o, pT[:, w, c * P:(c + 1) * P], v[:, u, c, h * HD:(h + 1) * HD], start=(c == 0), stop=False)
                for c in range(2):
                    ins = pe.matmul(o, pT[:, w, LAT + c * P:LAT + (c + 1) * P], vc[:, c, h * HD:(h + 1) * HD], start=False, stop=(c == 1))
                ins.then_inc(s_pv, 1)

            def turn_o(t, u):
                pe.wait_ge(s_on, t * 2 + u + 1)
                for c in range(PAIRS):
                    ins = pe.transpose(po[:, u, c * P:(c + 1) * P], on[:, c * P:(c + 1) * P], ident[:, :])
                ins.then_inc(s_ot, 1)

            def body(t, last):
                first = isinstance(t, int) and t == 0
                for u in range(2):
                    for h in range(HEADS):
                        if h < HEADS - 1:
                            scores(t, u, h + 1)
                        elif not u:
                            scores(t, 1, 0)
                        elif not last:
                            scores(t + 1, 0, 0)
                        turn(t, u, h)
                        if h:
                            weigh(t, u, h - 1)
                        elif u:
                            weigh(t, 0, HEADS - 1)
                        elif not first:
                            weigh(t - 1, 1, HEADS - 1)
                        if h == 4 and not (first and u == 0):
                            turn_o(t, 0) if u else turn_o(t - 1, 1)

            pe.wait_ge(s_k, 16)
            pe.wait_ge(s_c, 32)
            scores(0, 0, 0)
            body(0, False)
            with steps(pe, 1, QB * 2 - 1) as t:
                body(t, False)
            body(QB * 2 - 1, True)
            weigh(QB * 2 - 1, 1, HEADS - 1)
            turn_o(QB * 2 - 1, 1)


def mixing(nc, sem, A, x, w_gated, ln_g, ln_b, w_router, S):
    modc, ident, score = A["modc"], A["ident"], A["score"]
    N0 = 3 * DC
    with ExitStack() as ctx:
        sb = lambda name, shape, dt=F32: ctx.enter_context(nc.sbuf_tensor(name, shape, dt))
        ps = lambda name, shape, dt=F32: ctx.enter_context(nc.psum_tensor(name, shape, dt))
        whi = sb("mi_whi", [P, DC, D], F32R)
        wlo = sb("mi_wlo", [P, DC, D], F32R)
        mt = sb("mi_mt", [P, 2, DC, P])
        mhi = sb("mi_mhi", [P, 2, DC, P], F32R)
        mlo = sb("mi_mlo", [P, 2, DC, P], F32R)
        xt = sb("mi_x", [P, 2, D])
        r = sb("mi_r", [P, D])
        x1 = sb("mi_x1", [P, 2, D])
        z2 = sb("mi_z2", [P, 2, D])
        h2 = sb("mi_h2", [P, 2, DC, P])
        g, b = sb("mi_g", [P, D]), sb("mi_b", [P, D])
        wr = sb("mi_wr", [P, DC, E])
        st, mv, rs = sb("mi_st", [P, 2, 12]), sb("mi_mv", [P, 2, 2]), sb("mi_rs", [P, 2, 2])
        half = sb("mi_half", [P, 2])
        y = ps("mi_y", [P, 2, D])
        turned = ps("mi_turned", [P, 2, 512])
        logit = ps("mi_logit", [P, 512])
        s_g = sem("mi_ln_in")
        s_whi, s_wlo = sem("mi_w_hi"), sem("mi_w_lo")
        s_mt = [sem(f"mi_mix_in{i}") for i in range(2)]
        s_x = [sem(f"mi_x_in{i}") for i in range(2)]
        s_mhi, s_mlo, s_y = sem("mi_mix_hi"), sem("mi_mix_lo"), sem("mi_y_done")
        s_r, s_dv, s_mom, s_ve, s_rs = sem("mi_residual"), sem("mi_dve_step"), sem("mi_moments"), sem("mi_var_eps"), sem("mi_rstd")
        s_x1, s_z2 = sem("mi_x1"), sem("mi_z2")
        s_x1s = [sem(f"mi_x1_out{i}") for i in range(2)]
        s_z2s = [sem(f"mi_z2_out{i}") for i in range(2)]
        s_turn, s_h2, s_lg, s_sg, s_half = sem("mi_turned"), sem("mi_h2"), sem("mi_logits"), sem("mi_score"), sem("mi_half")
        mix_v = S["mixT"].rearrange("(c p) t -> p c t", p=P)
        block = ctx.enter_context(nc.Block())
        DV = 4

        @block.sync
        def _(sp):
            for t in range(2):
                sp.dma_start(mt[:, t, :, :], mix_v[:, :, t * P:(t + 1) * P]).then_inc(s_mt[t], 16)
                sp.dma_start(xt[:, t, :], x[t * P:(t + 1) * P, :]).then_inc(s_x[t], 16)
            sp.dma_start(wr[:, :, :], w_router.rearrange("(j p) e -> p j e", p=P)).then_inc(s_g, 16)
            sp.dma_start(g[:, :], ln_g.partition_broadcast(P)).then_inc(s_g, 16)
            sp.dma_start(b[:, :], ln_b.partition_broadcast(P)).then_inc(s_g, 16)
            with steps(sp, 2, TILES, 2) as t0:
                for u in range(2):
                    t = t0 + u
                    sp.wait_ge(s_mlo, t - 1)
                    sp.dma_start(mt[:, u, :, :], mix_v[:, :, ds(t * P, P)]).then_inc(s_mt[u], 16)
                    sp.wait_ge(s_r, (t - 1) * 2)
                    sp.dma_start(xt[:, u, :], x[ds(t * P, P), :]).then_inc(s_x[u], 16)

        @block.gpsimd
        def _(pool):
            pool.memset(half[:, 0:1], -0.5).then_inc(s_half, 1)
            pool.memset(half[:, 1:2], EPS).then_inc(s_half, 1)
            pool.wait_ge(s_half, 2)

            def lo(t, u):
                pool.wait_ge(s_mhi, t + 1)
                pool.tensor_tensor(mlo[:, u, :, :], mt[:, u, :, :], mhi[:, u, :, :].bitcast(F32), ALU.subtract).then_inc(s_mlo, 1)

            def rstd(n, k):
                pool.wait_ge(s_mom, n + 1)
                pool.tensor_tensor(rs[:, k, 0:1], mv[:, k, 1:2], half[:, 1:2], ALU.add).then_inc(s_ve, 1)
                pool.wait_ge(s_ve, n + 1)
                pool.tensor_tensor(rs[:, k, 1:2], rs[:, k, 0:1], half[:, 0:1], ALU.pow).then_inc(s_rs, 1)

            lo(0, 0)
            lo(1, 1)
            with steps(pool, 0, TILES - 2, 2) as t0:
                for u in range(2):
                    t = t0 + u
                    rstd(t * 2, 0)
                    lo(t + 2, u)
                    rstd(t * 2 + 1, 1)
            for t in range(TILES - 2, TILES):
                rstd(2 * t, 0)
                rstd(2 * t + 1, 1)

        @block.vector
        def _(dve):
            for j in range(DC):
                dve.wait_ge(s_whi, j + 1)
                dve.tensor_tensor(wlo[:, j, :], w_gated[:, j, :], whi[:, j, :].bitcast(F32), ALU.subtract).then_inc(s_wlo, 1)

            def stats(src, k):
                for i in range(2):
                    ins = dve.bn_stats(st[:, k, 6 * i:6 * i + 6], src[:, 512 * i:512 * i + 512])
                ins.then_inc(s_dv, 1)

            def tile(t, u, first):
                d = t * DV
                dve.wait_ge(s_x[u], t * 8 + 16 - 8 * u)
                dve.wait_ge(s_y, t + 1)
                for i in range(2):
                    c = slice(512 * i, 512 * i + 512)
                    dve.scalar_tensor_tensor(out=r[:, c], in0=xt[:, u, c], scalar=ALPHA, in1=y[:, u, c],
                                             op0=ALU.mult, op1=ALU.add).then_inc(s_r, 1)
                dve.wait_ge(s_r, t * 2 + 2)
                stats(r, 0)
                dve.wait_ge(s_dv, d + 1)
                dve.nop(nofuse=True)
                dve.bn_aggr(mv[:, 0, :], st[:, 0, :]).then_inc(s_mom, 1)
                dve.wait_ge(s_rs, t * 2 + 1)
                dve.tensor_scalar(r[:, :], r[:, :], mv[:, 0, 0:1], rs[:, 0, 1:2], ALU.subtract, ALU.mult).then_inc(s_dv, 1)
                dve.wait_ge(s_dv, d + 2)
                dve.tensor_tensor(r[:, :], r[:, :], g[:, :], ALU.mult).then_inc(s_dv, 1)
                if not first:
                    dve.wait_ge(s_x1s[u], t * 8 - 8 * u)
                dve.wait_ge(s_dv, d + 3)
                dve.tensor_tensor(x1[:, u, :], r[:, :], b[:, :], ALU.add).then_inc(s_x1, 1)
                dve.wait_ge(s_x1, t + 1)
                stats(x1[:, u, :], 1)
                dve.wait_ge(s_dv, d + 4)
                dve.nop(nofuse=True)
                dve.bn_aggr(mv[:, 1, :], st[:, 1, :]).then_inc(s_mom, 1)
                dve.wait_ge(s_rs, t * 2 + 2)
                if not first:
                    dve.wait_ge(s_z2s[u], t * 8 - 8 * u)
                    dve.wait_ge(s_turn, t - 1)
                dve.tensor_scalar(z2[:, u, :], x1[:, u, :], mv[:, 1, 0:1], rs[:, 1, 1:2], ALU.subtract, ALU.mult).then_inc(s_z2, 1)

            dve.wait_ge(s_g, 48)
            tile(0, 0, True)
            tile(1, 1, True)
            with steps(dve, 2, TILES, 2) as t0:
                for u in range(2):
                    tile(t0 + u, u, False)

        @block.scalar
        def _(act):
            def hi(t, u):
                act.wait_ge(s_mt[u], t * 8 + 16 - 8 * u)
                pos(act, s_y, t - 1)
                act.activation(mhi[:, u, :, :], mt[:, u, :, :], ACT.Copy).then_inc(s_mhi, 1)

            def modulate(t, u):
                act.wait_ge(s_turn, t + 1)
                pos(act, s_lg, t - 1)
                for j in range(DC):
                    ins = act.activation(h2[:, u, j, :], turned[:, j // 4, (j % 4) * P:(j % 4 + 1) * P], ACT.Identity,
                                         bias=modc[:, 0, N0 + j:N0 + j + 1], scale=modc[:, 0, N0 + DC + j:N0 + DC + j + 1])
                ins.then_inc(s_h2, 1)

            def scores(t):
                act.wait_ge(s_lg, t + 1)
                cols = score[:, ds(t, 1), :].rearrange("p a e -> p (a e)") if not isinstance(t, int) else score[:, t, :]
                act.activation(cols, logit[:, 0:E], ACT.Sigmoid).then_inc(s_sg, 1)

            def store(t, u):
                rows = ds(t * P, P) if not isinstance(t, int) else slice(t * P, (t + 1) * P)
                act.wait_ge(s_x1, t + 1)
                act.dma_start(S["x1"][rows, :], x1[:, u, :]).then_inc(s_x1s[u], 16)
                act.wait_ge(s_z2, t + 1)
                act.dma_start(S["z2"][rows, :], z2[:, u, :]).then_inc(s_z2s[u], 16)

            for j in range(DC):
                act.activation(whi[:, j, :], w_gated[:, j, :], ACT.Copy).then_inc(s_whi, 1)
                if j == 1:
                    hi(0, 0)
                    hi(1, 1)
            hi(2, 0)
            store(0, 0)
            hi(3, 1)
            modulate(0, 0)
            store(1, 1)
            with steps(act, 2, TILES - 2, 2) as t0:
                for u in range(2):
                    t = t0 + u
                    hi(t + 2, u)
                    modulate(t - 1, 1 - u)
                    scores(t - 2)
                    store(t, u)
            for t in range(TILES - 2, TILES + 2):
                if t - 1 < TILES:
                    modulate(t - 1, (t - 1) % 2)
                scores(t - 2)
                if t < TILES:
                    store(t, t % 2)
            act.wait_ge(s_sg, TILES)
            for u in range(2):
                act.wait_ge(s_x1s[u], 8 * TILES)
                act.wait_ge(s_z2s[u], 8 * TILES)

        @block.tensor
        def _(pe):
            def products(t, u):
                pe.wait_ge(s_mlo, t + 1)
                pos(pe, s_r, (t - 1) * 2)
                for j in range(DC):
                    if isinstance(t, int) and t == 0:
                        pe.wait_ge(s_wlo, j + 1)
                    for i in range(2):
                        c = slice(512 * i, 512 * i + 512)
                        pe.matmul(y[:, u, c], mhi[:, u, j, :], whi[:, j, c], start=(j == 0), stop=False)
                        pe.matmul(y[:, u, c], mhi[:, u, j, :], wlo[:, j, c], start=False, stop=False)
                    for i in range(2):
                        c = slice(512 * i, 512 * i + 512)
                        ins = pe.matmul(y[:, u, c], mlo[:, u, j, :], whi[:, j, c], start=False, stop=(j == DC - 1))
                ins.then_inc(s_y, 1)

            def turn(t, u):
                pe.wait_ge(s_z2, t + 1)
                pos(pe, s_h2, t)
                for j in range(DC):
                    ins = pe.transpose(turned[:, j // 4, (j % 4) * P:(j % 4 + 1) * P], z2[:, u, j * P:(j + 1) * P], ident[:, :])
                ins.then_inc(s_turn, 1)

            def route(t, u):
                pe.wait_ge(s_h2, t + 1)
                pos(pe, s_sg, t)
                for j in range(DC):
                    ins = pe.matmul(logit[:, 0:E], h2[:, u, j, :], wr[:, j, :], start=(j == 0), stop=(j == DC - 1))
                ins.then_inc(s_lg, 1)

            products(0, 0)
            products(1, 1)
            turn(0, 0)
            pe.wait_ge(s_g, 48)
            with steps(pe, 2, TILES, 2) as t0:
                for u in range(2):
                    t = t0 + u
                    products(t, u)
                    turn(t - 1, 1 - u)
                    route(t - 2, u)
            turn(TILES - 1, 1)
            route(TILES - 2, 0)
            route(TILES - 1, 1)


def routing(nc, sem, A, router_bias, K):
    score, slots, gates, table = A["score"], A["slots"], A["gates"], A["table"]
    T, J, KT = TILES, SLOT_TILES, SEQ // P
    HB = 8
    with ExitStack() as ctx:
        sb = lambda name, shape, dt=F32: ctx.enter_context(nc.sbuf_tensor(name, shape, dt))
        ps = lambda name, shape, dt=F32: ctx.enter_context(nc.psum_tensor(name, shape, dt))
        rb = sb("ro_rb", [P, E])
        less4, less16 = sb("ro_less4", [P, 4, 4]), sb("ro_less16", [P, E, E])
        iot = sb("ro_iota", [P, P])
        k128 = sb("ro_k128", [P, KT])
        triu, ones = sb("ro_triu", [P, P]), sb("ro_ones", [P, P])
        sbias = sb("ro_sbias", [P, T, E])
        gt, eq = sb("ro_gt", [P, T * NG, 4, 4]), sb("ro_eq", [P, T * NG, 4, 4])
        rank, top = sb("ro_rank", [P, T * NG, 4]), sb("ro_top", [P, T * NG, 4])
        gs = sb("ro_gs", [P, T, NG])
        grank = sb("ro_grank", [P, T, NG])
        sel, w = sb("ro_sel", [P, T, E]), sb("ro_w", [P, T, E])
        tmp = sb("ro_tmp", [P, T, E])
        tsum = sb("ro_tsum", [P, 2, T])
        cnt = sb("ro_cnt", [P, E])
        full = sb("ro_full", [P, E, KT])
        nt, start, end = (sb(f"ro_{n}", [P, E]) for n in ("nt", "start", "end"))
        sq = sb("ro_sq", [P, E, E])
        slot = sb("ro_slot", [P, T, E])
        ab = sb("ro_ab", [P, 2, T])
        jt = sb("ro_jt", [P, J, E])
        jrow = sb("ro_jrow", [P, 3, J])
        tokf = sb("ro_tokf", [P, T])
        part7, partf = sb("ro_part7", [P, 2, 2, T], U32), sb("ro_partf", [P, 2, 2, T])
        hot_j, hot_p = sb("ro_hot_j", [P, 2 * T, J]), sb("ro_hot_p", [P, 2, HB, P])
        before = ps("ro_before", [P, T, E])
        total = ps("ro_total", [P, E])
        names = ps("ro_names", [P, J])
        s_in, s_one, s_tok = sem("ro_in"), sem("ro_ones"), sem("ro_tok")
        s_dv, s_sel, s_cnt, s_hot, s_hotd = sem("ro_dve_step"), sem("ro_sel"), sem("ro_counted"), sem("ro_one_hot"), sem("ro_named")
        block = ctx.enter_context(nc.Block())

        @block.sync
        def _(sp):
            sp.dma_start(rb[:, :], router_bias.partition_broadcast(P)).then_inc(s_in, 16)
            sp.dma_start(less4[:, :, :], K["k_less4"].partition_broadcast(P)).then_inc(s_in, 16)
            sp.dma_start(less16[:, :, :], K["k_less16"].partition_broadcast(P)).then_inc(s_in, 16)
            sp.dma_start(iot[:, :], K["k_iota"].partition_broadcast(P)).then_inc(s_in, 16)
            sp.dma_start(triu[:, :], K["k_triu"]).then_inc(s_in, 16)

        @block.gpsimd
        def _(pool):
            pool.memset(ones[:, :], 1.0).then_inc(s_one, 1)
            pool.iota(tokf[:, :], pattern=[[P, T]], base=0, channel_multiplier=1,
                      allow_small_or_imprecise_dtypes=True).then_inc(s_tok, 1)

        @block.vector
        def _(dve):
            n = [0]

            def step(ins):
                n[0] += 1
                ins.then_inc(s_dv, 1)
                dve.wait_ge(s_dv, n[0])

            def wide(ap, pattern):
                return bass.AP(ap.tensor, ap.offset, [list(ap.ap[0])] + pattern)

            def ranks(vals, count, out):
                mine, other = wide(vals, [[4, count], [1, 4], [0, 4]]), wide(vals, [[4, count], [0, 4], [1, 4]])
                dve.tensor_tensor(gt[:, 0:count], other, mine, ALU.is_gt)
                step(dve.tensor_tensor(eq[:, 0:count], other, mine, ALU.is_equal))
                step(dve.tensor_tensor(eq[:, 0:count], eq[:, 0:count], wide(less4[:, 0, 0:1], [[0, count], [4, 4], [1, 4]]), ALU.mult))
                step(dve.tensor_tensor(gt[:, 0:count], gt[:, 0:count], eq[:, 0:count], ALU.add))
                step(dve.tensor_reduce(out, gt[:, 0:count], AX.X, ALU.add))

            dve.wait_ge(s_in, 80)
            step(dve.tensor_scalar(k128[:, :], iot[:, 0:KT], float(P), None, ALU.mult))
            step(dve.tensor_tensor(sbias[:, :, :], score[:, :, :], wide(rb[:, 0:1], [[0, T], [1, E]]), ALU.add))
            ranks(sbias[:, 0, 0:1], T * NG, rank[:, :, :])
            step(dve.tensor_scalar(top[:, :, :], rank[:, :, :], 2.0, None, ALU.is_lt))
            top_e = top[:, :, :].rearrange("p (t g) j -> p t (g j)", g=NG)
            step(dve.tensor_tensor(tmp[:, :, :], sbias[:, :, :], top_e, ALU.mult))
            step(dve.tensor_reduce(gs[:, :, :], tmp[:, :, :].rearrange("p t (g j) -> p t g j", g=NG), AX.X, ALU.add))
            ranks(gs[:, 0, 0:1], T, grank[:, :, :])
            step(dve.tensor_scalar(grank[:, :, :], grank[:, :, :], 1.0, None, ALU.is_lt))
            step(dve.tensor_tensor(sel[:, :, :].rearrange("p t (g j) -> p (t g) j", g=NG), top[:, :, :],
                                   wide(grank[:, 0, 0:1], [[1, T * NG], [0, 4]]), ALU.mult))
            step(dve.tensor_tensor(w[:, :, :], sel[:, :, :], score[:, :, :], ALU.mult))
            n[0] += 1
            dve.tensor_reduce(tsum[:, 0, :], w[:, :, :], AX.X, ALU.add).then_inc(s_dv, 1)
            dve.wait_ge(s_dv, n[0])
            step(dve.reciprocal(tsum[:, 1, :], tsum[:, 0, :]))
            dve.tensor_tensor(w[:, :, :], w[:, :, :], wide(tsum[:, 1, 0:1], [[1, T], [0, E]]), ALU.mult).then_inc(s_sel, 1)
            dve.wait_ge(s_sel, 1)
            dve.wait_ge(s_cnt, 1)
            step(dve.tensor_copy(cnt[:, :], total[:, :]))
            step(dve.tensor_tensor(full[:, :, :], wide(cnt[:, 0:1], [[1, E], [0, KT]]), wide(k128[:, 0:1], [[0, E], [1, KT]]), ALU.is_gt))
            step(dve.tensor_reduce(nt[:, :], full[:, :, :], AX.X, ALU.add))
            step(dve.tensor_scalar(nt[:, :], nt[:, :], 1.0, None, ALU.max))
            step(dve.tensor_tensor(sq[:, :, :], less16[:, :, :], wide(nt[:, 0:1], [[0, E], [1, E]]), ALU.mult))
            step(dve.tensor_reduce(start[:, :], sq[:, :, :], AX.X, ALU.add))
            dve.tensor_tensor(end[:, :], start[:, :], nt[:, :], ALU.add)
            step(dve.tensor_scalar(start[:, :], start[:, :], float(P), None, ALU.mult))
            step(dve.tensor_tensor(slot[:, :, :], before[:, :, :], wide(start[:, 0:1], [[0, T], [1, E]]), ALU.add))
            step(dve.tensor_scalar(tmp[:, :, :], sel[:, :, :], -1.0e6, 1.0e6, ALU.mult, ALU.add))
            step(dve.tensor_tensor(tmp[:, :, :], tmp[:, :, :], slot[:, :, :], ALU.add))
            step(dve.tensor_reduce(ab[:, 0, :], tmp[:, :, :], AX.X, ALU.min))
            step(dve.tensor_tensor(tmp[:, :, :], sel[:, :, :], slot[:, :, :], ALU.mult))
            step(dve.tensor_reduce(ab[:, 1, :], tmp[:, :, :], AX.X, ALU.max))
            step(dve.tensor_copy(slots[:, :, :], ab[:, :, :]))
            for k in range(2):
                step(dve.tensor_tensor(tmp[:, :, :], slot[:, :, :], wide(ab[:, k, 0:1], [[1, T], [0, E]]), ALU.is_equal))
                step(dve.tensor_tensor(tmp[:, :, :], tmp[:, :, :], w[:, :, :], ALU.mult))
                step(dve.tensor_reduce(gates[:, k, :], tmp[:, :, :], AX.X, ALU.add))
            step(dve.tensor_scalar(part7[:, 0], slots[:, :, :], P - 1, None, ALU.bitwise_and))
            step(dve.tensor_scalar(part7[:, 1], slots[:, :, :], 7, None, ALU.logical_shift_right))
            step(dve.tensor_copy(partf[:, :, :, :], part7[:, :, :, :]))
            step(dve.tensor_tensor(hot_j[:, :, :], wide(partf[:, 1, 0, 0:1], [[1, 2 * T], [0, J]]),
                                   wide(iot[:, 0:1], [[0, 2 * T], [1, J]]), ALU.is_equal))
            for k in range(2):
                dve.wait_ge(s_tok, 1)
                step(dve.tensor_tensor(hot_j[:, k * T:(k + 1) * T, :], hot_j[:, k * T:(k + 1) * T, :],
                                       wide(tokf[:, 0:1], [[1, T], [0, J]]), ALU.mult))
            mods = partf[:, 0].rearrange("p k t -> p (k t)")
            for n8 in range(2 * T // HB):
                if n8 >= 2:
                    dve.wait_ge(s_hotd, n8 - 1)
                dve.tensor_tensor(hot_p[:, n8 % 2], wide(mods[:, n8 * HB:n8 * HB + 1], [[1, HB], [0, P]]),
                                  wide(iot[:, 0:1], [[0, HB], [1, P]]), ALU.is_equal).then_inc(s_hot, 1)
            step(dve.tensor_tensor(jt[:, :, :], wide(end[:, 0:1], [[0, J], [1, E]]), wide(iot[:, 0:1], [[1, J], [0, E]]), ALU.is_le))
            step(dve.tensor_reduce(jrow[:, 0, :], jt[:, :, :], AX.X, ALU.add))
            step(dve.tensor_scalar(jrow[:, 0, :], jrow[:, 0, :], float(E - 1), None, ALU.min))
            dve.tensor_tensor(jrow[:, 1, 1:J], jrow[:, 0, 1:J], jrow[:, 0, 0:J - 1], ALU.subtract)
            step(dve.memset(jrow[:, 1, 0:1], 1.0))
            step(dve.tensor_scalar(jrow[:, 2, :], jrow[:, 0, :], float(E - 1), None, ALU.is_lt))
            step(dve.tensor_tensor(jrow[:, 1, :], jrow[:, 1, :], jrow[:, 2, :], ALU.mult))
            step(dve.tensor_scalar(jrow[:, 2, :], jrow[:, 0, :], 1.0, None, ALU.add))
            step(dve.tensor_tensor(jrow[:, 1, :], jrow[:, 1, :], jrow[:, 2, :], ALU.mult))
            step(dve.tensor_copy(table[:, :, :], jrow[:, 0:2, :]))
            dve.wait_ge(s_hotd, 2 * T // HB)
            step(dve.tensor_copy(A["tok"][:, :], names[:, :]))

        @block.tensor
        def _(pe):
            pe.wait_ge(s_in, 80)
            pe.wait_ge(s_one, 1)
            pe.wait_ge(s_sel, 1)
            flat = before[:, :, :].rearrange("p t e -> p (t e)")
            pe.matmul(flat, triu[:, :], sel[:, :, :].rearrange("p t e -> p (t e)"), start=True, stop=False, skip_group_check=True)
            for t in range(T - 1):
                one = sel[:, t, 0:1]
                moving = bass.AP(one.tensor, one.offset, [list(one.ap[0]), [0, T - 1 - t], [1, E]])
                pe.matmul(flat[:, (t + 1) * E:T * E], ones[:, :], moving, start=False, stop=(t == T - 2), skip_group_check=True)
            for t in range(T):
                ins = pe.matmul(total[:, :], ones[:, :], sel[:, t, :], start=(t == 0), stop=(t == T - 1))
            ins.then_inc(s_cnt, 1)
            for n8 in range(2 * T // HB):
                pe.wait_ge(s_hot, n8 + 1)
                for i in range(HB):
                    n = n8 * HB + i
                    ins = pe.matmul(names[:, :], hot_p[:, n8 % 2, i, :], hot_j[:, n, :], start=(n == 0), stop=(n == 2 * T - 1))
                ins.then_inc(s_hotd, 1)


def experts(nc, sem, A, w_gate, w_up, w_down, S):
    modc, ident, gate5, table = A["modc"], A["ident"], A["gate5"], A["table"]
    N0, J, FC = 3 * DC, SLOT_TILES, DE // P
    HC = DC // 2
    with ExitStack() as ctx:
        sb = lambda name, shape, dt=F32: ctx.enter_context(nc.sbuf_tensor(name, shape, dt))
        ps = lambda name, shape, dt=F32: ctx.enter_context(nc.psum_tensor(name, shape, dt))
        tok = A["tok"]
        cell = sb("ex_cell", [P, 2, 1], U32)
        xg = sb("ex_x", [P, 2, D])
        h = sb("ex_h", [P, 2, DC, P])
        hhi, hlo = sb("ex_hhi", [P, 2, DC, P], F32R), sb("ex_hlo", [P, 2, DC, P], F32R)
        graw, draw = sb("ex_graw", [P, DC, 2 * DE]), sb("ex_draw", [P, FC, D])
        ghi, glo = sb("ex_ghi", [P, 2, DC, 2 * DE], F32R), sb("ex_glo", [P, 2, DC, 2 * DE], F32R)
        dhi, dlo = sb("ex_dhi", [P, 2, FC, D], F32R), sb("ex_dlo", [P, 2, FC, D], F32R)
        sg = sb("ex_silu", [P, 2, DE])
        hid = sb("ex_hid", [P, 2, DE])
        hidhi, hidlo = sb("ex_hidhi", [P, 2, DE], F32R), sb("ex_hidlo", [P, 2, DE], F32R)
        yr, y = sb("ex_y_raw", [P, 2, D]), sb("ex_y", [P, 2, D])
        pg = ps("ex_pgu", [P, 2, 2 * DE])
        ph = ps("ex_phid", [P, 512])
        py = ps("ex_py", [P, D])
        turned = ps("ex_turned", [P, 2, 512])
        s_cell = sem("ex_cell")
        s_x = [sem(f"ex_x_in{i}") for i in range(2)]
        s_gin, s_din = sem("ex_gate_up_in"), sem("ex_down_in")
        s_ghi, s_glo, s_dhi, s_dlo = sem("ex_gate_up_hi"), sem("ex_gate_up_lo"), sem("ex_down_hi"), sem("ex_down_lo")
        s_turn, s_h, s_hhi, s_hlo = sem("ex_turned"), sem("ex_h"), sem("ex_h_hi"), sem("ex_h_lo")
        s_gu, s_silu, s_hid = sem("ex_gate_up"), sem("ex_silu"), sem("ex_hid")
        s_th, s_hidT, s_dn, s_yr, s_y = sem("ex_hid_turned"), sem("ex_hid_split"), sem("ex_down"), sem("ex_y_raw"), sem("ex_y")
        s_yst = [sem(f"ex_y_out{i}") for i in range(2)]
        block = ctx.enter_context(nc.Block())

        def value(eng, row, j, top):
            cell = table[0:1, row, j:j + 1] if isinstance(j, int) else table[0:1, row, ds(j, 1)]
            eng.nop(nofuse=True)
            return eng.value_load(cell, min_val=0, max_val=top)

        def real(j):
            return not isinstance(j, int) or 0 <= j < J

        def run(eng, step):
            for j in range(-3, 2):
                step(j, j % 2)
            with steps(eng, 2, J - 4, 2) as j0:
                for u in range(2):
                    step(j0 + u, u)
            for j in range(J - 4, J + 1):
                step(j, j % 2)

        @block.sync
        def _(sp):
            def load(e, which):
                for k, w in enumerate((w_gate, w_up)):
                    sp.dma_start(graw[:, :, k * DE:(k + 1) * DE], which(w).rearrange("a (j p) f -> p (a j) f", p=P)).then_inc(s_gin, 16)
                if not isinstance(e, int):
                    sp.wait_ge(s_dlo, e)
                    sp.nop(nofuse=True)
                sp.dma_start(draw[:, :, :], which(w_down).rearrange("a (c p) n -> p (a c) n", p=P)).then_inc(s_din, 16)

            load(0, lambda w: w[0:1, :, :])
            with steps(sp, 1, E) as e:
                sp.wait_ge(s_glo, e * 2)
                sp.nop(nofuse=True)
                load(e, lambda w: w[ds(e, 1), :, :])

        @block.gpsimd
        def _(pool):
            def step(j, u):
                if real(j + 4):
                    pos(pool, s_turn, j + 3)
                    pool.nop(nofuse=True)
                    pool.tensor_copy(cell[:, u, :], tok[:, j + 4:j + 5] if isinstance(j, int) else tok[:, ds(j + 4, 1)]).then_inc(s_cell, 1)
                    pool.wait_ge(s_cell, j + 5)
                    pool.nop(nofuse=True)
                    pool.indirect_dma_start(out=xg[:, u, :], out_offset=None, in_=S["z2"],
                                            in_offset=bass.IndirectOffsetOnAxis(ap=cell[:, u, :], axis=0)).then_inc(s_x[u], 16)
                if real(j + 1):
                    pool.wait_ge(s_hhi, j + 2)
                    pool.tensor_tensor(hlo[:, 1 - u], h[:, 1 - u], hhi[:, 1 - u].bitcast(F32), ALU.subtract).then_inc(s_hlo, 1)
                if real(j - 1):
                    pool.wait_ge(s_yr, j)
                    if not (isinstance(j, int) and j < 3):
                        pool.wait_ge(s_yst[1 - u], (j - 1 + u) * 8 - 8)
                    pool.tensor_tensor(y[:, 1 - u], yr[:, 1 - u], gate5[:, :], ALU.mult).then_inc(s_y, 1)

            step(-4, 0)
            run(pool, step)

        @block.scalar
        def _(act):
            def gate_up_hi(e, par):
                act.wait_ge(s_gin, e * 32 + 32)
                for i in range(2):
                    c = slice(HC * i, HC * i + HC)
                    act.nop(nofuse=True)
                    act.activation(ghi[:, par, c].rearrange("p a j f -> p (a j) f"), graw[:, c, :], ACT.Copy).then_inc(s_ghi, 1)

            def down_hi(e, par):
                act.wait_ge(s_din, e * 16 + 16)
                act.nop(nofuse=True)
                act.activation(dhi[:, par].rearrange("p a c n -> p (a c) n"), draw[:, :, :], ACT.Copy).then_inc(s_dhi, 1)

            def step(j, u):
                if real(j):
                    e = value(act, 1, j, E - 1)
                if real(j + 2):
                    act.wait_ge(s_turn, j + 3)
                    pos(act, s_hlo, j + 1)
                    for c in range(DC):
                        ins = act.activation(h[:, u, c, :], turned[:, c // 4, (c % 4) * P:(c % 4 + 1) * P], ACT.Identity,
                                             bias=modc[:, 0, N0 + c:N0 + c + 1], scale=modc[:, 0, N0 + DC + c:N0 + DC + c + 1])
                    ins.then_inc(s_h, 1)
                if real(j):
                    pos(act, s_gu, j)
                    act.nop(nofuse=True)
                    with act.If(e):
                        gate_up_hi(e, ds(e & 1, 1))
                    act.wait_ge(s_gu, j + 1)
                    pos(act, s_hid, j - 1)
                    act.activation(sg[:, u, :], pg[:, u, 0:DE], ACT.Silu).then_inc(s_silu, 1)
                if real(j - 1):
                    act.wait_ge(s_dn, j)
                    pos(act, s_y, j - 2)
                    act.activation(yr[:, 1 - u, :], py[:, :], ACT.Copy).then_inc(s_yr, 1)
                if real(j):
                    act.nop(nofuse=True)
                    with act.If(e):
                        down_hi(e, ds(e & 1, 1))
                    act.nop(nofuse=True)
                if real(j - 1):
                    rows = ds((j - 1) * P, P) if not isinstance(j, int) else slice((j - 1) * P, j * P)
                    act.wait_ge(s_y, j)
                    act.dma_start(S["ye"][rows, :], y[:, 1 - u, :]).then_inc(s_yst[1 - u], 16)

            gate_up_hi(0, slice(0, 1))
            down_hi(0, slice(0, 1))
            run(act, step)
            for u in range(2):
                act.wait_ge(s_yst[u], 8 * J)

        @block.vector
        def _(dve):
            def gate_up_lo(e, par, i):
                c = slice(HC * i, HC * i + HC)
                dve.wait_ge(s_ghi, e * 2 + 1 + i)
                dve.nop(nofuse=True)
                dve.tensor_tensor(glo[:, par, c].rearrange("p a j f -> p (a j) f"), graw[:, c, :],
                                  ghi[:, par, c].rearrange("p a j f -> p (a j) f").bitcast(F32), ALU.subtract).then_inc(s_glo, 1)

            def down_lo(e, par):
                dve.wait_ge(s_dhi, e + 1)
                dve.nop(nofuse=True)
                dve.tensor_tensor(dlo[:, par].rearrange("p a c n -> p (a c) n"), draw[:, :, :],
                                  dhi[:, par].rearrange("p a c n -> p (a c) n").bitcast(F32), ALU.subtract).then_inc(s_dlo, 1)

            def step(j, u):
                if real(j):
                    e = value(dve, 1, j, E - 1)
                if real(j + 1):
                    dve.wait_ge(s_h, j + 2)
                    pos(dve, s_gu, j)
                    dve.tensor_copy(hhi[:, 1 - u], h[:, 1 - u]).then_inc(s_hhi, 1)
                if real(j - 1):
                    dve.wait_ge(s_th, j)
                    pos(dve, s_dn, j - 2)
                    dve.tensor_copy(hidhi[:, 1 - u, :], ph[:, 0:DE]).then_inc(s_hidT, 1)
                    dve.wait_ge(s_hidT, j * 2 - 1)
                    dve.tensor_tensor(hidlo[:, 1 - u, :], ph[:, 0:DE], hidhi[:, 1 - u, :].bitcast(F32), ALU.subtract).then_inc(s_hidT, 1)
                if real(j):
                    dve.nop(nofuse=True)
                    with dve.If(e):
                        gate_up_lo(e, ds(e & 1, 1), 0)
                        gate_up_lo(e, ds(e & 1, 1), 1)
                    dve.wait_ge(s_silu, j + 1)
                    pos(dve, s_th, j - 1)
                    dve.tensor_tensor(hid[:, u, :], sg[:, u, :], pg[:, u, DE:2 * DE], ALU.mult).then_inc(s_hid, 1)
                    dve.nop(nofuse=True)
                    with dve.If(e):
                        down_lo(e, ds(e & 1, 1))
                    dve.nop(nofuse=True)

            gate_up_lo(0, slice(0, 1), 0)
            gate_up_lo(0, slice(0, 1), 1)
            down_lo(0, slice(0, 1))
            run(dve, step)

        @block.tensor
        def _(pe):
            def turn_hid(j, u):
                pe.wait_ge(s_hid, j + 1)
                pos(pe, s_hidT, j * 2)
                for c in range(FC):
                    ins = pe.transpose(ph[:, c * P:(c + 1) * P], hid[:, u, c * P:(c + 1) * P], ident[:, :])
                ins.then_inc(s_th, 1)

            def step(j, u):
                if real(j):
                    e = value(pe, 0, j, E - 1)
                    pe.wait_ge(s_glo, e * 2 + 2)
                    par = e & 1
                    pe.wait_ge(s_hlo, j + 1)
                    pos(pe, s_hid, j - 1)
                    for c in range(DC):
                        if c == DC // 2 and real(j - 1):
                            turn_hid(j - 1, 1 - u)
                        wh, wl = (w[:, ds(par, 1), c, :].rearrange("p a f -> p (a f)") for w in (ghi, glo))
                        pe.matmul(pg[:, u, :], hhi[:, u, c, :], wh, start=(c == 0), stop=False)
                        pe.matmul(pg[:, u, :], hhi[:, u, c, :], wl, start=False, stop=False)
                        ins = pe.matmul(pg[:, u, :], hlo[:, u, c, :], wh, start=False, stop=(c == DC - 1))
                    ins.then_inc(s_gu, 1)
                elif real(j - 1):
                    turn_hid(j - 1, 1 - u)
                if real(j - 1):
                    e = value(pe, 0, j - 1, E - 1)
                    pe.wait_ge(s_dlo, e + 1)
                    par = e & 1
                    pe.wait_ge(s_hidT, j * 2)
                    pos(pe, s_yr, j - 1)
                    for c in range(FC):
                        a, b = (part[:, 1 - u, c * P:(c + 1) * P] for part in (hidhi, hidlo))
                        for i in range(2):
                            cols = slice(512 * i, 512 * i + 512)
                            wh, wl = (w[:, ds(par, 1), c, cols].rearrange("p a f -> p (a f)") for w in (dhi, dlo))
                            pe.matmul(py[:, cols], a, wh, start=(c == 0), stop=False)
                            pe.matmul(py[:, cols], a, wl, start=False, stop=False)
                        for i in range(2):
                            cols = slice(512 * i, 512 * i + 512)
                            wh = dhi[:, ds(par, 1), c, cols].rearrange("p a f -> p (a f)")
                            ins = pe.matmul(py[:, cols], b, wh, start=False, stop=(c == FC - 1))
                    ins.then_inc(s_dn, 1)
                if real(j + 3):
                    n = j + 3
                    pe.wait_ge(s_x[1 - u], (n // 2 + 1) * 16 if isinstance(n, int) else (n + u) * 8 + 8)
                    pos(pe, s_h, n)
                    for c in range(DC):
                        ins = pe.transpose(turned[:, c // 4, (c % 4) * P:(c % 4 + 1) * P], xg[:, 1 - u, c * P:(c + 1) * P], ident[:, :])
                    ins.then_inc(s_turn, 1)

            run(pe, step)


def combine(nc, sem, A, ln_g, ln_b, S, out):
    slots, gates = A["slots"], A["gates"]
    with ExitStack() as ctx:
        sb = lambda name, shape, dt=F32: ctx.enter_context(nc.sbuf_tensor(name, shape, dt))
        NB = 4
        ya, yb = sb("co_ya", [P, NB, D]), sb("co_yb", [P, NB, D])
        cell = sb("co_cell", [P, 2, NB, 1], U32)
        xt = sb("co_x1", [P, NB, D])
        r = sb("co_r", [P, NB, D])
        o = sb("co_o", [P, NB, D])
        g, b = sb("co_g", [P, D]), sb("co_b", [P, D])
        st, mv = sb("co_st", [P, 12]), sb("co_mv", [P, 2, 2])
        rs = sb("co_rs", [P, 2, 4])
        const = sb("co_const", [P, 3])
        s_g, s_const, s_cell = sem("co_ln_in"), sem("co_consts"), sem("co_cell")
        s_ya, s_yb, s_x = ([sem(f"co_{n}_in{i}") for i in range(NB)] for n in ("ya", "yb", "x1"))
        s_a, s_b, s_r, s_st, s_mom, s_pl, s_rs = (sem(f"co_{n}") for n in ("a", "b", "residual", "stats", "moments", "pool_step", "rstd"))
        s_z, s_zg, s_o = sem("co_z"), sem("co_zg"), sem("co_o")
        s_os = [sem(f"co_out{i}") for i in range(NB)]
        block = ctx.enter_context(nc.Block())

        def real(t):
            return not isinstance(t, int) or 0 <= t < TILES

        def run(eng, step):
            for t in range(-3, NB):
                step(t, t % NB)
            with steps(eng, NB, TILES - NB, NB) as t0:
                for u in range(NB):
                    step(t0 + u, u)
            for t in range(TILES - NB, TILES + 2):
                step(t, t % NB)

        def fills(t, u):
            return (t - u) * (16 // NB) + 16

        @block.sync
        def _(sp):
            sp.dma_start(g[:, :], ln_g.partition_broadcast(P)).then_inc(s_g, 16)
            sp.dma_start(b[:, :], ln_b.partition_broadcast(P)).then_inc(s_g, 16)
            for t in range(NB):
                sp.dma_start(xt[:, t, :], S["x1"][t * P:(t + 1) * P, :]).then_inc(s_x[t], 16)
            with steps(sp, NB, TILES, NB) as t0:
                for u in range(NB):
                    sp.wait_ge(s_r, t0 + u - NB + 1)
                    sp.dma_start(xt[:, u, :], S["x1"][ds((t0 + u) * P, P), :]).then_inc(s_x[u], 16)

        @block.gpsimd
        def _(pool):
            for i, value in enumerate((-0.5, EPS, -1.0)):
                pool.memset(const[:, i:i + 1], value).then_inc(s_const, 1)
            pool.wait_ge(s_const, 3)

            def step(t, u):
                if real(t + 3):
                    n, un = t + 3, (u + 3) % NB
                    pos(pool, s_b, t)
                    for k, (dst, s) in enumerate(((ya, s_ya), (yb, s_yb))):
                        pool.nop(nofuse=True)
                        pool.tensor_copy(cell[:, k, un, :], slots[:, k, n:n + 1] if isinstance(n, int) else slots[:, k, ds(n, 1)]).then_inc(s_cell, 1)
                        pool.wait_ge(s_cell, n * 2 + k + 1)
                        pool.nop(nofuse=True)
                        pool.indirect_dma_start(out=dst[:, un, :], out_offset=None, in_=S["ye"],
                                                in_offset=bass.IndirectOffsetOnAxis(ap=cell[:, k, un, :], axis=0)).then_inc(s[un], 16)
                if real(t):
                    w = u % 2
                    pool.wait_ge(s_mom, t + 1)
                    pool.tensor_tensor(rs[:, w, 0:1], mv[:, w, 1:2], const[:, 1:2], ALU.add).then_inc(s_pl, 1)
                    pool.tensor_tensor(rs[:, w, 2:3], mv[:, w, 0:1], const[:, 2:3], ALU.mult).then_inc(s_pl, 1)
                    pool.wait_ge(s_pl, t * 3 + 2)
                    pool.tensor_tensor(rs[:, w, 1:2], rs[:, w, 0:1], const[:, 0:1], ALU.pow).then_inc(s_pl, 1)
                    pool.wait_ge(s_pl, t * 3 + 3)
                    pool.tensor_tensor(rs[:, w, 3:4], rs[:, w, 2:3], rs[:, w, 1:2], ALU.mult).then_inc(s_rs, 1)
                if real(t - 1):
                    pool.wait_ge(s_zg, t)
                    up = (u + 3) % NB
                    pool.tensor_tensor(o[:, up, :], o[:, up, :], b[:, :], ALU.add).then_inc(s_o, 1)

            pool.wait_ge(s_g, 32)
            run(pool, step)

        @block.scalar
        def _(act):
            def step(t, u):
                if real(t + 1):
                    n, un = t + 1, (u + 1) % NB
                    act.wait_ge(s_ya[un], fills(n, un))
                    pos(act, s_zg, t - 2)
                    gcol = gates[:, 0, n:n + 1] if isinstance(n, int) else gates[:, 0, ds(n, 1)]
                    act.activation(r[:, un, :], ya[:, un, :], ACT.Copy, scale=gcol).then_inc(s_a, 1)
                if real(t):
                    act.wait_ge(s_rs, t + 1)
                    act.activation(r[:, u, :], r[:, u, :], ACT.Identity, bias=rs[:, u % 2, 3:4], scale=rs[:, u % 2, 1:2]).then_inc(s_z, 1)
                if real(t - 2):
                    n, un = t - 2, (u + 2) % NB
                    rows = ds(n * P, P) if not isinstance(n, int) else slice(n * P, (n + 1) * P)
                    act.wait_ge(s_o, t - 1)
                    act.dma_start(out[rows, :], o[:, un, :]).then_inc(s_os[un], 16)

            run(act, step)
            for u in range(NB):
                act.wait_ge(s_os[u], 16 // NB * TILES)

        @block.vector
        def _(dve):
            dve.wait_ge(s_g, 32)

            def step(t, u):
                if real(t):
                    w = u % 2
                    dve.wait_ge(s_yb[u], fills(t, u))
                    dve.wait_ge(s_a, t + 1)
                    gcol = gates[:, 1, t:t + 1] if isinstance(t, int) else gates[:, 1, ds(t, 1)]
                    dve.scalar_tensor_tensor(out=r[:, u, :], in0=yb[:, u, :], scalar=gcol, in1=r[:, u, :],
                                             op0=ALU.mult, op1=ALU.add).then_inc(s_b, 1)
                    dve.wait_ge(s_b, t + 1)
                    dve.wait_ge(s_x[u], fills(t, u))
                    dve.scalar_tensor_tensor(out=r[:, u, :], in0=xt[:, u, :], scalar=ALPHA, in1=r[:, u, :],
                                             op0=ALU.mult, op1=ALU.add).then_inc(s_r, 1)
                    dve.wait_ge(s_r, t + 1)
                    for i in range(2):
                        dve.bn_stats(st[:, 6 * i:6 * i + 6], r[:, u, 512 * i:512 * i + 512]).then_inc(s_st, 1)
                    dve.wait_ge(s_st, t * 2 + 2)
                    dve.nop(nofuse=True)
                    dve.bn_aggr(mv[:, w, :], st[:, :]).then_inc(s_mom, 1)
                if real(t - 1):
                    up = (u + 3) % NB
                    dve.wait_ge(s_z, t)
                    if not (isinstance(t, int) and t - 1 < NB):
                        dve.wait_ge(s_os[up], fills(t - 1 - NB, up))
                    dve.tensor_tensor(o[:, up, :], r[:, up, :], g[:, :], ALU.mult).then_inc(s_zg, 1)

            run(dve, step)


def constants():
    qc, kc = np.arange(WIN_C)[:, None], np.arange(SPAN)[None, :]
    mask = np.zeros((QB, WIN_C, SPAN), np.float32)
    for n in range(QB):
        q = n * WIN_C + qc
        k = min(max(n * WIN_C - WIN_C // 2, 0), GRID_W - SPAN) + kc
        first = np.clip(q - WIN_C // 2, 0, GRID_W - WIN_C)
        mask[n] = np.where((k >= first) & (k < first + WIN_C), 0.0, -BIG)
    a, b = np.arange(RAD), np.arange(P)
    nk = RAD // 2 + 1
    turn = 2 * np.pi * np.outer(a, np.arange(nk)) / RAD
    parts = np.concatenate([np.cos(turn), -np.sin(turn[:, 1:nk - 1])], 1)
    short = np.einsum("ac,jk->ajck", parts, np.eye(8)).reshape(P, P)
    th = 2 * np.pi * b[None, :, None] * (RAD * b[None, None, :] + np.arange(nk)[:, None, None]) / SEQ
    long = np.concatenate([np.cos(th), -np.sin(th), np.sin(th), np.cos(th)], 2)
    tc = 2 * np.pi * np.outer(np.arange(64), np.arange(64)) / 64
    norm = (SEQ * 64) ** -0.5
    chan = np.stack([np.kron(np.eye(2), np.cos(tc)), np.kron(np.eye(2), np.sin(tc))]) * norm
    return {"k_mask": mask, "k_ident": np.eye(P, dtype=np.float32), "k_short": short.astype(np.float32),
            "k_long": long.astype(np.float32), "k_chan": chan.astype(np.float32),
            "k_less4": np.tril(np.ones((4, 4), np.float32), -1), "k_less16": np.tril(np.ones((E, E), np.float32), -1),
            "k_iota": np.arange(P, dtype=np.float32), "k_triu": np.triu(np.ones((P, P), np.float32), 1)}


INPUTS = ["x", "c", "ctx", "c_ctx", "w_mod", "b_mod", "w_in", "rpb", "w_four", "w_out", "ln1_g", "ln1_b", "ln2_g",
          "ln2_b", "w_router", "router_bias", "w_gate", "w_up", "w_down"]
SCRATCH = {"xbias": [QB, WIN_C, HEADS, 15, SPAN], "qT": [NAW, SEQ], "kT": [NAW, SEQ], "kcT": [NAW, CTX],
           "vc": [CTX, NAW], "vf": [SEQ, NAW + FW],
           "hpart": [RAD, P, FW], "mixT": [NAW + FW, SEQ], "x1": [SEQ, D], "z2": [SEQ, D],
           "ye": [SLOTS, D]}


def build(nc, T, S, out):
    with ExitStack() as top:
        first_half = []

        def sem(name):
            first_half.append(nc.alloc_semaphore(name=name))
            return first_half[-1]

        keep = lambda name, shape, dt=F32: top.enter_context(nc.sbuf_tensor(name, shape, dt))
        A = {"modc": keep("modc", [P, 2, MODS * DC]), "ident": keep("ident", [P, P]),
             "score": keep("score", [P, TILES, E]), "slots": keep("slots", [P, 2, TILES], U32),
             "gates": keep("gates", [P, 2, TILES]), "tok": keep("tok", [P, SLOT_TILES], U32),
             "table": keep("table", [P, 2, SLOT_TILES], U32)}
        with ExitStack() as shared:
            sb = lambda name, shape: shared.enter_context(nc.sbuf_tensor(name, shape, F32))
            M = {"x": sb("x_tiles", [P, 2, D]), "stage": sb("stage", [P, 4, 1024]), "sc": sb("silu_c", [P, 2, DC]),
                 "bcol": sb("b_mod_col", [P, MODS * DC]),
                 "s_x": [sem(f"x_in{i}") for i in range(2)], "s_w": [sem(f"w_in_in{i}") for i in range(2)]}
            M["wst"] = [M["stage"][:, 2 * i:2 * i + 2, :].rearrange("p a b -> p (a b)") for i in range(2)]
            modulation(nc, sem, A, M, T["c"], T["c_ctx"], T["w_mod"], T["b_mod"], T["rpb"], T["k_mask"], T["k_ident"],
                       S["xbias"], T["w_in"], T["ctx"])
            projection(nc, sem, A, M, T["x"], T["w_in"], T["w_mod"], S)
        A["gate2"], A["gate5"] = keep("gate2", [P, D]), keep("gate5", [P, D])
        w_ctx = top.enter_context(ExitStack())
        wraw = w_ctx.enter_context(nc.sbuf_tensor("w_out_raw", [P, DC, D], F32))
        with ExitStack() as shared:
            sb = lambda name, shape: shared.enter_context(nc.sbuf_tensor(name, shape, F32))
            L = {"qT": sb("qT", [P, PAIRS, SEQ]), "kT": sb("kT", [P, PAIRS, SEQ]), "kcT": sb("kcT", [P, PAIRS, CTX]),
                 "vc": sb("vc", [P, 2, NAW]), "s_q": sem("q_in"), "s_k": sem("k_in"), "s_c": sem("ctx_in")}
            fourier(nc, sem, A, T["w_four"], T, S, L, wraw)
            attention(nc, sem, A, S, L, T["w_out"], wraw)
        nc.clear_and_free_semaphores(first_half)
        nc.all_engine_barrier()
        sem = lambda name: top.enter_context(nc.semaphore(name))
        mixing(nc, sem, A, T["x"], wraw, T["ln1_g"], T["ln1_b"], T["w_router"], S)
        w_ctx.close()
        routing(nc, sem, A, T["router_bias"], T)
        experts(nc, sem, A, T["w_gate"], T["w_up"], T["w_down"], S)
        combine(nc, sem, A, T["ln2_g"], T["ln2_b"], S, out)


def kernel(**inputs):
    import numpy as _np
    import concourse.bacc as _bacc
    from concourse import mybir as _mybir
    from concourse.bass_utils import run_bass_kernel_spmd as _run

    nc = _bacc.Bacc("TRN2", target_bir_lowering=False, num_devices=1)
    arrays = {name: _np.ascontiguousarray(inputs[name]) for name in INPUTS}
    arrays.update(constants())
    T = {}
    for name, a in arrays.items():
        t = nc.dram_tensor(f"in_{name}", a.shape, _mybir.dt.float32, kind="ExternalInput").ap()
        lead = name not in ("c_ctx", "w_router", "router_bias") and not name.startswith("k_")
        T[name] = t[0] if lead else t
    S = {name: nc.dram_tensor(f"s_{name}", shape, F32, kind="Internal").ap() for name, shape in SCRATCH.items()}
    out = nc.dram_tensor("out", (1, SEQ, D), _mybir.dt.float32, kind="ExternalOutput").ap()
    build(nc, T, S, out[0])
    r = _run(nc, [{f"in_{k}": v for k, v in arrays.items()}], core_ids=[0])
    return r.results[0]["out"]
```

```python
from contextlib import ExitStack, contextmanager

import numpy as np

import concourse.bass as bass
from concourse import mybir
from concourse.alu_op_type import AluOpType as ALU

F32 = mybir.dt.float32
F32R = mybir.dt.float32r
I32 = mybir.dt.int32
U32 = mybir.dt.uint32
ACT = mybir.ActivationFunctionType
AX = mybir.AxisListType
ds = bass.ds

P = 128
D = 1024
DC = D // P
SEQ, CTX = 2048, 256
TILES = SEQ // P
GRID_W, ROWS = 64, SEQ // 64
HEADS, HD = 8, 64
PAIRS = HEADS // 2
NAW = HEADS * HD
WIN_R, WIN_C = 8, 16
SPAN = 2 * WIN_C
FW = 512
IN_W = 3 * NAW + FW
E, EG, NG = 16, 4, 4
DE = 256
SLOT_TILES = 47
SLOTS = SLOT_TILES * P
TABLED = SLOT_TILES + 5
ALPHA = 2.0 ** 0.25
EPS = 1e-6
BIG = 1.0e30
QB = 4
RAD = 16
MODS = 6


def pos(eng, sem, value):
    if not isinstance(value, int) or value > 0:
        eng.wait_ge(sem, value)


@contextmanager
def steps(eng, start, stop, step=1):
    with eng.Fori(0, (stop - start) // step) as i:
        yield i * step + start


def modulation(nc, sem, A, M, c, c_ctx, w_mod, b_mod, rpb, colmask, ident_d, xbias_d, w_in, ctx_in):
    modc, ident, sc, bcol = A["modc"], A["ident"], M["sc"], M["bcol"]
    NCH = MODS * DC
    PW = 512
    NP = 2 * D // PW
    HR = HEADS * 15
    with ExitStack() as ctx:
        sb = lambda name, shape, dt=F32: ctx.enter_context(nc.sbuf_tensor(name, shape, dt))
        ps = lambda name, shape, dt=F32: ctx.enter_context(nc.psum_tensor(name, shape, dt))
        cv = sb("mo_cv", [P, 2, DC])
        sig = sb("mo_sig", [P, 2, DC])
        w = sb("mo_w", [P, NP, DC, PW])
        brow = sb("mo_brow", [NCH, P])
        pad = sb("mo_pad", [HR, 64])
        msk = sb("mo_msk", [HR, QB, WIN_C, SPAN])
        xb = sb("mo_xb", [HR, QB, WIN_C, SPAN])
        rows = sb("mo_rows", [2, NP, PW])
        pcol = ps("mo_pcol", [P, 512])
        prow = ps("mo_prow", [2, NP, 512])
        pT = ps("mo_pT", [P, 512])
        s_in, s_rpb, s_id = sem("mo_in"), sem("mo_rpb_in"), sem("mo_ident_in")
        s_w = [sem(f"mo_piece_in{i}") for i in range(NP)]
        s_sig, s_silu = sem("mo_sigmoid"), sem("mo_silu")
        s_done, s_bT, s_bcol = sem("mo_pieces_done"), sem("mo_b_turned"), sem("mo_b_col")
        s_row, s_turned = sem("mo_row_read"), sem("mo_rows_turned")
        s_col, s_pad, s_xb, s_st = sem("mo_cols"), sem("mo_pad_set"), sem("mo_xbias"), sem("mo_xbias_out")
        w_v = w_mod.rearrange("(p j) n -> p j n", j=DC)
        block = ctx.enter_context(nc.Block())

        @block.sync
        def _(sp):
            sp.dma_start(cv[:, 0, :], c.rearrange("(p j) -> p j", j=DC)).then_inc(s_in, 16)
            sp.dma_start(cv[:, 1, :], c_ctx.rearrange("(p j) -> p j", j=DC)).then_inc(s_in, 16)
            sp.dma_start(ident[:, :], ident_d).then_inc(s_id, 16)
            sp.dma_start(brow[:, :], b_mod.rearrange("(n p) -> n p", p=P)).then_inc(s_id, 16)
            for p in range(NP):
                sp.dma_start(w[:, p, :, :], w_v[:, :, p * PW:(p + 1) * PW]).then_inc(s_w[p], 16)
                if p == 0:
                    sp.wait_ge(s_pad, 1)
                    sp.dma_start(pad[:, 16:47], rpb.rearrange("h r c -> (h r) c")).then_inc(s_rpb, 16)
                    sp.dma_start(msk[:, :, :, :], colmask.partition_broadcast(HR)).then_inc(s_rpb, 16)
            for t in range(2):
                sp.dma_start(M["x"][:, t, :], ctx_in[t * P:(t + 1) * P, :]).then_inc(M["s_x"][t], 16)
            for j in range(2):
                sp.dma_start(M["wst"][j], w_in[j * P:(j + 1) * P, :]).then_inc(M["s_w"][j], 16)
            sp.wait_ge(s_xb, QB)
            for n in range(QB):
                sp.dma_start(xbias_d[n].rearrange("q h r k -> (h r) q k"), xb[:, n, :, :]).then_inc(s_st, 16)
            sp.wait_ge(s_st, 16 * QB)

        @block.gpsimd
        def _(pool):
            pool.memset(pad[:, :], 0.0).then_inc(s_pad, 1)

        @block.scalar
        def _(act):
            act.wait_ge(s_in, 32)
            act.activation(sig[:, :, :], cv[:, :, :], ACT.Sigmoid).then_inc(s_sig, 1)
            for p in range(NP):
                act.wait_ge(s_done, p + 1)
                act.activation(rows[:, p, :], prow[:, p, :], ACT.Copy).then_inc(s_row, 1)

        @block.vector
        def _(dve):
            dve.wait_ge(s_sig, 1)
            dve.tensor_tensor(sc[:, :, :], cv[:, :, :], sig[:, :, :], ALU.mult).then_inc(s_silu, 1)
            dve.wait_ge(s_rpb, 32)
            for n, shift in enumerate((0, -8, -8, -16)):
                base = pad[:, 31 + shift:32 + shift]
                skew = bass.AP(base.tensor, base.offset, [list(base.ap[0]), [-1, WIN_C], [1, SPAN]])
                dve.tensor_tensor(xb[:, n, :, :], skew, msk[:, n, :, :], ALU.add).then_inc(s_xb, 1)
            dve.wait_ge(s_bT, 1)
            dve.tensor_copy(bcol[:, :], pT[:, 0:NCH]).then_inc(s_bcol, 1)
            dve.wait_ge(s_bcol, 1)
            dve.wait_ge(s_turned, NP)
            n = slice(0, 2 * DC)
            for v in range(2):
                dve.tensor_tensor(modc[:, v, n], pcol[:, 0:4 * DC].rearrange("p (n v) -> p v n", v=2)[:, v, :],
                                  bcol[:, n], ALU.add).then_inc(s_col, 1)
            dve.wait_ge(s_col, 2)
            dve.tensor_scalar(modc[:, :, DC:2 * DC], modc[:, :, DC:2 * DC], 1.0, None, ALU.add).then_inc(s_col, 1)
            dve.wait_ge(s_col, 3)

        @block.tensor
        def _(pe):
            pe.wait_ge(s_id, 32)
            pe.transpose(pT[:, 0:NCH], brow[:, :], ident[0:NCH, 0:NCH]).then_inc(s_bT, 1)
            pe.wait_ge(s_silu, 1)

            def turn(p):
                pe.wait_ge(s_row, p + 1)
                for n in range(PW // P):
                    col = 2 * (p * (PW // P) + n)
                    ins = pe.transpose(pcol[:, col:col + 2], rows[:, p, n * P:(n + 1) * P], ident[0:2, 0:2])
                ins.then_inc(s_turned, 1)

            for p in range(NP):
                pe.wait_ge(s_w[p], 16)
                for j in range(DC):
                    mm = pe.matmul(prow[:, p, :], sc[:, :, j], w[:, p, j, :], start=(j == 0), stop=(j == DC - 1))
                mm.then_inc(s_done, 1)
                if p:
                    turn(p - 1)
            turn(NP - 1)


def projection(nc, sem, A, M, x, w_in, w_mod, S):
    modc, ident = A["modc"], A["ident"]
    PW = 512
    GW = 2 * P
    NGRP = SEQ // GW
    NO = 6
    OUTS_CTX, OUTS = 6, 12
    with ExitStack() as ctx:
        sb = lambda name, shape, dt=F32: ctx.enter_context(nc.sbuf_tensor(name, shape, dt))
        ps = lambda name, shape, dt=F32: ctx.enter_context(nc.psum_tensor(name, shape, dt))
        whi = sb("pr_whi", [P, DC, IN_W], F32R)
        wlo = sb("pr_wlo", [P, DC, IN_W], F32R)
        hhi = sb("pr_hhi", [P, 2, DC, GW], F32R)
        hlo = sb("pr_hlo", [P, 2, DC, GW], F32R)
        h = sb("pr_h", [P, DC, P])
        xt, stage = M["x"], M["stage"]
        wm = sb("pr_w_mod", [P, 4, PW])
        acc = sb("pr_acc", [P, PW])
        ones = sb("pr_ones", [P, 1])
        st = sb("pr_st", [P, 2, 12])
        mv = sb("pr_mv", [P, 2, 2])
        ve = sb("pr_ve", [P, 2])
        rs = sb("pr_rs", [P, 2])
        half = sb("pr_half", [P, 2])
        turned = ps("pr_turned", [P, 2, 512])
        out = ps("pr_out", [P, NO, 512])
        s_x, s_w, wst = M["s_x"], M["s_w"], M["wst"]
        s_wm = [sem(f"pr_w_mod_in{i}") for i in range(4)]
        s_ones, s_mac, s_pc, s_mc = sem("pr_ones"), sem("pr_mac"), sem("pr_piece"), sem("pr_piece_added")
        s_whi, s_wlo = sem("pr_w_hi"), sem("pr_w_lo")
        s_stats, s_mom, s_ve, s_rstd, s_z = sem("pr_stats"), sem("pr_moments"), sem("pr_var_eps"), sem("pr_rstd"), sem("pr_z")
        s_turn, s_mod, s_hi, s_lo = sem("pr_turned"), sem("pr_modulated"), sem("pr_h_hi"), sem("pr_h_lo")
        s_out, s_ev, s_half = sem("pr_out_ready"), sem("pr_out_read"), sem("pr_half")
        s_st = [sem(f"pr_stage_out{i}") for i in range(4)]
        mod_v = w_mod.rearrange("(p j) n -> p j n", j=DC)
        block = ctx.enter_context(nc.Block())

        @block.sync
        def _(sp):
            def load_x(t, u):
                sp.wait_ge(s_turn, t - 1)
                sp.dma_start(xt[:, u, :], x[ds((t - 2) * P, P), :]).then_inc(s_x[u], 16)

            def load_mod(g, u):
                cols = slice(2 * D, 2 * D + PW) if isinstance(g, int) and g == 0 else ds(g * PW + 2 * D, PW)
                for i in range(4):
                    pos(sp, s_mac, g * 8 + 4 * u + i - 3)
                    sp.dma_start(wm[:, i, :], mod_v[:, 4 * u + i, cols]).then_inc(s_wm[i], 16)

            for j in range(2, DC):
                sp.wait_ge(s_wlo, j - 1)
                sp.dma_start(wst[j % 2], w_in[j * P:(j + 1) * P, :]).then_inc(s_w[j % 2], 16)
            load_x(2, 0)
            load_x(3, 1)
            load_mod(0, 0)
            with steps(sp, 1, NGRP) as g:
                load_x(g * 2 + 2, 0)
                load_mod(g - 1, 1)
                load_x(g * 2 + 3, 1)
                load_mod(g, 0)
            load_mod(NGRP - 1, 1)

        @block.gpsimd
        def _(pool):
            pool.memset(half[:, 0:1], -0.5).then_inc(s_half, 1)
            pool.memset(half[:, 1:2], EPS).then_inc(s_half, 1)
            pool.memset(ones[:, :], 1.0).then_inc(s_ones, 1)
            pool.wait_ge(s_half, 2)

            def tile(t, u, par):
                pool.wait_ge(s_mom, t + 1)
                pool.tensor_tensor(ve[:, u:u + 1], mv[:, u, 1:2], half[:, 1:2], ALU.add).then_inc(s_ve, 1)
                pool.wait_ge(s_ve, t + 1)
                pool.tensor_tensor(rs[:, u:u + 1], ve[:, u:u + 1], half[:, 0:1], ALU.pow).then_inc(s_rstd, 1)
                pool.wait_ge(s_hi, t + 1)
                hs = slice(u * P, (u + 1) * P)
                pool.tensor_tensor(hlo[:, par, :, hs], h[:, :, :], hhi[:, par, :, hs].bitcast(F32), ALU.subtract).then_inc(s_lo, 1)

            tile(0, 0, 0)
            tile(1, 1, 0)
            with steps(pool, 2, 2 + TILES, 4) as t0:
                for k in range(4):
                    tile(t0 + k, k % 2, (1 + k // 2) % 2)

        @block.vector
        def _(dve):
            def add_piece(g):
                cols = ds(g * 4 + 2 * DC, 4) if not isinstance(g, int) else slice(2 * DC + 4 * g, 2 * DC + 4 * g + 4)
                dve.wait_ge(s_pc, g + 1)
                dve.nop(nofuse=True)
                dve.tensor_tensor(modc[:, 0, cols], turned[:, 0, 0:4], M["bcol"][:, cols], ALU.add).then_inc(s_mc, 1)

            def mac(g, u):
                for i in range(4):
                    n, j = g * 8 + 4 * u + i, 4 * u + i
                    dve.wait_ge(s_wm[i], (g * 2 + u + 1) * 16)
                    pos(dve, s_mac, n)
                    if j == 0:
                        pos(dve, s_pc, g)
                        dve.tensor_scalar(acc[:, :], wm[:, i, :], M["sc"][:, 0, 0:1], None, ALU.mult).then_inc(s_mac, 1)
                    else:
                        dve.scalar_tensor_tensor(out=acc[:, :], in0=wm[:, i, :], scalar=M["sc"][:, 0, j:j + 1], in1=acc[:, :],
                                                 op0=ALU.mult, op1=ALU.add).then_inc(s_mac, 1)

            def tile(t, u, v, piece=None):
                dve.wait_ge(s_x[u], (t - u) * 8 + 16)
                for i in range(2):
                    dve.bn_stats(st[:, u, 6 * i:6 * i + 6], xt[:, u, 512 * i:512 * i + 512]).then_inc(s_stats, 1)
                dve.wait_ge(s_stats, 2 * t + 2)
                dve.nop(nofuse=True)
                dve.bn_aggr(mv[:, u, :], st[:, u, :]).then_inc(s_mom, 1)
                dve.wait_ge(s_rstd, t + 1)
                dve.tensor_scalar(xt[:, u, :], xt[:, u, :], mv[:, u, 0:1], rs[:, u:u + 1], ALU.subtract, ALU.mult).then_inc(s_z, 1)
                if piece is not None:
                    add_piece(piece)
                dve.wait_ge(s_turn, t + 1)
                pos(dve, s_lo, t)
                for j in range(DC):
                    ins = dve.tensor_scalar(h[:, j, :], turned[:, j // 4, (j % 4) * P:(j % 4 + 1) * P],
                                            modc[:, v, DC + j:DC + j + 1], modc[:, v, j:j + 1], ALU.mult, ALU.add)
                ins.then_inc(s_mod, 1)

            for j in range(DC):
                dve.wait_ge(s_whi, j + 1)
                dve.tensor_tensor(wlo[:, j, :], wst[j % 2], whi[:, j, :].bitcast(F32), ALU.subtract).then_inc(s_wlo, 1)
                if 1 <= j <= 2:
                    tile(j - 1, j - 1, 1)
            tile(2, 0, 0)
            mac(0, 0)
            tile(3, 1, 0)
            mac(0, 1)
            with steps(dve, 1, NGRP) as g:
                tile(g * 2 + 2, 0, 0, g - 1)
                mac(g, 0)
                tile(g * 2 + 3, 1, 0)
                mac(g, 1)
            add_piece(NGRP - 1)
            dve.wait_ge(s_mc, NGRP)
            dve.tensor_scalar(modc[:, 0, 4 * DC:5 * DC], modc[:, 0, 4 * DC:5 * DC], 1.0, None, ALU.add).then_inc(s_mc, 1)
            dve.wait_ge(s_mc, NGRP + 1)

        def base(s):
            return 0 if isinstance(s, int) and s == 0 else s * OUTS - (OUTS - OUTS_CTX)

        @block.scalar
        def _(act):
            def hi(t, u, par):
                act.wait_ge(s_mod, t + 1)
                act.activation(hhi[:, par, :, u * P:(u + 1) * P], h[:, :, :], ACT.Copy).then_inc(s_hi, 1)

            def evac(n, slot, width, dst, scale=1.0):
                act.wait_ge(s_out, n + 1)
                act.activation(dst, out[:, slot, 0:width], ACT.Copy, scale=scale).then_inc(s_ev, 1)

            def group(s, par, is_ctx, last):
                n, k = base(s), 0
                per = 2 if is_ctx else 4
                cols = slice(0, GW) if is_ctx else ds((s - 1) * GW, GW)
                for which in range(2):
                    pos(act, s_st[which], 16 * s)
                    for o in range(per):
                        evac(n + k, k % NO, GW, stage[:, which, o * GW:(o + 1) * GW],
                             HD ** -0.5 if which == 0 and not is_ctx else 1.0)
                        k += 1
                    act.wait_ge(s_ev, n + k)
                    dst = S["kcT"][which * 2 * P:(which + 1) * 2 * P, :] if is_ctx else S["qT"] if which == 0 else S["kT"]
                    act.dma_start(dst.rearrange("(c p) t -> p c t", p=P)[:, :, cols],
                                  stage[:, which, 0:per * GW].rearrange("p (c t) -> p c t", c=per)).then_inc(s_st[which], 16)
                    if not last:
                        hi(2 * s + 2 + which, which, 1 - par)
                for u in range(2):
                    pos(act, s_st[2 + u], 16 * s)
                    for f in range(1 if is_ctx else 2):
                        evac(n + k, k % NO, 512, stage[:, 2 + u, 512 * f:512 * f + 512])
                        k += 1
                    act.wait_ge(s_ev, n + k)
                    dst, width = (S["vc"][u * P:(u + 1) * P, :], 512) if is_ctx else (S["vf"][ds((s - 1) * GW + u * P, P), :], 1024)
                    act.dma_start(dst, stage[:, 2 + u, 0:width]).then_inc(s_st[2 + u], 16)

            for j in range(DC):
                act.wait_ge(s_w[j % 2], 16 * (j // 2 + 1))
                act.activation(whi[:, j, :], wst[j % 2], ACT.Copy).then_inc(s_whi, 1)
                if 2 <= j <= 3:
                    hi(j - 2, j - 2, 0)
            group(0, 0, True, False)
            with steps(act, 1, NGRP - 1, 2) as s0:
                group(s0, 1, False, False)
                group(s0 + 1, 0, False, False)
            group(NGRP - 1, 1, False, False)
            group(NGRP, 0, False, True)
            for i in range(4):
                act.wait_ge(s_st[i], 16 * (NGRP + 1))

        @block.tensor
        def _(pe):
            def turn(t, u):
                pe.wait_ge(s_z, t + 1)
                pos(pe, s_mod, t)
                for j in range(DC):
                    ins = pe.transpose(turned[:, j // 4, (j % 4) * P:(j % 4 + 1) * P], xt[:, u, j * P:(j + 1) * P], ident[:, :])
                ins.then_inc(s_turn, 1)

            def begin(n):
                pos(pe, s_ev, n - NO + 1)

            def by_channel(n, slot, par, col):
                begin(n)
                o = out[:, slot, 0:GW]
                for j in range(DC):
                    a, b = whi[:, j, col:col + P], wlo[:, j, col:col + P]
                    pe.matmul(o, a, hhi[:, par, j, :], start=(j == 0), stop=False)
                    pe.matmul(o, a, hlo[:, par, j, :], start=False, stop=False)
                    ins = pe.matmul(o, b, hhi[:, par, j, :], start=False, stop=(j == DC - 1))
                ins.then_inc(s_out, 1)

            def by_token(n, slot, par, u, col):
                begin(n)
                o = out[:, slot, :]
                for j in range(DC):
                    a, b = hhi[:, par, j, u * P:(u + 1) * P], hlo[:, par, j, u * P:(u + 1) * P]
                    pe.matmul(o, a, whi[:, j, col:col + 512], start=(j == 0), stop=False)
                    pe.matmul(o, a, wlo[:, j, col:col + 512], start=False, stop=False)
                    ins = pe.matmul(o, b, whi[:, j, col:col + 512], start=False, stop=(j == DC - 1))
                ins.then_inc(s_out, 1)

            def turn_next(s, which):
                if which == 0:
                    pos(pe, s_mc, s)
                turn(s * 2 + 2 + which, which)

            def piece(g):
                pe.wait_ge(s_mac, g * 8 + 8)
                for n in range(PW // P):
                    ins = pe.matmul(turned[:, 0, n:n + 1], acc[:, n * P:(n + 1) * P], ones[:, :], start=True, stop=True)
                ins.then_inc(s_pc, 1)

            def context():
                pe.wait_ge(s_lo, 2)
                for j in range(DC):
                    pe.wait_ge(s_wlo, j + 1)
                    for k in range(4):
                        o, col = out[:, k, 0:GW], NAW + k * P
                        a, b = whi[:, j, col:col + P], wlo[:, j, col:col + P]
                        pe.matmul(o, a, hhi[:, 0, j, :], start=(j == 0), stop=False)
                        pe.matmul(o, a, hlo[:, 0, j, :], start=False, stop=False)
                        ins = pe.matmul(o, b, hhi[:, 0, j, :], start=False, stop=(j == DC - 1))
                        if j == DC - 1:
                            ins.then_inc(s_out, 1)
                    for u in range(2):
                        o, col = out[:, 4 + u, :], 2 * NAW
                        a, b = hhi[:, 0, j, u * P:(u + 1) * P], hlo[:, 0, j, u * P:(u + 1) * P]
                        pe.matmul(o, a, whi[:, j, col:col + NAW], start=(j == 0), stop=False)
                        pe.matmul(o, a, wlo[:, j, col:col + NAW], start=False, stop=False)
                        ins = pe.matmul(o, b, whi[:, j, col:col + NAW], start=False, stop=(j == DC - 1))
                        if j == DC - 1:
                            ins.then_inc(s_out, 1)
                for which in range(2):
                    turn_next(0, which)
                piece(0)

            def group(s, par, last):
                n, k = base(s), 0
                pe.wait_ge(s_lo, s * 2 + 2)
                for which in range(2):
                    for o in range(4):
                        by_channel(n + k, k % NO, par, k * P)
                        k += 1
                    if not last:
                        turn_next(s, which)
                for u in range(2):
                    for f in range(2):
                        by_token(n + k, k % NO, par, u, 2 * NAW + 512 * f)
                        k += 1
                if not last:
                    piece(s)

            turn(0, 0)
            turn(1, 1)
            context()
            with steps(pe, 1, NGRP - 1, 2) as s0:
                group(s0, 1, False)
                group(s0 + 1, 0, False)
            group(NGRP - 1, 1, False)
            group(NGRP, 0, True)


def fourier(nc, sem, A, w_four, K, S, L, room):
    NK = RAD // 2 + 1
    Q = FW // P
    part = {("cos", k): k for k in range(NK)} | {("sin", k): NK - 1 + k for k in range(1, NK - 1)}
    with ExitStack() as ctx:
        sb = lambda name, shape, dt=F32: ctx.enter_context(nc.sbuf_tensor(name, shape, dt))
        ps = lambda name, shape, dt=F32: ctx.enter_context(nc.psum_tensor(name, shape, dt))
        short = sb("fo_short", [P, P])
        long = sb("fo_long", [P, NK, 4 * P])
        chan = sb("fo_chan", [P, 2, P])
        w4 = sb("fo_w4", [P, Q, P])
        mix = sb("fo_mix", [P, 2, Q, P])
        f = sb("fo_f", [P, RAD, FW])
        hs = room[:, :, :].rearrange("p a (b c) -> p (a b) c", c=FW)
        hb = f
        us = sb("fo_us", [P, 2, Q, 2 * P])
        ims = sb("fo_ims", [P, 2, Q, P])
        yT = room[:, :, :].rearrange("p (q a) c -> p q (a c)", q=Q)
        pu = ps("fo_pu", [P, Q, 512])
        py = ps("fo_py", [P, Q, 512])
        s_k, s_w4z, s_w4, s_lk = sem("fo_consts_in"), sem("fo_w4_zeroed"), sem("fo_w4_in"), sem("fo_long_in")
        s_f = [sem(f"fo_f_in{i}") for i in range(4)]
        s_hp, s_hs, s_hst = sem("fo_short_done"), sem("fo_short_read"), sem("fo_short_out")
        s_hd = sem("fo_short_read_dve")
        s_hb = [sem(f"fo_part_in{i}") for i in range(NK)]
        s_gp, s_gr = sem("fo_gate_done"), sem("fo_gate_read")
        s_im = sem("fo_imaginary_read")
        s_mp, s_mix = sem("fo_mix_done"), sem("fo_mix_read")
        s_u, s_us, s_y, s_yr = sem("fo_u_done"), sem("fo_u_read"), sem("fo_y_done"), sem("fo_y_read")
        f_v = S["vf"][:, NAW:].rearrange("(a t j) c -> t a j c", a=RAD, j=8)
        h_v = S["hpart"].rearrange("c (t j) k -> t c j k", j=8)
        block = ctx.enter_context(nc.Block())

        @block.sync
        def _(sp):
            sp.dma_start(short[:, :], K["k_short"]).then_inc(s_k, 16)
            sp.dma_start(chan[:, :, :], K["k_chan"].rearrange("v p c -> p v c")).then_inc(s_k, 16)
            for t in range(RAD):
                sp.dma_start(f[:, t, :], f_v[t]).then_inc(s_f[t // 4], 16)
            sp.wait_ge(s_w4z, 1)
            for g in range(2):
                sp.dma_start(w4[64 * g:64 * g + 64, :, 64 * g:64 * g + 64],
                             w_four.rearrange("(q g) c e -> g c q e", g=2)[g]).then_inc(s_w4, 16)
            sp.dma_start(long[:, :, :], K["k_long"].rearrange("k b n -> b k n")).then_inc(s_lk, 16)
            sp.wait_ge(s_hst, 16 * RAD)
            for k in range(NK):
                for kind in ("cos", "sin"):
                    if (kind, k) in part:
                        c = part[kind, k]
                        sp.dma_start(hb[:, c, :], S["hpart"][c]).then_inc(s_hb[k], 16)
            for name, s in (("kT", "s_k"), ("qT", "s_q"), ("kcT", "s_c"), ("vc", "s_c")):
                sp.dma_start(L[name][:, :, :], S[name].rearrange("(c p) t -> p c t", p=P)).then_inc(L[s], 16)
            for q in range(Q):
                sp.wait_ge(s_yr, Q * (NK - 1) + q + 1)
                sp.dma_start(S["mixT"][NAW + q * P:NAW + (q + 1) * P, :], yT[:, q, :]).then_inc(L["s_y"], 16)

        @block.gpsimd
        def _(pool):
            pool.memset(w4[:, :, :], 0.0).then_inc(s_w4z, 1)

        @block.scalar
        def _(act):
            for t in range(RAD):
                act.wait_ge(s_hp, t + 1)
                act.activation(hs[:, t, :], pu[:, t % 4, :], ACT.Copy).then_inc(s_hs, 1)
                act.wait_ge(s_hs, t + 1)
                act.dma_start(h_v[t], hs[:, t, :]).then_inc(s_hst, 16)
            for k in range(NK + 1):
                for q in range(Q if k < NK else 0):
                    act.wait_ge(s_u, k * Q + q + 1)
                    if k >= 2:
                        act.wait_ge(s_y, (k - 2) * Q + q + 1)
                    act.activation(us[:, k % 2, q, :], pu[:, q, 0:2 * P], ACT.Copy).then_inc(s_us, 1)
                for q in range(Q if k else 0):
                    n = (k - 1) * Q + q
                    act.wait_ge(s_y, n + 1)
                    if k >= 3:
                        act.wait_ge(s_yr, n - 2 * Q + 1)
                    act.activation(ims[:, (k - 1) % 2, q, :], py[:, q, P:2 * P], ACT.Copy).then_inc(s_im, 1)

        @block.vector
        def _(dve):
            for k, gate in enumerate((A["gate2"], A["gate5"])):
                dve.wait_ge(s_gp, k + 1)
                dve.tensor_copy(gate[:, :], py[:, 2 * k:2 * k + 2, :].rearrange("p a n -> p (a n)")).then_inc(s_gr, 1)
            for v in range(2):
                dve.wait_ge(s_mp, v + 1)
                dve.tensor_copy(mix[:, v, :, :], py[:, v, :].rearrange("p (q c) -> p q c", q=Q)).then_inc(s_mix, 1)
            dve.wait_ge(s_hst, 16 * RAD)
            for k in range(NK):
                for q in range(Q):
                    dve.wait_ge(s_im, k * Q + q + 1)
                    a, b = py[:, q, 0:P], ims[:, k % 2, q, :]
                    last = dve.tensor_tensor(yT[:, q, k::RAD], a, b, ALU.add)
                    if 0 < k < NK - 1:
                        last = dve.tensor_tensor(yT[:, q, SEQ - k::-RAD], a, b, ALU.subtract)
                    last.then_inc(s_yr, 1)

        @block.tensor
        def _(pe):
            for k, first in enumerate((2 * DC, 5 * DC)):
                for j in range(DC):
                    m = A["modc"][:, 0, first + j:first + j + 1]
                    ins = pe.matmul(py[:, 2 * k + j // 4, (j % 4) * P:(j % 4 + 1) * P],
                                    bass.AP(m.tensor, m.offset, [list(m.ap[0]), [0, P]]), A["ident"][:, :], start=True, stop=True)
                ins.then_inc(s_gp, 1)
            pe.wait_ge(s_k, 32)
            for t in range(RAD):
                pe.wait_ge(s_f[t // 4], 64)
                if t >= 4:
                    pe.wait_ge(s_hs, t - 3)
                pe.matmul(pu[:, t % 4, :], short[:, :], f[:, t, :], start=True, stop=True).then_inc(s_hp, 1)
            pe.wait_ge(s_w4, 32)
            pe.wait_ge(s_gr, 2)
            for v in range(2):
                pe.matmul(py[:, v, :], chan[:, v, :], w4[:, :, :].rearrange("p q c -> p (q c)"), start=True, stop=True).then_inc(s_mp, 1)
            pe.wait_ge(s_lk, 16)
            pe.wait_ge(s_hs, RAD)
            pe.wait_ge(s_mix, 2)

            def u(k):
                both = ("sin", k) in part
                pe.wait_ge(s_hb[k], 32 if both else 16)
                for q in range(Q):
                    if k:
                        pe.wait_ge(s_us, (k - 1) * Q + q + 1)
                    cs = slice(q * P, (q + 1) * P)
                    ins = pe.matmul(pu[:, q, 0:2 * P], hb[:, part["cos", k], cs], long[:, k, 0:2 * P], start=True, stop=not both)
                    if both:
                        ins = pe.matmul(pu[:, q, 0:2 * P], hb[:, part["sin", k], cs], long[:, k, 2 * P:4 * P], start=False, stop=True)
                    ins.then_inc(s_u, 1)

            def y(k):
                for q in range(Q):
                    pe.wait_ge(s_us, k * Q + q + 1)
                    if k:
                        pe.wait_ge(s_yr, (k - 1) * Q + q + 1)
                    for part_ri in range(2):
                        c = slice(part_ri * P, (part_ri + 1) * P)
                        ins = pe.matmul(py[:, q, c], mix[:, part_ri, q, :], us[:, k % 2, q, c], start=True, stop=True)
                    ins.then_inc(s_y, 1)

            u(0)
            for k in range(1, NK):
                u(k)
                y(k - 1)
            y(NK - 1)


def attention(nc, sem, A, S, L, w_out, wraw):
    ident = A["ident"]
    NBLK = QB * QB
    KR = 16
    ITER = NBLK // 4
    LAT = KR * SPAN
    ALL = LAT + CTX
    with ExitStack() as ctx:
        sb = lambda name, shape, dt=F32: ctx.enter_context(nc.sbuf_tensor(name, shape, dt))
        ps = lambda name, shape, dt=F32: ctx.enter_context(nc.psum_tensor(name, shape, dt))
        qT, kT, kcT, vc = (L[name] for name in ("qT", "kT", "kcT", "vc"))
        v = sb("at_v", [P, 2, LAT // P, NAW])
        bias = sb("at_bias", [P, 2, HEADS, LAT])
        qs = sb("at_qs", [P, 2, HEADS, P])
        sn = sb("at_sn", [P, 2, LAT])
        nm = sb("at_nm", [P, 2, 3])
        pr = sb("at_pr", [P, 2, ALL])
        pT = sb("at_pT", [P, 2, ALL])
        sums = sb("at_sums", [P, 2, 2, HEADS])
        den = sb("at_den", [P, 2, HEADS])
        on = sb("at_on", [P, NAW])
        oT = qT
        sl = ps("at_sl", [P, 2, LAT])
        sx = ps("at_sx", [P, 2, 512])
        tl = ps("at_tl", [P, LAT])
        tx = ps("at_tx", [P, 512])
        po = ps("at_po", [P, 2, NAW])
        s_q, s_k, s_c = L["s_q"], L["s_k"], L["s_c"]
        s_wr, s_m2 = sem("at_w_out_in"), sem("at_w_out_gated")
        s_v = [sem(f"at_v_in{i}") for i in range(2)]
        s_b = [sem(f"at_bias_in{i}") for i in range(2)]
        s_clr, s_qs, s_qz = sem("at_bias_cleared"), sem("at_queries"), sem("at_queries_zeroed")
        s_s, s_red, s_m = sem("at_scores"), sem("at_reduced"), sem("at_max")
        s_e, s_t, s_evl, s_evx, s_pv = sem("at_exp"), sem("at_turned"), sem("at_turn_read_dve"), sem("at_turn_read_act"), sem("at_pv")
        s_den, s_on, s_ot, s_oe, s_st = sem("at_den"), sem("at_normed"), sem("at_o_turned"), sem("at_o_read"), sem("at_o_out")
        mix_v = S["mixT"][0:NAW, :].rearrange("(c p) t -> p c t", p=P)
        block = ctx.enter_context(nc.Block())

        def lat(s):
            return LAT if s else LAT - 4 * SPAN

        def corner(k, s, u):
            half, m = k // 2, k % 2
            R, row = (half + 1, half * 8 + 4) if s else (half * 3, half * 20)
            return row * GRID_W + (m * 3 + u) * 8, R * (8 * GRID_W) + (m * 2 + u) * WIN_C

        def previous(k, s, u, h):
            if h:
                return k, s, u, h - 1
            if u:
                return k, s, 0, HEADS - 1
            if s:
                return k, 0, 1, HEADS - 1
            return None if isinstance(k, int) and k == 0 else (k - 1, 1, 1, HEADS - 1)

        def following(k, s, u, h):
            if h < HEADS - 1:
                return k, s, u, h + 1
            if not u:
                return k, s, 1, 0
            if not s:
                return k, 1, 0, 0
            return None if isinstance(k, int) and k == ITER - 1 else (k + 1, 0, 0, 0)

        def units(k):
            return [(k, s, u, h) for s in range(2) for u in range(2) for h in range(HEADS)]

        @block.sync
        def _(sp):
            def load(half, m, s, u):
                R, row0 = (half + 1, half * 8 + 4) if s else (half * 3, half * 20)
                b = m * 4 + (8 * half + 2 * s + u)
                if isinstance(b, int) and b < 2:
                    pass
                else:
                    sp.wait_ge(s_pv, (b - 1) * HEADS)
                for kr in range(4):
                    first = m * 24 + (u * 8 + (row0 + kr) * GRID_W)
                    base = S["vf"][ds(first, 32), 0:NAW]
                    n = lat(s) // P
                    src = bass.AP(base.tensor, base.offset, [list(base.ap[0]), [4 * GRID_W * (NAW + FW), n], [1, NAW]])
                    sp.dma_start(v[32 * kr:32 * kr + 32, u, 0:n, :], src).then_inc(s_v[u], 16)
                sp.wait_ge(s_clr, b + 1)
                for qr in range(8):
                    rel = (max(qr - 4, 0), qr, qr, min(qr, 4))[R]
                    dr = row0 + rel - (8 * R + qr) + 7
                    src = S["xbias"][ds(m * 2 + u, 1), :, :, dr:dr + 8, :].rearrange("n q h r k -> (n q) h (r k)")
                    sp.dma_start(bias[16 * qr:16 * qr + 16, u, :, rel * SPAN:(rel + 8) * SPAN], src).then_inc(s_b[u], 16)

            for m in range(2):
                for s in range(2):
                    for u in range(2):
                        load(0, m, s, u)
            sp.wait_ge(L["s_y"], 16 * (FW // P))
            sp.dma_start(wraw[:, :, :], w_out.rearrange("(j p) n -> p j n", p=P)).then_inc(s_wr, 16)
            with steps(sp, 0, 2) as m:
                for s in range(2):
                    for u in range(2):
                        load(1, m, s, u)
            for blocks, first, count in ((8, 0, 1024), (14, 1536, 512), (16, 1024, 512)):
                sp.wait_ge(s_oe, blocks)
                sp.dma_start(mix_v[:, :, first:first + count], oT[:, :, first:first + count]).then_inc(s_st, 16)
            sp.wait_ge(s_st, 48)

        @block.gpsimd
        def _(pool):
            def queries(k, s, u):
                q0 = corner(k, s, u)[1]
                for a in range(2):
                    base = qT[64 * a:64 * a + 64, 0, q0:q0 + 1] if isinstance(q0, int) else qT[64 * a:64 * a + 64, 0, ds(q0, 1)]
                    src = bass.AP(base.tensor, base.offset, [list(base.ap[0]), [SEQ, PAIRS], [GRID_W, 8], [1, WIN_C]])
                    pool.tensor_copy(qs[64 * a:64 * a + 64, u, a::2, :].rearrange("p c (r k) -> p c r k", r=8), src).then_inc(s_qs, 1)

            pool.memset(qs[:, :, :, :], 0.0).then_inc(s_qz, 1)
            for u in range(2):
                pool.memset(bias[:, u, :, :], -BIG).then_inc(s_clr, 1)
            pool.wait_ge(s_qz, 1)
            pool.wait_ge(s_clr, 2)
            pool.wait_ge(s_q, 16)
            queries(0, 0, 0)
            queries(0, 0, 1)

            def renew(k, s, u):
                b = k * 4 + (2 * s + u)
                pool.wait_ge(s_clr, b)
                pool.wait_ge(s_s, (b - 1) * HEADS)
                pool.nop(nofuse=True)
                queries(k, s, u)
                pool.wait_ge(s_qs, b * 2 + 2)
                pool.wait_ge(s_m, (b - 1) * HEADS)
                pool.nop(nofuse=True)
                pool.memset(bias[:, u, :, :], -BIG).then_inc(s_clr, 1)

            for u in range(2):
                renew(0, 1, u)
            with steps(pool, 1, ITER) as k:
                for s in range(2):
                    for u in range(2):
                        renew(k, s, u)
            pool.wait_ge(s_wr, 16)
            for j in range(DC):
                pool.tensor_tensor(wraw[:, j, :], wraw[:, j, :], A["gate2"][:, :], ALU.mult).then_inc(s_m2, 1)
            pool.wait_ge(s_m2, DC)

        @block.vector
        def _(dve):
            def reduce(k, s, u, h):
                b, n = k * 4 + (2 * s + u), lat(s)
                i, w = b * HEADS + h, h % 2
                if h == 0:
                    dve.wait_ge(s_b[u], (k * 2 + s) * 128 + 128)
                dve.wait_ge(s_s, i + 1)
                pos(dve, s_e, (i - 1) * 2)
                dve.tensor_reduce(nm[:, w, 1:2], sx[:, w, 0:CTX], AX.X, ALU.max, negate=True).then_inc(s_red, 1)
                dve.tensor_tensor_reduce(sn[:, w, 0:n], sl[:, w, 0:n], bias[:, u, h, 0:n], -1.0, 2 * BIG, ALU.add, ALU.min,
                                         nm[:, w, 0:1]).then_inc(s_red, 1)
                dve.wait_ge(s_red, i * 2 + 2)
                dve.tensor_tensor(nm[:, w, 2:3], nm[:, w, 0:1], nm[:, w, 1:2], ALU.min).then_inc(s_m, 1)

            def read_turned(k, s, u, h):
                i, n = (k * 4 + (2 * s + u)) * HEADS + h, lat(s)
                dve.wait_ge(s_t, i + 1)
                pos(dve, s_pv, i - 1)
                dve.tensor_copy(pT[:, h % 2, 0:n], tl[:, 0:n]).then_inc(s_evl, 1)

            def norm(k, s, u, h):
                b = k * 4 + (2 * s + u)
                dve.wait_ge(s_pv, b * HEADS + HEADS)
                pos(dve, s_ot, b)
                dve.tensor_tensor(den[:, 0, :], sums[:, u, 0, :], sums[:, u, 1, :], ALU.add).then_inc(s_den, 1)
                dve.wait_ge(s_den, b * 2 + 1)
                dve.reciprocal(den[:, 1, :], den[:, 0, :]).then_inc(s_den, 1)
                dve.wait_ge(s_den, b * 2 + 2)
                wide = bass.AP(den[:, 1, :].tensor, den[:, 1, :].offset, [list(den[:, 1, :].ap[0]), [1, HEADS], [0, HD]])
                dve.tensor_tensor(on[:, :].rearrange("p (h d) -> p h d", h=HEADS), po[:, u, :].rearrange("p (h d) -> p h d", h=HEADS),
                                  wide, ALU.mult).then_inc(s_on, 1)

            def body(k):
                for unit in units(k):
                    reduce(*unit)
                    before = previous(*unit)
                    if before:
                        read_turned(*before)
                    done = previous(*unit[:3], 0) if unit[3] == 2 else None
                    if done:
                        norm(*done)

            body(0)
            with steps(dve, 1, ITER) as k:
                body(k)
            read_turned(ITER - 1, 1, 1, HEADS - 1)
            norm(ITER - 1, 1, 1, HEADS - 1)

        @block.scalar
        def _(act):
            def exps(k, s, u, h):
                i, w, n = (k * 4 + (2 * s + u)) * HEADS + h, h % 2, lat(s)
                act.wait_ge(s_m, i + 1)
                pos(act, s_t, i - 1)
                act.activation(pr[:, w, LAT:ALL], sx[:, w, 0:CTX], ACT.Exp, bias=nm[:, w, 2:3],
                               accum_out=sums[:, u, 1, h:h + 1]).then_inc(s_e, 1)
                act.activation(pr[:, w, 0:n], sn[:, w, 0:n], ACT.Exp, bias=nm[:, w, 2:3], scale=-1.0,
                               accum_out=sums[:, u, 0, h:h + 1]).then_inc(s_e, 1)

            def read_turned(k, s, u, h):
                i = (k * 4 + (2 * s + u)) * HEADS + h
                act.wait_ge(s_t, i + 1)
                act.activation(pT[:, h % 2, LAT:ALL], tx[:, 0:CTX], ACT.Copy).then_inc(s_evx, 1)

            def keep(k, s, u, h):
                b = k * 4 + (2 * s + u)
                act.wait_ge(s_ot, b + 1)
                q0 = corner(k, s, u)[1]
                base = oT[:, 0, ds(q0, 1)] if not isinstance(q0, int) else oT[:, 0, q0:q0 + 1]
                dst = bass.AP(base.tensor, base.offset, [list(base.ap[0]), [SEQ, PAIRS], [GRID_W, 8], [1, WIN_C]])
                act.activation(dst, po[:, u, :].rearrange("p (c r k) -> p c r k", c=PAIRS, r=8), ACT.Copy).then_inc(s_oe, 1)

            def body(k):
                for unit in units(k):
                    exps(*unit)
                    before = previous(*unit)
                    if before:
                        read_turned(*before)
                    done = previous(*unit[:3], 0) if unit[3] == 5 else None
                    if done:
                        keep(*done)

            body(0)
            with steps(act, 1, ITER) as k:
                body(k)
            read_turned(ITER - 1, 1, 1, HEADS - 1)
            keep(ITER - 1, 1, 1, HEADS - 1)

        @block.tensor
        def _(pe):
            def scores(k, s, u, h):
                b, n = k * 4 + (2 * s + u), lat(s)
                i, w = b * HEADS + h, h % 2
                if h == 0:
                    pe.wait_ge(s_qs, b * 2 + 2)
                pos(pe, s_m, i - 1)
                pos(pe, s_e, (i - 1) * 2)
                k0 = corner(k, s, u)[0]
                base = kT[:, h // 2, ds(k0, 1)] if not isinstance(k0, int) else kT[:, h // 2, k0:k0 + 1]
                keys = bass.AP(base.tensor, base.offset, [list(base.ap[0]), [GRID_W, n // SPAN], [1, SPAN]])
                q = qs[:, u, h, :]
                pe.matmul(sl[:, w, 0:n], q, keys, start=True, stop=True)
                pe.matmul(sx[:, w, 0:CTX], q, kcT[:, h // 2, :], start=True, stop=True).then_inc(s_s, 1)

            def turn(k, s, u, h):
                i, w = (k * 4 + (2 * s + u)) * HEADS + h, h % 2
                pe.wait_ge(s_e, i * 2 + 2)
                pos(pe, s_evl, i)
                pos(pe, s_evx, i)
                for c in range(lat(s) // P):
                    pe.transpose(tl[:, c * P:(c + 1) * P], pr[:, w, c * P:(c + 1) * P], ident[:, :])
                for c in range(CTX // P):
                    ins = pe.transpose(tx[:, c * P:(c + 1) * P], pr[:, w, LAT + c * P:LAT + (c + 1) * P], ident[:, :])
                ins.then_inc(s_t, 1)

            def weigh(k, s, u, h):
                b = k * 4 + (2 * s + u)
                i, w = b * HEADS + h, h % 2
                if h == 0:
                    pe.wait_ge(s_v[u], (k * 2 + s) * 64 + 64)
                    pos(pe, s_oe, b - 1)
                pe.wait_ge(s_evl, i + 1)
                pe.wait_ge(s_evx, i + 1)
                o = po[:, u, h * HD:(h + 1) * HD]
                n = lat(s) // P
                for c in range(n):
                    pe.matmul(o, pT[:, w, c * P:(c + 1) * P], v[:, u, c, h * HD:(h + 1) * HD], start=(c == 0), stop=False)
                for c in range(2):
                    ins = pe.matmul(o, pT[:, w, LAT + c * P:LAT + (c + 1) * P], vc[:, c, h * HD:(h + 1) * HD], start=False, stop=(c == 1))
                ins.then_inc(s_pv, 1)

            def turn_o(k, s, u, h):
                pe.wait_ge(s_on, k * 4 + (2 * s + u + 1))
                for c in range(PAIRS):
                    ins = pe.transpose(po[:, u, c * P:(c + 1) * P], on[:, c * P:(c + 1) * P], ident[:, :])
                ins.then_inc(s_ot, 1)

            def body(k):
                for unit in units(k):
                    after, before = following(*unit), previous(*unit)
                    if after:
                        scores(*after)
                    turn(*unit)
                    if before:
                        weigh(*before)
                    done = previous(*unit[:3], 0) if unit[3] == 4 else None
                    if done:
                        turn_o(*done)

            pe.wait_ge(s_k, 16)
            pe.wait_ge(s_c, 32)
            scores(0, 0, 0, 0)
            body(0)
            with steps(pe, 1, ITER - 1) as k:
                body(k)
            body(ITER - 1)
            weigh(ITER - 1, 1, 1, HEADS - 1)
            turn_o(ITER - 1, 1, 1, HEADS - 1)


def mixing(nc, sem, A, x, w_gated, ln_g, ln_b, w_router, S):
    modc, ident, score = A["modc"], A["ident"], A["score"]
    N0 = 3 * DC
    with ExitStack() as ctx:
        sb = lambda name, shape, dt=F32: ctx.enter_context(nc.sbuf_tensor(name, shape, dt))
        ps = lambda name, shape, dt=F32: ctx.enter_context(nc.psum_tensor(name, shape, dt))
        whi = sb("mi_whi", [P, DC, D], F32R)
        wlo = sb("mi_wlo", [P, DC, D], F32R)
        mt = sb("mi_mt", [P, 2, DC, P])
        mhi = sb("mi_mhi", [P, 2, DC, P], F32R)
        mlo = sb("mi_mlo", [P, 2, DC, P], F32R)
        xt = sb("mi_x", [P, 2, D])
        r = sb("mi_r", [P, D])
        x1 = sb("mi_x1", [P, 2, D])
        z2 = sb("mi_z2", [P, 2, D])
        h2 = sb("mi_h2", [P, 2, DC, P])
        g, b = sb("mi_g", [P, D]), sb("mi_b", [P, D])
        wr = sb("mi_wr", [P, DC, E])
        st, mv, rs = sb("mi_st", [P, 2, 12]), sb("mi_mv", [P, 2, 2]), sb("mi_rs", [P, 2, 2])
        half = sb("mi_half", [P, 2])
        y = ps("mi_y", [P, 2, D])
        turned = ps("mi_turned", [P, 2, 512])
        logit = ps("mi_logit", [P, 512])
        s_g = sem("mi_ln_in")
        s_whi, s_wlo = sem("mi_w_hi"), sem("mi_w_lo")
        s_mt = [sem(f"mi_mix_in{i}") for i in range(2)]
        s_x = [sem(f"mi_x_in{i}") for i in range(2)]
        s_mhi, s_mlo, s_y = sem("mi_mix_hi"), sem("mi_mix_lo"), sem("mi_y_done")
        s_r, s_dv, s_mom, s_ve, s_rs = sem("mi_residual"), sem("mi_dve_step"), sem("mi_moments"), sem("mi_var_eps"), sem("mi_rstd")
        s_x1, s_z2 = sem("mi_x1"), sem("mi_z2")
        s_x1s = [sem(f"mi_x1_out{i}") for i in range(2)]
        s_z2s = [sem(f"mi_z2_out{i}") for i in range(2)]
        s_turn, s_h2, s_lg, s_sg, s_half = sem("mi_turned"), sem("mi_h2"), sem("mi_logits"), sem("mi_score"), sem("mi_half")
        mix_v = S["mixT"].rearrange("(c p) t -> p c t", p=P)
        block = ctx.enter_context(nc.Block())
        DV = 4

        @block.sync
        def _(sp):
            for t in range(2):
                sp.dma_start(mt[:, t, :, :], mix_v[:, :, t * P:(t + 1) * P]).then_inc(s_mt[t], 16)
                sp.dma_start(xt[:, t, :], x[t * P:(t + 1) * P, :]).then_inc(s_x[t], 16)
            sp.dma_start(wr[:, :, :], w_router.rearrange("(j p) e -> p j e", p=P)).then_inc(s_g, 16)
            sp.dma_start(g[:, :], ln_g.partition_broadcast(P)).then_inc(s_g, 16)
            sp.dma_start(b[:, :], ln_b.partition_broadcast(P)).then_inc(s_g, 16)
            with steps(sp, 2, TILES, 2) as t0:
                for u in range(2):
                    t = t0 + u
                    sp.wait_ge(s_mlo, t - 1)
                    sp.dma_start(mt[:, u, :, :], mix_v[:, :, ds(t * P, P)]).then_inc(s_mt[u], 16)
                    sp.wait_ge(s_r, (t - 1) * 2)
                    sp.dma_start(xt[:, u, :], x[ds(t * P, P), :]).then_inc(s_x[u], 16)

        @block.gpsimd
        def _(pool):
            pool.memset(half[:, 0:1], -0.5).then_inc(s_half, 1)
            pool.memset(half[:, 1:2], EPS).then_inc(s_half, 1)
            pool.wait_ge(s_half, 2)

            def lo(t, u):
                pool.wait_ge(s_mhi, t + 1)
                pool.tensor_tensor(mlo[:, u, :, :], mt[:, u, :, :], mhi[:, u, :, :].bitcast(F32), ALU.subtract).then_inc(s_mlo, 1)

            def rstd(n, k):
                pool.wait_ge(s_mom, n + 1)
                pool.tensor_tensor(rs[:, k, 0:1], mv[:, k, 1:2], half[:, 1:2], ALU.add).then_inc(s_ve, 1)
                pool.wait_ge(s_ve, n + 1)
                pool.tensor_tensor(rs[:, k, 1:2], rs[:, k, 0:1], half[:, 0:1], ALU.pow).then_inc(s_rs, 1)

            lo(0, 0)
            lo(1, 1)
            with steps(pool, 0, TILES - 2, 2) as t0:
                for u in range(2):
                    t = t0 + u
                    rstd(t * 2, 0)
                    lo(t + 2, u)
                    rstd(t * 2 + 1, 1)
            for t in range(TILES - 2, TILES):
                rstd(2 * t, 0)
                rstd(2 * t + 1, 1)

        @block.vector
        def _(dve):
            for j in range(DC):
                dve.wait_ge(s_whi, j + 1)
                dve.tensor_tensor(wlo[:, j, :], w_gated[:, j, :], whi[:, j, :].bitcast(F32), ALU.subtract).then_inc(s_wlo, 1)

            def stats(src, k):
                for i in range(2):
                    ins = dve.bn_stats(st[:, k, 6 * i:6 * i + 6], src[:, 512 * i:512 * i + 512])
                ins.then_inc(s_dv, 1)

            def tile(t, u, first):
                d = t * DV
                dve.wait_ge(s_x[u], t * 8 + 16 - 8 * u)
                dve.wait_ge(s_y, t + 1)
                for i in range(2):
                    c = slice(512 * i, 512 * i + 512)
                    dve.scalar_tensor_tensor(out=r[:, c], in0=xt[:, u, c], scalar=ALPHA, in1=y[:, u, c],
                                             op0=ALU.mult, op1=ALU.add).then_inc(s_r, 1)
                dve.wait_ge(s_r, t * 2 + 2)
                stats(r, 0)
                dve.wait_ge(s_dv, d + 1)
                dve.nop(nofuse=True)
                dve.bn_aggr(mv[:, 0, :], st[:, 0, :]).then_inc(s_mom, 1)
                dve.wait_ge(s_rs, t * 2 + 1)
                dve.tensor_scalar(r[:, :], r[:, :], mv[:, 0, 0:1], rs[:, 0, 1:2], ALU.subtract, ALU.mult).then_inc(s_dv, 1)
                dve.wait_ge(s_dv, d + 2)
                dve.tensor_tensor(r[:, :], r[:, :], g[:, :], ALU.mult).then_inc(s_dv, 1)
                if not first:
                    dve.wait_ge(s_x1s[u], t * 8 - 8 * u)
                dve.wait_ge(s_dv, d + 3)
                dve.tensor_tensor(x1[:, u, :], r[:, :], b[:, :], ALU.add).then_inc(s_x1, 1)
                dve.wait_ge(s_x1, t + 1)
                stats(x1[:, u, :], 1)
                dve.wait_ge(s_dv, d + 4)
                dve.nop(nofuse=True)
                dve.bn_aggr(mv[:, 1, :], st[:, 1, :]).then_inc(s_mom, 1)
                dve.wait_ge(s_rs, t * 2 + 2)
                if not first:
                    dve.wait_ge(s_z2s[u], t * 8 - 8 * u)
                    dve.wait_ge(s_turn, t - 1)
                dve.tensor_scalar(z2[:, u, :], x1[:, u, :], mv[:, 1, 0:1], rs[:, 1, 1:2], ALU.subtract, ALU.mult).then_inc(s_z2, 1)

            dve.wait_ge(s_g, 48)
            tile(0, 0, True)
            tile(1, 1, True)
            with steps(dve, 2, TILES, 2) as t0:
                for u in range(2):
                    tile(t0 + u, u, False)

        @block.scalar
        def _(act):
            def hi(t, u):
                act.wait_ge(s_mt[u], t * 8 + 16 - 8 * u)
                pos(act, s_y, t - 1)
                act.activation(mhi[:, u, :, :], mt[:, u, :, :], ACT.Copy).then_inc(s_mhi, 1)

            def modulate(t, u):
                act.wait_ge(s_turn, t + 1)
                pos(act, s_lg, t - 1)
                for j in range(DC):
                    ins = act.activation(h2[:, u, j, :], turned[:, j // 4, (j % 4) * P:(j % 4 + 1) * P], ACT.Identity,
                                         bias=modc[:, 0, N0 + j:N0 + j + 1], scale=modc[:, 0, N0 + DC + j:N0 + DC + j + 1])
                ins.then_inc(s_h2, 1)

            def scores(t):
                act.wait_ge(s_lg, t + 1)
                cols = score[:, ds(t, 1), :].rearrange("p a e -> p (a e)") if not isinstance(t, int) else score[:, t, :]
                act.activation(cols, logit[:, 0:E], ACT.Sigmoid).then_inc(s_sg, 1)

            def store(t, u):
                rows = ds(t * P, P) if not isinstance(t, int) else slice(t * P, (t + 1) * P)
                act.wait_ge(s_x1, t + 1)
                act.dma_start(S["x1"][rows, :], x1[:, u, :]).then_inc(s_x1s[u], 16)
                act.wait_ge(s_z2, t + 1)
                act.dma_start(S["z2"][rows, :], z2[:, u, :]).then_inc(s_z2s[u], 16)

            for j in range(DC):
                act.activation(whi[:, j, :], w_gated[:, j, :], ACT.Copy).then_inc(s_whi, 1)
                if j == 1:
                    hi(0, 0)
                    hi(1, 1)
            hi(2, 0)
            store(0, 0)
            hi(3, 1)
            modulate(0, 0)
            store(1, 1)
            with steps(act, 2, TILES - 2, 2) as t0:
                for u in range(2):
                    t = t0 + u
                    hi(t + 2, u)
                    modulate(t - 1, 1 - u)
                    scores(t - 2)
                    store(t, u)
            for t in range(TILES - 2, TILES + 2):
                if t - 1 < TILES:
                    modulate(t - 1, (t - 1) % 2)
                scores(t - 2)
                if t < TILES:
                    store(t, t % 2)
            act.wait_ge(s_sg, TILES)
            for u in range(2):
                act.wait_ge(s_x1s[u], 8 * TILES)
                act.wait_ge(s_z2s[u], 8 * TILES)

        @block.tensor
        def _(pe):
            def products(t, u):
                pe.wait_ge(s_mlo, t + 1)
                pos(pe, s_r, (t - 1) * 2)
                for j in range(DC):
                    if isinstance(t, int) and t == 0:
                        pe.wait_ge(s_wlo, j + 1)
                    for i in range(2):
                        c = slice(512 * i, 512 * i + 512)
                        pe.matmul(y[:, u, c], mhi[:, u, j, :], whi[:, j, c], start=(j == 0), stop=False)
                        pe.matmul(y[:, u, c], mhi[:, u, j, :], wlo[:, j, c], start=False, stop=False)
                    for i in range(2):
                        c = slice(512 * i, 512 * i + 512)
                        ins = pe.matmul(y[:, u, c], mlo[:, u, j, :], whi[:, j, c], start=False, stop=(j == DC - 1))
                ins.then_inc(s_y, 1)

            def turn(t, u):
                pe.wait_ge(s_z2, t + 1)
                pos(pe, s_h2, t)
                for j in range(DC):
                    ins = pe.transpose(turned[:, j // 4, (j % 4) * P:(j % 4 + 1) * P], z2[:, u, j * P:(j + 1) * P], ident[:, :])
                ins.then_inc(s_turn, 1)

            def route(t, u):
                pe.wait_ge(s_h2, t + 1)
                pos(pe, s_sg, t)
                for j in range(DC):
                    ins = pe.matmul(logit[:, 0:E], h2[:, u, j, :], wr[:, j, :], start=(j == 0), stop=(j == DC - 1))
                ins.then_inc(s_lg, 1)

            products(0, 0)
            products(1, 1)
            turn(0, 0)
            pe.wait_ge(s_g, 48)
            with steps(pe, 2, TILES, 2) as t0:
                for u in range(2):
                    t = t0 + u
                    products(t, u)
                    turn(t - 1, 1 - u)
                    route(t - 2, u)
            turn(TILES - 1, 1)
            route(TILES - 2, 0)
            route(TILES - 1, 1)


def expert_weights(nc, keep, sem, T):
    sb = lambda name, shape, dt=F32: keep.enter_context(nc.sbuf_tensor(name, shape, dt))
    return {"w_gate": T["w_gate"], "w_up": T["w_up"], "w_down": T["w_down"],
            "graw": sb("ew_graw", [P, 2, DC, 2 * DE]), "draw": sb("ew_draw", [P, DE // P, D]),
            "ghi": sb("ew_ghi", [P, 2, DC, 2 * DE], F32R), "glo": sb("ew_glo", [P, 2, DC, 2 * DE], F32R),
            "dhi": sb("ew_dhi", [P, 2, DE // P, D], F32R), "dlo": sb("ew_dlo", [P, 2, DE // P, D], F32R),
            "s_gin": sem("ew_gate_up_in"), "s_din": sem("ew_down_in"), "s_ghi": sem("ew_gate_up_hi"),
            "s_glo": [sem(f"ew_gate_up_lo{i}") for i in range(2)], "s_dhi": sem("ew_down_hi"), "s_dlo": sem("ew_down_lo")}


def expert(w, e):
    return w[ds(e, 1), :, :] if not isinstance(e, int) else w[e:e + 1, :, :]


def load_gate_up(sp, W, e, u):
    if not isinstance(e, int):
        for i in range(2):
            sp.wait_ge(W["s_glo"][i], e - 1)
            sp.nop(nofuse=True)
    pos(sp, W["s_gin"], e * 32)
    sp.nop(nofuse=True)
    for k, name in enumerate(("w_gate", "w_up")):
        sp.dma_start(W["graw"][:, u, :, k * DE:(k + 1) * DE],
                     expert(W[name], e).rearrange("a (j p) f -> p (a j) f", p=P)).then_inc(W["s_gin"], 16)


def load_down(sp, W, e):
    pos(sp, W["s_dlo"], e)
    sp.nop(nofuse=True)
    sp.dma_start(W["draw"][:, :, :], expert(W["w_down"], e).rearrange("a (c p) n -> p (a c) n", p=P)).then_inc(W["s_din"], 16)


def halves(W, name, par, i):
    return W[name][:, par, i * DC // 2:(i + 1) * DC // 2].rearrange("p a j f -> p (a j) f")


def gate_up_hi(act, W, e, par):
    act.wait_ge(W["s_gin"], e * 32 + 32)
    for i in range(2):
        act.nop(nofuse=True)
        act.activation(halves(W, "ghi", par, i), halves(W, "graw", par, i), ACT.Copy).then_inc(W["s_ghi"], 1)


def gate_up_lo(eng, W, e, par, i):
    eng.wait_ge(W["s_ghi"], e * 2 + 1 + i)
    eng.nop(nofuse=True)
    eng.tensor_tensor(halves(W, "glo", par, i), halves(W, "graw", par, i), halves(W, "ghi", par, i).bitcast(F32),
                      ALU.subtract).then_inc(W["s_glo"][i], 1)


def down_hi(act, W, e, par):
    act.wait_ge(W["s_din"], e * 16 + 16)
    act.nop(nofuse=True)
    act.activation(W["dhi"][:, par].rearrange("p a c n -> p (a c) n"), W["draw"][:, :, :], ACT.Copy).then_inc(W["s_dhi"], 1)


def down_lo(eng, W, e, par):
    eng.wait_ge(W["s_dhi"], e + 1)
    eng.nop(nofuse=True)
    eng.tensor_tensor(W["dlo"][:, par].rearrange("p a c n -> p (a c) n"), W["draw"][:, :, :],
                      W["dhi"][:, par].rearrange("p a c n -> p (a c) n").bitcast(F32), ALU.subtract).then_inc(W["s_dlo"], 1)


def routing(nc, sem, A, W, router_bias, K):
    score, slots, gates, table = A["score"], A["slots"], A["gates"], A["table"]
    pairs = A["pairs"]
    T, J, KT = TILES, TABLED, SEQ // P
    HB = 8
    with ExitStack() as ctx:
        sb = lambda name, shape, dt=F32: ctx.enter_context(nc.sbuf_tensor(name, shape, dt))
        ps = lambda name, shape, dt=F32: ctx.enter_context(nc.psum_tensor(name, shape, dt))
        rb = sb("ro_rb", [P, E])
        less4, less16 = sb("ro_less4", [P, 4, 4]), sb("ro_less16", [P, E, E])
        iot = sb("ro_iota", [P, P])
        k128 = sb("ro_k128", [P, KT])
        triu, ones = sb("ro_triu", [P, P]), sb("ro_ones", [P, P])
        sbias = sb("ro_sbias", [P, T, E])
        gt, eq = sb("ro_gt", [P, T * NG, 4, 4]), sb("ro_eq", [P, T * NG, 4, 4])
        rank, top = sb("ro_rank", [P, T * NG, 4]), sb("ro_top", [P, T * NG, 4])
        gs = sb("ro_gs", [P, T, NG])
        grank = sb("ro_grank", [P, T, NG])
        sel, w = sb("ro_sel", [P, T, E]), sb("ro_w", [P, T, E])
        tmp = sb("ro_tmp", [P, T, E])
        tsum = sb("ro_tsum", [P, 2, T])
        cnt = sb("ro_cnt", [P, E])
        full = sb("ro_full", [P, E, KT])
        nt, start, end = (sb(f"ro_{n}", [P, E]) for n in ("nt", "start", "end"))
        sq = sb("ro_sq", [P, E, E])
        slot = sb("ro_slot", [P, T, E])
        ab = sb("ro_ab", [P, 2, T])
        jt = sb("ro_jt", [P, J, E])
        jrow = sb("ro_jrow", [P, 4, J])
        tokf = sb("ro_tokf", [P, T])
        part7, partf = sb("ro_part7", [P, 2, 2, T], U32), sb("ro_partf", [P, 2, 2, T])
        hot_j, hot_p = sb("ro_hot_j", [P, 2 * T, J]), sb("ro_hot_p", [P, 2, HB, P])
        before = ps("ro_before", [P, T, E])
        total = ps("ro_total", [P, E])
        names = ps("ro_names", [P, J])
        s_in, s_one, s_tok = sem("ro_in"), sem("ro_ones"), sem("ro_tok")
        s_dv, s_sel, s_cnt, s_hot, s_hotd = sem("ro_dve_step"), sem("ro_sel"), sem("ro_counted"), sem("ro_one_hot"), sem("ro_named")
        block = ctx.enter_context(nc.Block())

        @block.sync
        def _(sp):
            sp.dma_start(rb[:, :], router_bias.partition_broadcast(P)).then_inc(s_in, 16)
            sp.dma_start(less4[:, :, :], K["k_less4"].partition_broadcast(P)).then_inc(s_in, 16)
            sp.dma_start(less16[:, :, :], K["k_less16"].partition_broadcast(P)).then_inc(s_in, 16)
            sp.dma_start(iot[:, :], K["k_iota"].partition_broadcast(P)).then_inc(s_in, 16)
            sp.dma_start(triu[:, :], K["k_triu"]).then_inc(s_in, 16)
            load_gate_up(sp, W, 0, 0)
            load_down(sp, W, 0)
            load_gate_up(sp, W, 1, 1)

        @block.scalar
        def _(act):
            gate_up_hi(act, W, 0, slice(0, 1))
            down_hi(act, W, 0, slice(0, 1))

        @block.gpsimd
        def _(pool):
            pool.memset(ones[:, :], 1.0).then_inc(s_one, 1)
            pool.iota(tokf[:, :], pattern=[[P, T]], base=0, channel_multiplier=1,
                      allow_small_or_imprecise_dtypes=True).then_inc(s_tok, 1)
            for i in range(2):
                gate_up_lo(pool, W, 0, slice(0, 1), i)
            down_lo(pool, W, 0, slice(0, 1))

        @block.vector
        def _(dve):
            n = [0]

            def step(ins):
                n[0] += 1
                ins.then_inc(s_dv, 1)
                dve.wait_ge(s_dv, n[0])

            def wide(ap, pattern):
                return bass.AP(ap.tensor, ap.offset, [list(ap.ap[0])] + pattern)

            def ranks(vals, count, out):
                mine, other = wide(vals, [[4, count], [1, 4], [0, 4]]), wide(vals, [[4, count], [0, 4], [1, 4]])
                dve.tensor_tensor(gt[:, 0:count], other, mine, ALU.is_gt)
                step(dve.tensor_tensor(eq[:, 0:count], other, mine, ALU.is_equal))
                step(dve.tensor_tensor(eq[:, 0:count], eq[:, 0:count], wide(less4[:, 0, 0:1], [[0, count], [4, 4], [1, 4]]), ALU.mult))
                step(dve.tensor_tensor(gt[:, 0:count], gt[:, 0:count], eq[:, 0:count], ALU.add))
                step(dve.tensor_reduce(out, gt[:, 0:count], AX.X, ALU.add))

            dve.wait_ge(s_in, 80)
            step(dve.tensor_scalar(k128[:, :], iot[:, 0:KT], float(P), None, ALU.mult))
            step(dve.tensor_tensor(sbias[:, :, :], score[:, :, :], wide(rb[:, 0:1], [[0, T], [1, E]]), ALU.add))
            ranks(sbias[:, 0, 0:1], T * NG, rank[:, :, :])
            step(dve.tensor_scalar(top[:, :, :], rank[:, :, :], 2.0, None, ALU.is_lt))
            top_e = top[:, :, :].rearrange("p (t g) j -> p t (g j)", g=NG)
            step(dve.tensor_tensor(tmp[:, :, :], sbias[:, :, :], top_e, ALU.mult))
            step(dve.tensor_reduce(gs[:, :, :], tmp[:, :, :].rearrange("p t (g j) -> p t g j", g=NG), AX.X, ALU.add))
            ranks(gs[:, 0, 0:1], T, grank[:, :, :])
            step(dve.tensor_scalar(grank[:, :, :], grank[:, :, :], 1.0, None, ALU.is_lt))
            step(dve.tensor_tensor(sel[:, :, :].rearrange("p t (g j) -> p (t g) j", g=NG), top[:, :, :],
                                   wide(grank[:, 0, 0:1], [[1, T * NG], [0, 4]]), ALU.mult))
            step(dve.tensor_tensor(w[:, :, :], sel[:, :, :], score[:, :, :], ALU.mult))
            n[0] += 1
            dve.tensor_reduce(tsum[:, 0, :], w[:, :, :], AX.X, ALU.add).then_inc(s_dv, 1)
            dve.wait_ge(s_dv, n[0])
            step(dve.reciprocal(tsum[:, 1, :], tsum[:, 0, :]))
            dve.tensor_tensor(w[:, :, :], w[:, :, :], wide(tsum[:, 1, 0:1], [[1, T], [0, E]]), ALU.mult).then_inc(s_sel, 1)
            dve.wait_ge(s_sel, 1)
            dve.wait_ge(s_cnt, 1)
            step(dve.tensor_copy(cnt[:, :], total[:, :]))
            step(dve.tensor_tensor(full[:, :, :], wide(cnt[:, 0:1], [[1, E], [0, KT]]), wide(k128[:, 0:1], [[0, E], [1, KT]]), ALU.is_gt))
            step(dve.tensor_reduce(nt[:, :], full[:, :, :], AX.X, ALU.add))
            step(dve.tensor_scalar(nt[:, :], nt[:, :], 1.0, None, ALU.max))
            step(dve.tensor_tensor(sq[:, :, :], less16[:, :, :], wide(nt[:, 0:1], [[0, E], [1, E]]), ALU.mult))
            step(dve.tensor_reduce(start[:, :], sq[:, :, :], AX.X, ALU.add))
            dve.tensor_tensor(end[:, :], start[:, :], nt[:, :], ALU.add)
            step(dve.tensor_scalar(start[:, :], start[:, :], float(P), None, ALU.mult))
            step(dve.tensor_tensor(slot[:, :, :], before[:, :, :], wide(start[:, 0:1], [[0, T], [1, E]]), ALU.add))
            step(dve.tensor_scalar(tmp[:, :, :], sel[:, :, :], -1.0e6, 1.0e6, ALU.mult, ALU.add))
            step(dve.tensor_tensor(tmp[:, :, :], tmp[:, :, :], slot[:, :, :], ALU.add))
            step(dve.tensor_reduce(ab[:, 0, :], tmp[:, :, :], AX.X, ALU.min))
            step(dve.tensor_tensor(tmp[:, :, :], sel[:, :, :], slot[:, :, :], ALU.mult))
            step(dve.tensor_reduce(ab[:, 1, :], tmp[:, :, :], AX.X, ALU.max))
            step(dve.tensor_copy(slots[:, :, :], ab[:, :, :]))
            for k in range(2):
                step(dve.tensor_tensor(tmp[:, :, :], slot[:, :, :], wide(ab[:, k, 0:1], [[1, T], [0, E]]), ALU.is_equal))
                step(dve.tensor_tensor(tmp[:, :, :], tmp[:, :, :], w[:, :, :], ALU.mult))
                step(dve.tensor_reduce(gates[:, k, :], tmp[:, :, :], AX.X, ALU.add))
            step(dve.tensor_scalar(part7[:, 0], slots[:, :, :], P - 1, None, ALU.bitwise_and))
            step(dve.tensor_scalar(part7[:, 1], slots[:, :, :], 7, None, ALU.logical_shift_right))
            step(dve.tensor_copy(partf[:, :, :, :], part7[:, :, :, :]))
            step(dve.tensor_tensor(hot_j[:, :, :], wide(partf[:, 1, 0, 0:1], [[1, 2 * T], [0, J]]),
                                   wide(iot[:, 0:1], [[0, 2 * T], [1, J]]), ALU.is_equal))
            for k in range(2):
                dve.wait_ge(s_tok, 1)
                step(dve.tensor_tensor(hot_j[:, k * T:(k + 1) * T, :], hot_j[:, k * T:(k + 1) * T, :],
                                       wide(tokf[:, 0:1], [[1, T], [0, J]]), ALU.mult))
            mods = partf[:, 0].rearrange("p k t -> p (k t)")
            for n8 in range(2 * T // HB):
                if n8 >= 2:
                    dve.wait_ge(s_hotd, n8 - 1)
                dve.tensor_tensor(hot_p[:, n8 % 2], wide(mods[:, n8 * HB:n8 * HB + 1], [[1, HB], [0, P]]),
                                  wide(iot[:, 0:1], [[0, HB], [1, P]]), ALU.is_equal).then_inc(s_hot, 1)
            step(dve.tensor_tensor(jt[:, :, :], wide(end[:, 0:1], [[0, J], [1, E]]), wide(iot[:, 0:1], [[1, J], [0, E]]), ALU.is_le))
            step(dve.tensor_reduce(jrow[:, 0, :], jt[:, :, :], AX.X, ALU.add))
            step(dve.tensor_scalar(jrow[:, 0, :], jrow[:, 0, :], float(E - 1), None, ALU.min))
            dve.tensor_tensor(jrow[:, 1, 1:J], jrow[:, 0, 1:J], jrow[:, 0, 0:J - 1], ALU.subtract)
            step(dve.memset(jrow[:, 1, 0:1], 1.0))
            step(dve.tensor_scalar(jrow[:, 2, :], jrow[:, 0, :], float(E - 1), None, ALU.is_lt))
            step(dve.tensor_tensor(jrow[:, 1, :], jrow[:, 1, :], jrow[:, 2, :], ALU.mult))
            step(dve.tensor_scalar(jrow[:, 2, :], jrow[:, 0, :], 1.0, None, ALU.add))
            step(dve.tensor_tensor(jrow[:, 1, :], jrow[:, 1, :], jrow[:, 2, :], ALU.mult))
            step(dve.tensor_tensor(jrow[:, 2, :], iot[:, 0:J], wide(end[:, E - 1:E], [[0, J]]), ALU.is_le))
            word = jrow[:, 3, :]
            step(dve.tensor_scalar(word, jrow[:, 0, :], 16.0, None, ALU.mult))
            step(dve.tensor_tensor(word[:, 1:J], word[:, 1:J], jrow[:, 0, 0:J - 1], ALU.add))
            for row, shift, ahead in ((0, 8, 1), (1, 12, 0), (1, 16, 1), (2, 20, 0)):
                step(dve.scalar_tensor_tensor(out=word[:, 0:J - ahead], in0=jrow[:, row, ahead:J], scalar=float(1 << shift),
                                              in1=word[:, 0:J - ahead], op0=ALU.mult, op1=ALU.add))
            dve.tensor_copy(table[:, :], word)
            step(dve.tensor_copy(pairs[:, :], end[:, E - 1:E]))
            step(dve.tensor_scalar(pairs[:, :], pairs[:, :], 1, None, ALU.logical_shift_right))
            dve.wait_ge(s_hotd, 2 * T // HB)
            step(dve.tensor_copy(A["tok"][:, :], names[:, :]))

        @block.tensor
        def _(pe):
            pe.wait_ge(s_in, 80)
            pe.wait_ge(s_one, 1)
            pe.wait_ge(s_sel, 1)
            flat = before[:, :, :].rearrange("p t e -> p (t e)")
            pe.matmul(flat, triu[:, :], sel[:, :, :].rearrange("p t e -> p (t e)"), start=True, stop=False, skip_group_check=True)
            for t in range(T - 1):
                one = sel[:, t, 0:1]
                moving = bass.AP(one.tensor, one.offset, [list(one.ap[0]), [0, T - 1 - t], [1, E]])
                pe.matmul(flat[:, (t + 1) * E:T * E], ones[:, :], moving, start=False, stop=(t == T - 2), skip_group_check=True)
            for t in range(T):
                ins = pe.matmul(total[:, :], ones[:, :], sel[:, t, :], start=(t == 0), stop=(t == T - 1))
            ins.then_inc(s_cnt, 1)
            for n8 in range(2 * T // HB):
                pe.wait_ge(s_hot, n8 + 1)
                for i in range(HB):
                    n = n8 * HB + i
                    ins = pe.matmul(names[:, :], hot_p[:, n8 % 2, i, :], hot_j[:, n, :], start=(n == 0), stop=(n == 2 * T - 1))
                ins.then_inc(s_hotd, 1)


def experts(nc, sem, A, W, S):
    modc, ident, gate5, table = A["modc"], A["ident"], A["gate5"], A["table"]
    N0, J, FC = 3 * DC, SLOT_TILES, DE // P
    with ExitStack() as ctx:
        sb = lambda name, shape, dt=F32: ctx.enter_context(nc.sbuf_tensor(name, shape, dt))
        ps = lambda name, shape, dt=F32: ctx.enter_context(nc.psum_tensor(name, shape, dt))
        tok = A["tok"]
        cell = sb("ex_cell", [P, 2, 1], U32)
        xg = sb("ex_x", [P, 2, D])
        h = sb("ex_h", [P, 2, DC, P])
        hhi, hlo = sb("ex_hhi", [P, 2, DC, P], F32R), sb("ex_hlo", [P, 2, DC, P], F32R)
        ghi, glo, dhi, dlo = (W[name] for name in ("ghi", "glo", "dhi", "dlo"))
        sg = sb("ex_silu", [P, 2, DE])
        hid = sb("ex_hid", [P, 2, DE])
        hidhi, hidlo = sb("ex_hidhi", [P, 2, DE], F32R), sb("ex_hidlo", [P, 2, DE], F32R)
        y = sb("ex_y", [P, 2, D])
        pg = ps("ex_pgu", [P, 2, 2 * DE])
        ph = ps("ex_phid", [P, 512])
        py = ps("ex_py", [P, D])
        turned = ps("ex_turned", [P, 2, 512])
        s_cell = sem("ex_cell")
        s_x = [sem(f"ex_x_in{i}") for i in range(2)]
        s_dlo, s_glo = W["s_dlo"], W["s_glo"]
        s_turn, s_h, s_hhi, s_hlo = sem("ex_turned"), sem("ex_h"), sem("ex_h_hi"), sem("ex_h_lo")
        s_gu, s_silu, s_hid = sem("ex_gate_up"), sem("ex_silu"), sem("ex_hid")
        s_th, s_hidT, s_dn, s_y = sem("ex_hid_turned"), sem("ex_hid_split"), sem("ex_down"), sem("ex_y")
        s_fill = sem("ex_filled")
        s_yst = [sem(f"ex_y_out{i}") for i in range(2)]
        block = ctx.enter_context(nc.Block())

        def value(eng, cell, top):
            eng.nop(nofuse=True)
            return eng.value_load(cell, min_val=0, max_val=top)

        def fields(word, u):
            return (word >> 4 * u) & 15, (word >> 4 + 4 * u) & 15, (word >> 12 + 4 * u) & 15

        def real(j):
            return not isinstance(j, int) or j >= 0

        def run(eng, step):
            for j in range(-3, 2):
                word = value(eng, table[0:1, j:j + 1], (1 << 21) - 1) if j >= 0 else None
                step(j, j % 2, *(fields(word, 0) if j >= 0 else (None,) * 3))
            with steps(eng, 2, J + 1, 2) as j0:
                word = value(eng, table[0:1, ds(j0, 1)], (1 << 21) - 1)
                with eng.If(word >> 20):
                    for u in range(2):
                        step(j0 + u, u, *(fields(word, u)))
                eng.nop(nofuse=True)

        @block.sync
        def _(sp):
            load_down(sp, W, 1)
            with steps(sp, 2, E, 2) as e0:
                for u in range(2):
                    load_gate_up(sp, W, e0 + u, u)
                    load_down(sp, W, e0 + u)
            with steps(sp, 2, J + 1, 2) as j0:
                word = value(sp, table[0:1, ds(j0, 1)], (1 << 21) - 1)
                with sp.If(word >> 20):
                    sp.sem_inc(s_fill, 32)
                with sp.Else():
                    for u in range(2):
                        sp.dma_start(S["ye"][ds((j0 + (u - 1)) * P, P), :], gate5[:, :]).then_inc(s_fill, 16)
                sp.nop(nofuse=True)
            sp.wait_ge(s_fill, (J - 1) // 2 * 32)

        @block.gpsimd
        def _(pool):
            def step(j, u, e_prev, e, e_next):
                if real(j + 4):
                    pos(pool, s_turn, j + 3)
                    pool.nop(nofuse=True)
                    pool.tensor_copy(cell[:, u, :], tok[:, j + 4:j + 5] if isinstance(j, int) else tok[:, ds(j + 4, 1)]).then_inc(s_cell, 1)
                    pool.wait_ge(s_cell, j + 5)
                    pool.nop(nofuse=True)
                    pool.indirect_dma_start(out=xg[:, u, :], out_offset=None, in_=S["z2"],
                                            in_offset=bass.IndirectOffsetOnAxis(ap=cell[:, u, :], axis=0)).then_inc(s_x[u], 16)
                if real(j + 1):
                    pool.wait_ge(s_hhi, j + 2)
                    pool.tensor_tensor(hlo[:, 1 - u], h[:, 1 - u], hhi[:, 1 - u].bitcast(F32), ALU.subtract).then_inc(s_hlo, 1)
                if real(j):
                    pool.nop(nofuse=True)
                    with pool.If(e_next):
                        gate_up_lo(pool, W, e_next, ds(e_next & 1, 1), 1)
                    pool.nop(nofuse=True)

            step(-4, 0, None, None, None)
            run(pool, step)
            n = value(pool, A["pairs"][0:1, 0:1], J // 2 + 1)
            for u in range(2):
                pool.wait_ge(s_x[u], n * 16 + 48)
                pool.nop(nofuse=True)

        @block.scalar
        def _(act):
            def step(j, u, e_prev, e, e_next):
                if real(j + 2):
                    act.wait_ge(s_turn, j + 3)
                    pos(act, s_hlo, j + 1)
                    for c in range(DC):
                        ins = act.activation(h[:, u, c, :], turned[:, c // 4, (c % 4) * P:(c % 4 + 1) * P], ACT.Identity,
                                             bias=modc[:, 0, N0 + c:N0 + c + 1], scale=modc[:, 0, N0 + DC + c:N0 + DC + c + 1])
                    ins.then_inc(s_h, 1)
                if real(j):
                    pos(act, s_gu, j)
                    act.nop(nofuse=True)
                    with act.If(e_next):
                        gate_up_hi(act, W, e_next, ds(e_next & 1, 1))
                    act.wait_ge(s_gu, j + 1)
                    pos(act, s_hid, j - 1)
                    act.activation(sg[:, u, :], pg[:, u, 0:DE], ACT.Silu).then_inc(s_silu, 1)
                if real(j):
                    pos(act, s_dn, j)
                    act.nop(nofuse=True)
                    with act.If(e_next):
                        down_hi(act, W, e_next, ds(e_next & 1, 1))
                    act.nop(nofuse=True)
                if real(j - 1):
                    act.wait_ge(s_y, j)
                    store(j - 1, 1 - u)

            def store(n, u):
                rows = ds(n * P, P) if not isinstance(n, int) else slice(n * P, (n + 1) * P)
                act.dma_start(S["ye"][rows, :], y[:, u, :]).then_inc(s_yst[u], 16)

            run(act, step)
            n = value(act, A["pairs"][0:1, 0:1], J // 2 + 1)
            for u in range(2):
                act.wait_ge(s_yst[u], n * 16 + 16 * (1 - u))
                act.nop(nofuse=True)

        @block.vector
        def _(dve):
            def step(j, u, e_prev, e, e_next):
                if real(j + 1):
                    dve.wait_ge(s_h, j + 2)
                    pos(dve, s_gu, j)
                    dve.tensor_copy(hhi[:, 1 - u], h[:, 1 - u]).then_inc(s_hhi, 1)
                if real(j - 1):
                    dve.wait_ge(s_th, j)
                    pos(dve, s_dn, j - 2)
                    dve.tensor_copy(hidhi[:, 1 - u, :], ph[:, 0:DE]).then_inc(s_hidT, 1)
                    dve.wait_ge(s_hidT, j * 2 - 1)
                    dve.tensor_tensor(hidlo[:, 1 - u, :], ph[:, 0:DE], hidhi[:, 1 - u, :].bitcast(F32), ALU.subtract).then_inc(s_hidT, 1)
                if real(j):
                    dve.nop(nofuse=True)
                    with dve.If(e_next):
                        gate_up_lo(dve, W, e_next, ds(e_next & 1, 1), 0)
                    dve.wait_ge(s_silu, j + 1)
                    pos(dve, s_th, j - 1)
                    dve.tensor_tensor(hid[:, u, :], sg[:, u, :], pg[:, u, DE:2 * DE], ALU.mult).then_inc(s_hid, 1)
                if real(j - 1):
                    dve.wait_ge(s_dn, j)
                    if not (isinstance(j, int) and j < 3):
                        dve.wait_ge(s_yst[1 - u], (j - 1 + u) * 8 - 8)
                    dve.tensor_tensor(y[:, 1 - u, :], py[:, :], gate5[:, :], ALU.mult).then_inc(s_y, 1)
                if real(j):
                    dve.nop(nofuse=True)
                    with dve.If(e_next):
                        down_lo(dve, W, e_next, ds(e_next & 1, 1))
                    dve.nop(nofuse=True)

            run(dve, step)

        @block.tensor
        def _(pe):
            def turn_hid(j, u):
                pe.wait_ge(s_hid, j + 1)
                pos(pe, s_hidT, j * 2)
                for c in range(FC):
                    ins = pe.transpose(ph[:, c * P:(c + 1) * P], hid[:, u, c * P:(c + 1) * P], ident[:, :])
                ins.then_inc(s_th, 1)

            def step(j, u, e_prev, e, e_next):
                if real(j):
                    for i in range(2):
                        pe.wait_ge(s_glo[i], e + 1)
                    par = e & 1
                    pe.wait_ge(s_hlo, j + 1)
                    pos(pe, s_hid, j - 1)
                    for c in range(DC):
                        if c == DC // 2 and real(j - 1):
                            turn_hid(j - 1, 1 - u)
                        wh, wl = (w[:, ds(par, 1), c, :].rearrange("p a f -> p (a f)") for w in (ghi, glo))
                        pe.matmul(pg[:, u, :], hhi[:, u, c, :], wh, start=(c == 0), stop=False)
                        pe.matmul(pg[:, u, :], hhi[:, u, c, :], wl, start=False, stop=False)
                        ins = pe.matmul(pg[:, u, :], hlo[:, u, c, :], wh, start=False, stop=(c == DC - 1))
                    ins.then_inc(s_gu, 1)
                elif real(j - 1):
                    turn_hid(j - 1, 1 - u)
                if real(j - 1):
                    pe.wait_ge(s_dlo, e_prev + 1)
                    par = e_prev & 1
                    pe.wait_ge(s_hidT, j * 2)
                    pos(pe, s_y, j - 1)
                    for c in range(FC):
                        a, b = (part[:, 1 - u, c * P:(c + 1) * P] for part in (hidhi, hidlo))
                        for i in range(2):
                            cols = slice(512 * i, 512 * i + 512)
                            wh, wl = (w[:, ds(par, 1), c, cols].rearrange("p a f -> p (a f)") for w in (dhi, dlo))
                            pe.matmul(py[:, cols], a, wh, start=(c == 0), stop=False)
                            pe.matmul(py[:, cols], a, wl, start=False, stop=False)
                        for i in range(2):
                            cols = slice(512 * i, 512 * i + 512)
                            wh = dhi[:, ds(par, 1), c, cols].rearrange("p a f -> p (a f)")
                            ins = pe.matmul(py[:, cols], b, wh, start=False, stop=(c == FC - 1))
                    ins.then_inc(s_dn, 1)
                if real(j + 3):
                    n = j + 3
                    pe.wait_ge(s_x[1 - u], (n // 2 + 1) * 16 if isinstance(n, int) else (n + u) * 8 + 8)
                    pos(pe, s_h, n)
                    for c in range(DC):
                        ins = pe.transpose(turned[:, c // 4, (c % 4) * P:(c % 4 + 1) * P], xg[:, 1 - u, c * P:(c + 1) * P], ident[:, :])
                    ins.then_inc(s_turn, 1)

            run(pe, step)


def combine(nc, sem, A, ln_g, ln_b, S, out):
    slots, gates = A["slots"], A["gates"]
    with ExitStack() as ctx:
        sb = lambda name, shape, dt=F32: ctx.enter_context(nc.sbuf_tensor(name, shape, dt))
        NB = 4
        ya, yb = sb("co_ya", [P, NB, D]), sb("co_yb", [P, NB, D])
        cell = sb("co_cell", [P, 2, NB, 1], U32)
        xt = sb("co_x1", [P, NB, D])
        r = sb("co_r", [P, NB, D])
        o = sb("co_o", [P, NB, D])
        g, b = sb("co_g", [P, D]), sb("co_b", [P, D])
        st, mv = sb("co_st", [P, 12]), sb("co_mv", [P, 2, 2])
        rs = sb("co_rs", [P, 2, 4])
        const = sb("co_const", [P, 3])
        s_g, s_const, s_cell = sem("co_ln_in"), sem("co_consts"), sem("co_cell")
        s_ya, s_yb, s_x = ([sem(f"co_{n}_in{i}") for i in range(NB)] for n in ("ya", "yb", "x1"))
        s_a, s_b, s_r, s_st, s_mom, s_pl, s_rs = (sem(f"co_{n}") for n in ("a", "b", "residual", "stats", "moments", "pool_step", "rstd"))
        s_z, s_zg, s_o = sem("co_z"), sem("co_zg"), sem("co_o")
        s_os = [sem(f"co_out{i}") for i in range(NB)]
        block = ctx.enter_context(nc.Block())

        def real(t):
            return not isinstance(t, int) or 0 <= t < TILES

        def run(eng, step):
            for t in range(-3, NB):
                step(t, t % NB)
            with steps(eng, NB, TILES - NB, NB) as t0:
                for u in range(NB):
                    step(t0 + u, u)
            for t in range(TILES - NB, TILES + 2):
                step(t, t % NB)

        def fills(t, u):
            return (t - u) * (16 // NB) + 16

        @block.sync
        def _(sp):
            sp.dma_start(g[:, :], ln_g.partition_broadcast(P)).then_inc(s_g, 16)
            sp.dma_start(b[:, :], ln_b.partition_broadcast(P)).then_inc(s_g, 16)
            for t in range(NB):
                sp.dma_start(xt[:, t, :], S["x1"][t * P:(t + 1) * P, :]).then_inc(s_x[t], 16)
            with steps(sp, NB, TILES, NB) as t0:
                for u in range(NB):
                    sp.wait_ge(s_r, t0 + u - NB + 1)
                    sp.dma_start(xt[:, u, :], S["x1"][ds((t0 + u) * P, P), :]).then_inc(s_x[u], 16)

        @block.gpsimd
        def _(pool):
            for i, value in enumerate((-0.5, EPS, -1.0)):
                pool.memset(const[:, i:i + 1], value).then_inc(s_const, 1)
            pool.wait_ge(s_const, 3)

            def step(t, u):
                if real(t + 3):
                    n, un = t + 3, (u + 3) % NB
                    pos(pool, s_b, t)
                    for k, (dst, s) in enumerate(((ya, s_ya), (yb, s_yb))):
                        pool.nop(nofuse=True)
                        pool.tensor_copy(cell[:, k, un, :], slots[:, k, n:n + 1] if isinstance(n, int) else slots[:, k, ds(n, 1)]).then_inc(s_cell, 1)
                        pool.wait_ge(s_cell, n * 2 + k + 1)
                        pool.nop(nofuse=True)
                        pool.indirect_dma_start(out=dst[:, un, :], out_offset=None, in_=S["ye"],
                                                in_offset=bass.IndirectOffsetOnAxis(ap=cell[:, k, un, :], axis=0)).then_inc(s[un], 16)
                if real(t):
                    w = u % 2
                    pool.wait_ge(s_mom, t + 1)
                    pool.tensor_tensor(rs[:, w, 0:1], mv[:, w, 1:2], const[:, 1:2], ALU.add).then_inc(s_pl, 1)
                    pool.tensor_tensor(rs[:, w, 2:3], mv[:, w, 0:1], const[:, 2:3], ALU.mult).then_inc(s_pl, 1)
                    pool.wait_ge(s_pl, t * 3 + 2)
                    pool.tensor_tensor(rs[:, w, 1:2], rs[:, w, 0:1], const[:, 0:1], ALU.pow).then_inc(s_pl, 1)
                    pool.wait_ge(s_pl, t * 3 + 3)
                    pool.tensor_tensor(rs[:, w, 3:4], rs[:, w, 2:3], rs[:, w, 1:2], ALU.mult).then_inc(s_rs, 1)
                if real(t - 1):
                    pool.wait_ge(s_zg, t)
                    up = (u + 3) % NB
                    pool.tensor_tensor(o[:, up, :], o[:, up, :], b[:, :], ALU.add).then_inc(s_o, 1)

            pool.wait_ge(s_g, 32)
            run(pool, step)

        @block.scalar
        def _(act):
            def step(t, u):
                if real(t + 1):
                    n, un = t + 1, (u + 1) % NB
                    act.wait_ge(s_ya[un], fills(n, un))
                    pos(act, s_zg, t - 2)
                    gcol = gates[:, 0, n:n + 1] if isinstance(n, int) else gates[:, 0, ds(n, 1)]
                    act.activation(r[:, un, :], ya[:, un, :], ACT.Copy, scale=gcol).then_inc(s_a, 1)
                if real(t):
                    act.wait_ge(s_rs, t + 1)
                    act.activation(r[:, u, :], r[:, u, :], ACT.Identity, bias=rs[:, u % 2, 3:4], scale=rs[:, u % 2, 1:2]).then_inc(s_z, 1)
                if real(t - 2):
                    n, un = t - 2, (u + 2) % NB
                    rows = ds(n * P, P) if not isinstance(n, int) else slice(n * P, (n + 1) * P)
                    act.wait_ge(s_o, t - 1)
                    act.dma_start(out[rows, :], o[:, un, :]).then_inc(s_os[un], 16)

            run(act, step)
            for u in range(NB):
                act.wait_ge(s_os[u], 16 // NB * TILES)

        @block.vector
        def _(dve):
            dve.wait_ge(s_g, 32)

            def step(t, u):
                if real(t):
                    w = u % 2
                    dve.wait_ge(s_yb[u], fills(t, u))
                    dve.wait_ge(s_a, t + 1)
                    gcol = gates[:, 1, t:t + 1] if isinstance(t, int) else gates[:, 1, ds(t, 1)]
                    dve.scalar_tensor_tensor(out=r[:, u, :], in0=yb[:, u, :], scalar=gcol, in1=r[:, u, :],
                                             op0=ALU.mult, op1=ALU.add).then_inc(s_b, 1)
                    dve.wait_ge(s_b, t + 1)
                    dve.wait_ge(s_x[u], fills(t, u))
                    dve.scalar_tensor_tensor(out=r[:, u, :], in0=xt[:, u, :], scalar=ALPHA, in1=r[:, u, :],
                                             op0=ALU.mult, op1=ALU.add).then_inc(s_r, 1)
                    dve.wait_ge(s_r, t + 1)
                    for i in range(2):
                        dve.bn_stats(st[:, 6 * i:6 * i + 6], r[:, u, 512 * i:512 * i + 512]).then_inc(s_st, 1)
                    dve.wait_ge(s_st, t * 2 + 2)
                    dve.nop(nofuse=True)
                    dve.bn_aggr(mv[:, w, :], st[:, :]).then_inc(s_mom, 1)
                if real(t - 1):
                    up = (u + 3) % NB
                    dve.wait_ge(s_z, t)
                    if not (isinstance(t, int) and t - 1 < NB):
                        dve.wait_ge(s_os[up], fills(t - 1 - NB, up))
                    dve.tensor_tensor(o[:, up, :], r[:, up, :], g[:, :], ALU.mult).then_inc(s_zg, 1)

            run(dve, step)


def constants():
    qc, kc = np.arange(WIN_C)[:, None], np.arange(SPAN)[None, :]
    mask = np.zeros((QB, WIN_C, SPAN), np.float32)
    for n in range(QB):
        q = n * WIN_C + qc
        k = min(max(n * WIN_C - WIN_C // 2, 0), GRID_W - SPAN) + kc
        first = np.clip(q - WIN_C // 2, 0, GRID_W - WIN_C)
        mask[n] = np.where((k >= first) & (k < first + WIN_C), 0.0, -BIG)
    a, b = np.arange(RAD), np.arange(P)
    nk = RAD // 2 + 1
    turn = 2 * np.pi * np.outer(a, np.arange(nk)) / RAD
    parts = np.concatenate([np.cos(turn), -np.sin(turn[:, 1:nk - 1])], 1)
    short = np.einsum("ac,jk->ajck", parts, np.eye(8)).reshape(P, P)
    th = 2 * np.pi * b[None, :, None] * (RAD * b[None, None, :] + np.arange(nk)[:, None, None]) / SEQ
    long = np.concatenate([np.cos(th), -np.sin(th), np.sin(th), np.cos(th)], 2)
    tc = 2 * np.pi * np.outer(np.arange(64), np.arange(64)) / 64
    norm = (SEQ * 64) ** -0.5
    chan = np.stack([np.kron(np.eye(2), np.cos(tc)), np.kron(np.eye(2), np.sin(tc))]) * norm
    return {"k_mask": mask, "k_ident": np.eye(P, dtype=np.float32), "k_short": short.astype(np.float32),
            "k_long": long.astype(np.float32), "k_chan": chan.astype(np.float32),
            "k_less4": np.tril(np.ones((4, 4), np.float32), -1), "k_less16": np.tril(np.ones((E, E), np.float32), -1),
            "k_iota": np.arange(P, dtype=np.float32), "k_triu": np.triu(np.ones((P, P), np.float32), 1)}


INPUTS = ["x", "c", "ctx", "c_ctx", "w_mod", "b_mod", "w_in", "rpb", "w_four", "w_out", "ln1_g", "ln1_b", "ln2_g",
          "ln2_b", "w_router", "router_bias", "w_gate", "w_up", "w_down"]
SCRATCH = {"xbias": [QB, WIN_C, HEADS, 15, SPAN], "qT": [NAW, SEQ], "kT": [NAW, SEQ], "kcT": [NAW, CTX],
           "vc": [CTX, NAW], "vf": [SEQ, NAW + FW],
           "hpart": [RAD, P, FW], "mixT": [NAW + FW, SEQ], "x1": [SEQ, D], "z2": [SEQ, D],
           "ye": [SLOTS, D]}


def build(nc, T, S, out):
    with ExitStack() as top:
        first_half = []

        def sem(name):
            first_half.append(nc.alloc_semaphore(name=name))
            return first_half[-1]

        keep = lambda name, shape, dt=F32: top.enter_context(nc.sbuf_tensor(name, shape, dt))
        A = {"modc": keep("modc", [P, 2, MODS * DC]), "ident": keep("ident", [P, P]),
             "score": keep("score", [P, TILES, E]), "slots": keep("slots", [P, 2, TILES], U32),
             "gates": keep("gates", [P, 2, TILES]), "tok": keep("tok", [P, TABLED], U32),
             "table": keep("table", [P, TABLED], U32), "pairs": keep("pairs", [P, 1], U32)}
        with ExitStack() as shared:
            sb = lambda name, shape: shared.enter_context(nc.sbuf_tensor(name, shape, F32))
            M = {"x": sb("x_tiles", [P, 2, D]), "stage": sb("stage", [P, 4, 1024]), "sc": sb("silu_c", [P, 2, DC]),
                 "bcol": sb("b_mod_col", [P, MODS * DC]),
                 "s_x": [sem(f"x_in{i}") for i in range(2)], "s_w": [sem(f"w_in_in{i}") for i in range(2)]}
            M["wst"] = [M["stage"][:, 2 * i:2 * i + 2, :].rearrange("p a b -> p (a b)") for i in range(2)]
            modulation(nc, sem, A, M, T["c"], T["c_ctx"], T["w_mod"], T["b_mod"], T["rpb"], T["k_mask"], T["k_ident"],
                       S["xbias"], T["w_in"], T["ctx"])
            projection(nc, sem, A, M, T["x"], T["w_in"], T["w_mod"], S)
        A["gate2"], A["gate5"] = keep("gate2", [P, D]), keep("gate5", [P, D])
        w_ctx = top.enter_context(ExitStack())
        wraw = w_ctx.enter_context(nc.sbuf_tensor("w_out_raw", [P, DC, D], F32))
        with ExitStack() as shared:
            sb = lambda name, shape: shared.enter_context(nc.sbuf_tensor(name, shape, F32))
            L = {"qT": sb("qT", [P, PAIRS, SEQ]), "kT": sb("kT", [P, PAIRS, SEQ]), "kcT": sb("kcT", [P, PAIRS, CTX]),
                 "vc": sb("vc", [P, 2, NAW]), "s_q": sem("q_in"), "s_k": sem("k_in"), "s_c": sem("ctx_in"), "s_y": sem("y_out")}
            fourier(nc, sem, A, T["w_four"], T, S, L, wraw)
            attention(nc, sem, A, S, L, T["w_out"], wraw)
        nc.clear_and_free_semaphores(first_half)
        nc.all_engine_barrier()
        sem = lambda name: top.enter_context(nc.semaphore(name))
        mixing(nc, sem, A, T["x"], wraw, T["ln1_g"], T["ln1_b"], T["w_router"], S)
        w_ctx.close()
        with ExitStack() as shared:
            W = expert_weights(nc, shared, sem, T)
            routing(nc, sem, A, W, T["router_bias"], T)
            experts(nc, sem, A, W, S)
        combine(nc, sem, A, T["ln2_g"], T["ln2_b"], S, out)


def kernel(**inputs):
    import numpy as _np
    import concourse.bacc as _bacc
    from concourse import mybir as _mybir
    from concourse.bass_utils import run_bass_kernel_spmd as _run

    nc = _bacc.Bacc("TRN2", target_bir_lowering=False, num_devices=1)
    arrays = {name: _np.ascontiguousarray(inputs[name]) for name in INPUTS}
    arrays.update(constants())
    T = {}
    for name, a in arrays.items():
        t = nc.dram_tensor(f"in_{name}", a.shape, _mybir.dt.float32, kind="ExternalInput").ap()
        lead = name not in ("c_ctx", "w_router", "router_bias") and not name.startswith("k_")
        T[name] = t[0] if lead else t
    S = {name: nc.dram_tensor(f"s_{name}", shape, F32, kind="Internal").ap() for name, shape in SCRATCH.items()}
    out = nc.dram_tensor("out", (1, SEQ, D), _mybir.dt.float32, kind="ExternalOutput").ap()
    build(nc, T, S, out[0])
    r = _run(nc, [{f"in_{k}": v for k, v in arrays.items()}], core_ids=[0])
    return r.results[0]["out"]
```
